# Optimizing a Trainium2 kernel written in Bass

```python
import jax, jax.numpy as jnp
from jax import lax
import numpy as np

D_MODEL = 1024
BATCH = 1
SEQ = 512
DEPTH = 2

GRID_W = 64
Q_BLOCK = 128
ROPE_THETA = 10000.0
EPS = 1e-6
N_HEADS_A = 8
N_KV_A = 2
GROUP_A = N_HEADS_A // N_KV_A
HEAD_DIM_A = 64
WIDTH_A = N_HEADS_A * HEAD_DIM_A
N_HEADS_B = 8
Q_LORA = 384
KV_LORA = 256
QK_NOPE = 64
QK_ROPE = 32
V_DIM_B = 64
WIDTH_B = N_HEADS_B * V_DIM_B
IN_SIZES = (WIDTH_A, N_KV_A * HEAD_DIM_A, N_KV_A * HEAD_DIM_A, Q_LORA, KV_LORA, QK_ROPE, D_MODEL, D_MODEL)
IN_COLS = sum(IN_SIZES)
N_MOD = 6
N_EXPERTS = 16
N_GROUPS = 4
EXPERTS_PER_GROUP = N_EXPERTS // N_GROUPS
TOP_K = 2
D_EXPERT = 512
MOE_BLOCK = 128

kernel_name = "hybrid_gqa_mla_grouped_moe_encoder"

def rms_norm(x, g):
    xf = x.astype(jnp.float32)
    y = xf * lax.rsqrt(jnp.mean(xf * xf, axis=-1, keepdims=True) + EPS)
    return (y * g.astype(jnp.float32)).astype(x.dtype)

def split_points(sizes):
    pts, acc = [], 0
    for s in sizes[:-1]:
        acc += s
        pts.append(acc)
    return pts

def axial_rope_tables(row, col, rot_dim):
    n = rot_dim // 4
    inv = 1.0 / (ROPE_THETA ** (jnp.arange(n, dtype=jnp.float32) / n))
    ang = jnp.concatenate([row[:, None] * inv, col[:, None] * inv], axis=-1)
    return jnp.cos(ang), jnp.sin(ang)

def apply_rope(x, cos, sin):
    half = x.shape[-1] // 2
    shape = (cos.shape[0],) + (1,) * (x.ndim - 3) + (half,)
    c = cos.reshape(shape).astype(x.dtype)
    s = sin.reshape(shape).astype(x.dtype)
    x1, x2 = x[..., :half], x[..., half:]
    return jnp.concatenate([x1 * c - x2 * s, x2 * c + x1 * s], axis=-1)

def gqa_attention(q, k, v):
    B, S, H, hd = q.shape
    nb = S // Q_BLOCK
    qb = q.reshape(B, nb, Q_BLOCK, N_KV_A, GROUP_A, hd).transpose(1, 0, 2, 3, 4, 5)
    scale = hd ** -0.5

    def block(qi):
        s = jnp.einsum('bqkgd,bskd->bkgqs', qi, k).astype(jnp.float32) * scale
        p = jax.nn.softmax(s, axis=-1).astype(v.dtype)
        return jnp.einsum('bkgqs,bskd->bqkgd', p, v)

    o = lax.map(block, qb)
    return o.transpose(1, 0, 2, 3, 4, 5).reshape(B, S, H * hd)

def mla_attention(q_nope, q_rope, k_nope, k_rope, v):
    B, S, H, dn = q_nope.shape
    dr = q_rope.shape[-1]
    nb = S // Q_BLOCK
    qn = q_nope.reshape(B, nb, Q_BLOCK, H, dn).swapaxes(0, 1)
    qr = q_rope.reshape(B, nb, Q_BLOCK, H, dr).swapaxes(0, 1)
    scale = (dn + dr) ** -0.5

    def block(args):
        qn_i, qr_i = args
        s = (jnp.einsum('bqhd,bshd->bhqs', qn_i, k_nope)
             + jnp.einsum('bqhr,bsr->bhqs', qr_i, k_rope)).astype(jnp.float32) * scale
        p = jax.nn.softmax(s, axis=-1).astype(v.dtype)
        return jnp.einsum('bhqs,bshd->bqhd', p, v)

    o = lax.map(block, (qn, qr))
    return o.swapaxes(0, 1).reshape(B, S, H * v.shape[-1])

def hybrid_mixer(h, w_in, q_norm_a, k_norm_a, q_a_norm, kv_norm, w_q_b, w_kv_b,
                 w_proj_a, w_proj_b, w_o, cos_a, sin_a, cos_b, sin_b):
    B, S, _ = h.shape
    z = h @ w_in
    q_a, k_a, v_a, q_lat, kv_lat, k_rope, gate_a, gate_b = jnp.split(z, split_points(IN_SIZES), axis=-1)

    qa = apply_rope(rms_norm(q_a.reshape(B, S, N_HEADS_A, HEAD_DIM_A), q_norm_a), cos_a, sin_a)
    ka = apply_rope(rms_norm(k_a.reshape(B, S, N_KV_A, HEAD_DIM_A), k_norm_a), cos_a, sin_a)
    va = v_a.reshape(B, S, N_KV_A, HEAD_DIM_A)
    y_a = gqa_attention(qa, ka, va) @ w_proj_a

    qb = (rms_norm(q_lat, q_a_norm) @ w_q_b).reshape(B, S, N_HEADS_B, QK_NOPE + QK_ROPE)
    qb_nope = qb[..., :QK_NOPE]
    qb_rope = apply_rope(qb[..., QK_NOPE:], cos_b, sin_b)
    kv = (rms_norm(kv_lat, kv_norm) @ w_kv_b).reshape(B, S, N_HEADS_B, QK_NOPE + V_DIM_B)
    k_nope, v_b = kv[..., :QK_NOPE], kv[..., QK_NOPE:]
    k_r = apply_rope(k_rope, cos_b, sin_b)
    y_b = mla_attention(qb_nope, qb_rope, k_nope, k_r, v_b) @ w_proj_b

    merged = jax.nn.sigmoid(gate_a) * y_a + jax.nn.sigmoid(gate_b) * y_b
    return merged @ w_o

def grouped_moe(h, w_router, router_bias, w1, w3, w2):
    T, D = h.shape
    scores = jax.nn.sigmoid((h @ w_router).astype(jnp.float32))
    biased = scores + router_bias.astype(jnp.float32)
    grp_score = lax.top_k(biased.reshape(T, N_GROUPS, EXPERTS_PER_GROUP), 2)[0].sum(-1)
    g_sel = jnp.argmax(grp_score, axis=-1)
    expert_group = jnp.arange(N_EXPERTS) // EXPERTS_PER_GROUP
    masked = jnp.where(expert_group[None, :] == g_sel[:, None], biased, -jnp.inf)
    _, expert = lax.top_k(masked, TOP_K)
    gw = jnp.take_along_axis(scores, expert, axis=1)
    gw = gw / jnp.sum(gw, axis=-1, keepdims=True)

    n_slots = T * TOP_K
    e_flat = expert.reshape(-1)
    tok_flat = jnp.repeat(jnp.arange(T), TOP_K)
    order = jnp.argsort(e_flat)
    e_sorted = e_flat[order]
    tok_sorted = tok_flat[order]
    g_sorted = gw.reshape(-1)[order]
    counts = jnp.bincount(e_flat, length=N_EXPERTS)
    padded = ((counts + MOE_BLOCK - 1) // MOE_BLOCK) * MOE_BLOCK
    starts = jnp.cumsum(counts) - counts
    pends = jnp.cumsum(padded)
    pstarts = pends - padded
    dest = pstarts[e_sorted] + (jnp.arange(n_slots) - starts[e_sorted])
    n_pad = ((n_slots + MOE_BLOCK - 1) // MOE_BLOCK) * MOE_BLOCK + N_EXPERTS * MOE_BLOCK
    n_blk = n_pad // MOE_BLOCK
    xs = jnp.zeros((n_pad, D), h.dtype).at[dest].set(h[tok_sorted])
    blk_e = jnp.clip(jnp.searchsorted(pends, jnp.arange(n_blk) * MOE_BLOCK, side='right'), 0, N_EXPERTS - 1)

    def expert_block(args):
        xb, e = args
        return (jax.nn.silu(xb @ w1[e]) * (xb @ w3[e])) @ w2[e]

    ys = lax.map(expert_block, (xs.reshape(n_blk, MOE_BLOCK, D), blk_e)).reshape(n_pad, D)
    return jnp.zeros((T, D), h.dtype).at[tok_sorted].add(ys[dest] * g_sorted[:, None].astype(h.dtype))

def setup_inputs(seed: int = 0) -> dict:
    key = jax.random.key(seed)
    ks = jax.random.split(key, 22)
    f32 = jnp.float32
    nrm = lambda k, shape, s: jax.random.normal(k, shape, f32) * s
    gain = lambda k, shape: 1.0 + 0.01 * jax.random.normal(k, shape, f32)
    return {
        "x": nrm(ks[0], (BATCH, SEQ, D_MODEL), 1.0),
        "c": nrm(ks[1], (BATCH, D_MODEL), 1.0),
        "w_ada": nrm(ks[2], (DEPTH, D_MODEL, N_MOD * D_MODEL), 0.5 * D_MODEL ** -0.5),
        "b_ada": nrm(ks[3], (DEPTH, N_MOD * D_MODEL), 0.01),
        "norm1": gain(ks[4], (DEPTH, D_MODEL)),
        "w_in": nrm(ks[5], (DEPTH, D_MODEL, IN_COLS), D_MODEL ** -0.5),
        "q_norm_a": gain(ks[6], (DEPTH, HEAD_DIM_A)),
        "k_norm_a": gain(ks[7], (DEPTH, HEAD_DIM_A)),
        "q_a_norm": gain(ks[8], (DEPTH, Q_LORA)),
        "kv_norm": gain(ks[9], (DEPTH, KV_LORA)),
        "w_q_b": nrm(ks[10], (DEPTH, Q_LORA, N_HEADS_B * (QK_NOPE + QK_ROPE)), Q_LORA ** -0.5),
        "w_kv_b": nrm(ks[11], (DEPTH, KV_LORA, N_HEADS_B * (QK_NOPE + V_DIM_B)), KV_LORA ** -0.5),
        "w_proj_a": nrm(ks[12], (DEPTH, WIDTH_A, D_MODEL), WIDTH_A ** -0.5),
        "w_proj_b": nrm(ks[13], (DEPTH, WIDTH_B, D_MODEL), WIDTH_B ** -0.5),
        "w_o": nrm(ks[14], (DEPTH, D_MODEL, D_MODEL), D_MODEL ** -0.5),
        "norm2": gain(ks[15], (DEPTH, D_MODEL)),
        "w_router": nrm(ks[16], (D_MODEL, N_EXPERTS), D_MODEL ** -0.5),
        "router_bias": nrm(ks[17], (N_EXPERTS,), 0.01),
        "w1": nrm(ks[18], (DEPTH, N_EXPERTS, D_MODEL, D_EXPERT), D_MODEL ** -0.5),
        "w3": nrm(ks[19], (DEPTH, N_EXPERTS, D_MODEL, D_EXPERT), D_MODEL ** -0.5),
        "w2": nrm(ks[20], (DEPTH, N_EXPERTS, D_EXPERT, D_MODEL), D_EXPERT ** -0.5),
        "norm_f": gain(ks[21], (D_MODEL,)),
    }

def reference(x, c, w_ada, b_ada, norm1, w_in, q_norm_a, k_norm_a, q_a_norm, kv_norm,
              w_q_b, w_kv_b, w_proj_a, w_proj_b, w_o, norm2, w_router, router_bias,
              w1, w3, w2, norm_f):
    B, S, D = x.shape
    rows = S // GRID_W
    row = jnp.broadcast_to(jnp.arange(rows, dtype=jnp.float32)[:, None], (rows, GRID_W)).reshape(S)
    col = jnp.broadcast_to(jnp.arange(GRID_W, dtype=jnp.float32)[None, :], (rows, GRID_W)).reshape(S)
    cos_a, sin_a = axial_rope_tables(row, col, HEAD_DIM_A)
    cos_b, sin_b = axial_rope_tables(row, col, QK_ROPE)
    cond = jax.nn.silu(c)

    for l in range(DEPTH):
        mod = (cond @ w_ada[l] + b_ada[l])[:, None, :]
        sh1, sc1, g1, sh2, sc2, g2 = jnp.split(mod, N_MOD, axis=-1)
        h = rms_norm(x, norm1[l]) * (1.0 + sc1) + sh1
        x = x + g1 * hybrid_mixer(h, w_in[l], q_norm_a[l], k_norm_a[l], q_a_norm[l], kv_norm[l],
                                  w_q_b[l], w_kv_b[l], w_proj_a[l], w_proj_b[l], w_o[l],
                                  cos_a, sin_a, cos_b, sin_b)
        h = rms_norm(x, norm2[l]) * (1.0 + sc2) + sh2
        x = x + g2 * grouped_moe(h.reshape(B * S, D), w_router, router_bias,
                                 w1[l], w3[l], w2[l]).reshape(B, S, D)

    return rms_norm(x, norm_f)


_drawn_inputs = setup_inputs


def setup_inputs(seed=0):
    import zlib

    import numpy as np

    out = dict(_drawn_inputs(seed))
    spreads = {}
    factors = {'norm1': 5.885,
     'q_norm_a': 8.0,
     'k_norm_a': 8.0,
     'q_a_norm': 8.0,
     'kv_norm': 8.0,
     'norm_f': 5.486}
    for name, (base, spread) in spreads.items():
        noise = np.random.default_rng([zlib.crc32(name.encode()), seed]).standard_normal(out[name].shape)
        drawn = base * np.exp(spread * noise) if base else spread * noise
        out[name] = __import__('jax').numpy.asarray(drawn.astype(out[name].dtype))
    for name, factor in factors.items():
        out[name] = (out[name] * factor).astype(out[name].dtype)
    return out
```

```python
from contextlib import ExitStack

import numpy as np
import concourse.bass as bass
from concourse import mybir

P = 128
D = 1024
SEQ = 512
NT = SEQ // P
NC = D // P
DEPTH = 2
NMOD = 6
GRID_W = 64
THETA = 10000.0
EPS = 1e-6
HD = 64
RD = 32
KD = HD + RD
QL, KVL = 384, 256
QK_HEADS = 10
ZC = 1440
Z_ITEMS = ((0, 512), (512, 256), (768, 384), (1152, 288))
Z_V, Z_QL, Z_KVL, Z_KR = 640, 768, 1152, 1408
E = 16
EG = 4
F = 512
BIG = 3.0e38
R = 6
SLOTS = (E + 1) * SEQ
MIX_ITEMS = 18
ITEMS = MIX_ITEMS + 3 * E
ADA_ITEMS = DEPTH * NMOD * D // 512
ADA_Q = NMOD * D // 512
TR = 90
UNITS = 64
TR_N1, TR_QK, TR_LAT, TR_MLA, TR_N2, TR_X0 = 0, 8, 13, 18, 34, 42
C_ID, C_UT, C_CA, C_SA, C_CB, C_SB, C_GW, C_EW, C_EO, C_TK = 0, 128, 256, 384, 512, 576, 640, 644, 660, 676
C_N = 680
GQA_UNITS = [(4 * s + j, t) for j in range(4) for s in range(2) for t in range(NT)]


def constants():
    c = np.zeros((P, C_N), np.float32)
    c[:, C_ID:C_ID + P] = np.eye(P, dtype=np.float32)
    c[:, C_UT:C_UT + P] = np.triu(np.ones((P, P), np.float32), 1)
    pos = np.arange(SEQ)
    row, col = (pos // GRID_W).astype(np.float32), (pos % GRID_W).astype(np.float32)
    for width, cc, cs in ((HD, C_CA, C_SA), (RD, C_CB, C_SB)):
        n = width // 4
        inv = (np.float32(1.0) / np.power(np.float32(THETA), np.arange(n, dtype=np.float32) / np.float32(n))).astype(np.float32)
        ang = np.concatenate([row[:, None] * inv, col[:, None] * inv], axis=-1).astype(np.float32)
        for at, f in ((cc, np.cos), (cs, np.sin)):
            t = f(ang.astype(np.float64)).astype(np.float32).reshape(NT, P, width // 2)
            c[:, at:at + NT * width // 2] = t.transpose(1, 0, 2).reshape(P, -1)
    c[:, C_GW:C_GW + EG] = EG - np.arange(EG)
    c[:, C_EW:C_EW + E] = E - np.arange(E)
    c[:, C_EO:C_EO + E] = SEQ * np.arange(E)
    c[:, C_TK:C_TK + NT] = np.arange(NT)[None, :] * P + np.arange(P)[:, None]
    return c


def trunk(nc, x_in, c_in, w_ada, b_ada, norm1, w_in, q_norm_a, k_norm_a, q_a_norm, kv_norm, w_q_b,
          w_kv_b, w_proj_a, w_proj_b, w_o, norm2, w_router, router_bias, w1, w3, w2, norm_f, consts, out):
    f32, i32 = mybir.dt.float32, mybir.dt.int32
    ALU = mybir.AluOpType
    ACT = mybir.ActivationFunctionType
    X = mybir.AxisListType.X

    mod_d = nc.dram_tensor("mod_d", [DEPTH, NMOD * D], f32, kind="Internal").ap()
    xn_d = nc.dram_tensor("xn_d", [SEQ, D], f32, kind="Internal").ap()
    tok_d = nc.dram_tensor("tok_d", [SLOTS, 2], i32, kind="Internal").ap()
    ys_d = nc.dram_tensor("ys_d", [SEQ * 2, D], f32, kind="Internal").ap()

    ada_v = w_ada.rearrange("l (p c) (q n) -> l q p c n", c=NC, n=512)
    in_v = w_in.rearrange("l (p c) n -> l p c n", c=NC)
    qb_v = w_q_b.rearrange("l (c p) n -> l p c n", p=P)
    kvb_v = w_kv_b.rearrange("l (c p) n -> l p c n", p=P)
    pa_v = w_proj_a.rearrange("l (c p) n -> l p c n", p=P)
    pb_v = w_proj_b.rearrange("l (c p) n -> l p c n", p=P)
    wo_v = w_o.rearrange("l (c p) n -> l p c n", p=P)
    w1_v = w1.rearrange("l e (p c) f -> (l e) p c f", c=NC)
    w3_v = w3.rearrange("l e (p c) f -> (l e) p c f", c=NC)
    w2_v = w2.rearrange("l e (c p) n -> (l e) p c n", p=P)

    with ExitStack() as ctx:
        def sb(name, shape, dt=f32):
            return ctx.enter_context(nc.sbuf_tensor(name, shape, dt))

        def sem(name):
            return ctx.enter_context(nc.semaphore(name))

        ring = sb("ring", [P, R, 4096])
        x = sb("x", [P, NT, D])
        hT = sb("hT", [P, NC, SEQ])
        reg_a = sb("reg_a", [P, 4096])
        reg_b = sb("reg_b", [P, 5760])
        reg_c = sb("reg_c", [P, 3072])
        reg_d = sb("reg_d", [P, 2560])
        vb = sb("vb", [P, NT, 4 * HD])
        reg_f = sb("reg_f", [P, 2048])
        cst = sb("cst", [P, C_N])
        ones = sb("ones", [P, P])
        gain_qk = sb("gain_qk", [P, 2, HD])
        gain_l = sb("gain_l", [P, 5])
        gain_n = sb("gain_n", [P, 2 * DEPTH, NC])
        mod_c = sb("mod_c", [P, DEPTH * NMOD, NC])
        wr = sb("wr", [P, NC, E])
        rbias = sb("rbias", [P, E])
        kr = sb("kr", [P, NT, RD])
        ssq = sb("ssq", [P, NT])
        rstd = sb("rstd", [P, NT])
        stz = sb("stz", [P, NT, 12])
        nmax = sb("nmax", [P, 4])
        lsum = sb("lsum", [P, 4])
        linv = sb("linv", [P, 4])
        cur = sb("cur", [P, NMOD, NC])
        cond = sb("cond", [P, 2, NC])
        gw = sb("gw", [P, 2, NT])
        dest = sb("dest", [P, 2, NT], i32)
        tok_i = sb("tok_i", [P, 2, NT, 2], i32)
        no_tok = sb("no_tok", [P, SLOTS // P, 2], i32)
        cnt_i = sb("cnt_i", [P, E], i32)
        idx = sb("idx", [P, 3, 2], i32)
        idy = sb("idy", [P, 2, 2], i32)

        ident = cst[:, C_ID:C_ID + P]
        utri = cst[:, C_UT:C_UT + P]
        cos_a = cst[:, C_CA:C_CA + 128].rearrange("p (t n) -> p t n", t=NT)
        sin_a = cst[:, C_SA:C_SA + 128].rearrange("p (t n) -> p t n", t=NT)
        cos_b = cst[:, C_CB:C_CB + 64].rearrange("p (t n) -> p t n", t=NT)
        sin_b = cst[:, C_SB:C_SB + 64].rearrange("p (t n) -> p t n", t=NT)
        xn = reg_a[:, :].rearrange("p (t n) -> p t n", t=NT)
        oT = reg_a[:, :].rearrange("p (c n) -> p c n", c=8)
        cy = reg_a[:, :].rearrange("p (b k n) -> p b k n", b=2, k=2)
        z = reg_b[:, :].rearrange("p (t n) -> p t n", t=NT)
        qbT = reg_b[:, 0:2048].rearrange("p (h n) -> p h n", h=4)
        kbT = reg_b[:, 2048:4096].rearrange("p (h n) -> p h n", h=4)
        mT = reg_b[:, 0:4096].rearrange("p (c n) -> p c n", c=NC)
        xg = reg_b[:, 0:2048].rearrange("p (b n) -> p b n", b=2)
        xsT = reg_b[:, 2048:4096].rearrange("p (b c n) -> p b c n", b=2, c=NC)
        u_s = reg_b[:, 4096:4608]
        sg_e = reg_b[:, 4608:5120]
        uT = reg_b[:, 5120:5632].rearrange("p (c n) -> p c n", c=4)
        brow = reg_b[0:1, 0:512]
        qaT = reg_c[:, 0:2048].rearrange("p (j n) -> p j n", j=4)
        kaT = reg_c[:, 2048:2560]
        va = reg_c[:, 2560:3072].rearrange("p (t n) -> p t n", t=NT)
        qn = reg_c[:, 0:1536].rearrange("p (t h n) -> p t h n", t=NT, h=4)
        kn = reg_c[:, 1536:3072].rearrange("p (t h n) -> p t h n", t=NT, h=4)
        g1_row, g2_row, nf_row = (reg_c[:, k * D:(k + 1) * D] for k in range(3))
        qlT = reg_d[:, 0:1536].rearrange("p (c n) -> p c n", c=3)
        kvlT = reg_d[:, 1536:2560].rearrange("p (c n) -> p c n", c=2)
        ysb = reg_d[:, 0:2048].rearrange("p (b n) -> p b n", b=2)
        prob = reg_f[:, 0:1024].rearrange("p (b n) -> p b n", b=2)
        probT = reg_f[:, 1024:2048].rearrange("p (b k n) -> p b k n", b=2, k=NT)
        zsq = reg_f[:, 0:1280].rearrange("p (b n) -> p b n", b=2)
        rot = reg_f[:, 1280:1920].rearrange("p (b n) -> p b n", b=2)
        rot_b = reg_f[:, 0:512].rearrange("p (b n) -> p b n", b=2)
        sg_m = reg_f[:, :].rearrange("p (b g n) -> p b g n", b=2, g=2)
        wo_t = reg_f[:, 0:1024].rearrange("p (b n) -> p b n", b=2)
        sq_j = reg_f[:, 1024:2048]

        def rt(k):
            return reg_f[:, k * 64:(k + 1) * 64].rearrange("p (t e) -> p t e", t=NT)
        score, biased, oh1, oh2, r_a, r_b, rank = (rt(k) for k in range(7))
        r_s = reg_f[:, 448:640]

        def modc(l, m):
            return mod_c[:, l * NMOD + m, :]

        def scale1(c):
            return cur[:, 1, c:c + 1]

        def shift1(c):
            return cur[:, 0, c:c + 1]

        def scale2(c):
            return cur[:, 4, c:c + 1]

        def shift2(c):
            return cur[:, 3, c:c + 1]

        def slot(s, a, n):
            return ring[:, s, 0:a * n].rearrange("p (a n) -> p a n", a=a)

        bank = [ctx.enter_context(nc.psum_tensor(f"bank{k}", [P, 512], f32)) for k in range(8)]

        c_in_s = sem("consts_loaded")
        x_in_s = sem("x_loaded")
        cond_in = sem("cond_loaded")
        cond_s = sem("cond_ready")
        ones_s = sem("ones_ready")
        cond_e = sem("cond_sigmoid")
        b_in = sem("ada_bias_loaded")
        ada_ps = sem("ada_psum_ready")
        ada_ev = sem("ada_psum_read")
        mod_st = sem("mod_stored")
        mod_ld = sem("mod_columns_loaded")
        mod_s = sem("mod_scales_ready")
        cur_s = sem("layer_mod_ready")
        w_rdy = [sem(f"slot{k}_loaded") for k in range(R)]
        tok0 = sem("token_list_cleared")
        x2 = sem("x_after_moe")
        x1 = sem("x_after_mixer")
        sq_s = sem("square_sums")
        ms_s = sem("mean_squares")
        rt_s = sem("roots")
        xn_s = sem("normed")
        tr_r = sem("transposes_ready")
        tr_e = sem("transposes_read")
        z_r = sem("z_psum_ready")
        z_e = sem("z_psum_read")
        zsq_s = sem("z_squares")
        zst_s = sem("z_square_sums_reduced")
        zms_s = sem("z_mean_squares")
        zrt_s = sem("z_roots")
        qk_s = sem("qk_lat_rotated")
        gl_s = sem("layer_gains_loaded")
        s_r = sem("scores_ready")
        mx_s = sem("row_max")
        ex_s = sem("exp_done")
        pn_s = sem("probs_normed")
        pt_r = sem("probsT_ready")
        pt_e = sem("probsT_read")
        o_r = sem("head_out_ready")
        o_e = sem("head_out_read")
        nat_r = sem("mla_psum_ready")
        nat_e = sem("mla_psum_read")
        rope_s = sem("mla_rotated")
        ga_r, gb_r, ya_r, yb_r = (sem(n) for n in ("gate_a_ready", "gate_b_ready", "proj_a_ready", "proj_b_ready"))
        sig_s = sem("gates_sigmoid")
        m_s = sem("merged")
        wo_r = sem("mixer_out_ready")
        row_ld = sem("gate_rows_loaded")
        xn_st = sem("normed_stored")
        lg_r = sem("logits_ready")
        sc_s = sem("router_scores")
        oh_s = sem("one_hots")
        rk_r = sem("ranks_ready")
        ds_s = sem("destinations")
        tk_s = sem("token_list_written")
        ix_s = sem("slot_tokens_loaded")
        iy_s = sem("slot_rows_loaded")
        xg_s = [sem(f"tokens_gathered{k}") for k in range(2)]
        h1_r, h3_r = sem("h1_ready"), sem("h3_ready")
        sge_s = sem("h1_sigmoid")
        u_s_s = sem("expert_hidden")
        y_r, y_e = sem("expert_out_ready"), sem("expert_out_read")
        ys_st = [sem(f"expert_out_stored{k}") for k in range(2)]
        cg_s = [sem(f"outputs_gathered{k}") for k in range(2)]
        ov_free = sem("extra_block_done")
        ov_w = sem("extra_weights_loaded")
        ov_i = sem("extra_slot_tokens")
        ov_x = sem("extra_tokens_gathered")
        ov_t = sem("extra_transposed")
        ov_te = sem("extra_transposes_read")
        ov_h = sem("extra_h_ready")
        ov_g = sem("extra_sigmoid")
        ov_u = sem("extra_hidden")
        ov_y = sem("extra_out_ready")
        ov_ye = sem("extra_out_read")
        ov_st = sem("extra_out_stored")
        ov_all = sem("extra_pass_done")
        out_s = sem("out_ready")
        out_st = sem("out_stored")

        ticks = sem("ticks")

        block = ctx.enter_context(nc.Block())

        def wait(eng, s, value):
            eng.wait_ge(s, value)
            eng.sem_inc(ticks, 1)

        def extra_blocks(eng, counter, body):
            with eng.Fori(0, E) as e:
                n = eng.value_load(cnt_i[0:1, bass.ds(e, 1)], min_val=0, max_val=SEQ)
                with eng.If(n > P):
                    with eng.Fori(1, eng.snap((n + (P - 1)) >> 7)) as b:
                        body(e, b * P, eng.snap(counter))
                        eng.reg_add(counter, counter, 1)

        @block.sync
        def _(sp):
            sp.dma_start(cond[:, 0, :], c_in[0].rearrange("(p c) -> p c", c=NC)).then_inc(cond_in, 16)

            with sp.Fori(0, DEPTH) as l:
                with sp.Fori(0, ADA_Q // R) as g:
                    for r in range(R):
                        wait(sp, ada_ps, l * ADA_Q + g * R + (r + 1))
                        sp.dma_start(slot(r, NC, 512), ada_v[l, g * R + r]).then_inc(w_rdy[r], 16)

            n_ov = sp.alloc_register("n_ov_sp")
            sp.reg_mov(n_ov, 0)
            wait(sp, ada_ps, R + ADA_ITEMS)
            with sp.Fori(0, DEPTH) as l:
                def load(k, dst_shape, src):
                    a, n = dst_shape
                    sp.dma_start(slot(k % R, a, n), src).then_inc(w_rdy[k % R], 16)

                for i, (at, n) in enumerate(Z_ITEMS):
                    load(i, (NC, n), in_v[l, :, :, at:at + n])
                for hf in range(2):
                    if hf == 1:
                        wait(sp, z_r, l * 16 + 8)
                    load(4 + 2 * hf, (3, 384), qb_v[l, :, :, hf * 384:(hf + 1) * 384])
                    load(5 + 2 * hf, (2, 512), kvb_v[l, :, :, hf * 512:(hf + 1) * 512])
                wait(sp, z_r, l * 16 + 12)
                load(8, (NC, 512), in_v[l, :, :, ZC:ZC + 512])
                wait(sp, z_r, l * 16 + 16)
                load(9, (NC, 512), in_v[l, :, :, ZC + D:ZC + D + 512])
                wait(sp, nat_r, l * 16 + 4)
                load(10, (4, 512), pa_v[l, :, :, 0:512])
                wait(sp, nat_r, l * 16 + 8)
                load(11, (4, 512), pb_v[l, :, :, 0:512])
                wait(sp, nat_r, l * 16 + 12)
                load(12, (NC, 512), in_v[l, :, :, ZC + 512:ZC + D])
                wait(sp, nat_r, l * 16 + 16)
                load(13, (NC, 512), in_v[l, :, :, ZC + D + 512:ZC + 2 * D])
                wait(sp, ga_r, l * 8 + 4)
                load(14, (4, 512), pa_v[l, :, :, 512:D])
                wait(sp, gb_r, l * 8 + 4)
                load(15, (4, 512), pb_v[l, :, :, 512:D])
                for n, s in ((0, ya_r), (1, yb_r)):
                    wait(sp, s, l * 8 + 4)
                    load(16 + n, (NC, 512), wo_v[l, :, :, n * 512:(n + 1) * 512])
                wait(sp, ga_r, l * 8 + 8)
                load(18, (NC, F), w1_v[l * E])
                wait(sp, gb_r, l * 8 + 8)
                load(19, (NC, F), w3_v[l * E])
                wait(sp, ya_r, l * 8 + 8)
                load(20, (NC, F), w1_v[l * E + 1])
                wait(sp, yb_r, l * 8 + 8)
                load(21, (NC, F), w3_v[l * E + 1])
                wait(sp, wo_r, l * 8 + 4)
                load(22, (4, D), w2_v[l * E])
                wait(sp, wo_r, l * 8 + 8)
                load(23, (NC, F), w1_v[l * E + 2])
                wait(sp, h1_r, l * E + 1)
                load(24, (NC, F), w3_v[l * E + 2])
                wait(sp, h3_r, l * E + 1)
                load(25, (4, D), w2_v[l * E + 1])
                with sp.Fori(0, 6) as i:
                    e0 = l * E + 2 * i
                    for r in range(2):
                        k = 26 + 3 * r
                        wait(sp, h1_r, e0 + (r + 2))
                        load(k, (NC, F), w1_v[e0 + (r + 3)])
                        wait(sp, h3_r, e0 + (r + 2))
                        load(k + 1, (NC, F), w3_v[e0 + (r + 3)])
                        wait(sp, y_r, (e0 + (r + 1)) * 2)
                        load(k + 2, (4, D), w2_v[e0 + (r + 2)])
                wait(sp, h1_r, l * E + 14)
                load(62, (NC, F), w1_v[l * E + 15])
                wait(sp, h3_r, l * E + 14)
                load(63, (NC, F), w3_v[l * E + 15])
                wait(sp, y_r, l * 2 * E + 26)
                load(64, (4, D), w2_v[l * E + 14])
                wait(sp, h1_r, l * E + 15)
                load(65, (4, D), w2_v[l * E + 15])
                wait(sp, y_r, l * 2 * E + 2 * E)

                def body(e, first, n):
                    wait(sp, ov_free, n + 1)
                    sp.dma_start(slot(0, NC, F), w1_v[l * E + e]).then_inc(ov_w, 16)
                    sp.dma_start(slot(1, NC, F), w3_v[l * E + e]).then_inc(ov_w, 16)
                    sp.dma_start(slot(2, 4, D), w2_v[l * E + e]).then_inc(ov_w, 16)
                wait(sp, ds_s, l + 1)
                extra_blocks(sp, n_ov, body)
                wait(sp, ov_all, l + 1)
            for t in range(NT):
                wait(sp, out_s, t + 1)
                sp.dma_start(out[0, t * P:(t + 1) * P, :], xn[:, t, :]).then_inc(out_st, 16)
            wait(sp, out_st, 16 * NT)

        @block.gpsimd
        def _(pool):
            pool.dma_start(cst[:, :], consts).then_inc(c_in_s, 16)
            pool.memset(ones[:, :], 1.0).then_inc(ones_s, 1)
            for t in range(NT):
                pool.dma_start(x[:, t, :], x_in[0, t * P:(t + 1) * P, :]).then_inc(x_in_s, 16)
            pool.dma_start(wr[:, :, :], w_router.rearrange("(p c) e -> p c e", c=NC)).then_inc(c_in_s, 16)
            pool.dma_start(rbias[:, :], router_bias.partition_broadcast(P)).then_inc(c_in_s, 16)
            for w, g in ((0, norm1), (1, norm2)):
                pool.dma_start(gain_n[:, w * DEPTH:(w + 1) * DEPTH, :], g.rearrange("l (p c) -> p l c", c=NC)).then_inc(c_in_s, 16)
            pool.memset(no_tok[:, :, 0:1], 0).then_inc(ones_s, 1)
            pool.memset(no_tok[:, :, 1:2], 2 * SEQ).then_inc(ones_s, 1)
            wait(pool, ones_s, 3)
            wait(pool, c_in_s, 16 * 5)
            wait(pool, mod_st, 16 * ADA_ITEMS)
            pool.dma_start(mod_c[:, :, :], mod_d.rearrange("l (m p c) -> p (l m) c", m=NMOD, c=NC)).then_inc(mod_ld, 16)

            n_ov = pool.alloc_register("n_ov_pool")
            pool.reg_mov(n_ov, 0)
            with pool.Fori(0, DEPTH) as l:
                wait(pool, x2, l * NT + NT)
                pool.dma_start(gain_qk[:, 0, :], q_norm_a[l].partition_broadcast(P)).then_inc(gl_s, 16)
                pool.dma_start(gain_qk[:, 1, :], k_norm_a[l].partition_broadcast(P)).then_inc(gl_s, 16)
                pool.dma_start(gain_l[:, 0:3], q_a_norm[l].rearrange("(c p) -> p c", p=P), allow_slow_non_contiguous=True).then_inc(gl_s, 16)
                pool.dma_start(gain_l[:, 3:5], kv_norm[l].rearrange("(c p) -> p c", p=P), allow_slow_non_contiguous=True).then_inc(gl_s, 16)
                pool.dma_start(tok_d.rearrange("(p n) o -> p (n o)", p=P), no_tok[:, :, :].rearrange("p n o -> p (n o)")).then_inc(tok0, 16)
                wait(pool, o_e, l * UNITS + UNITS)
                pool.dma_start(g1_row, mod_d[l, 2 * D:3 * D].partition_broadcast(P)).then_inc(row_ld, 16)
                pool.dma_start(g2_row, mod_d[l, 5 * D:6 * D].partition_broadcast(P)).then_inc(row_ld, 16)
                pool.dma_start(nf_row, norm_f.partition_broadcast(P)).then_inc(row_ld, 16)
                for t in range(NT):
                    wait(pool, xn_s, l * 2 * NT + NT + t + 1)
                    pool.dma_start(xn_d[t * P:(t + 1) * P, :], xn[:, t, :]).then_inc(xn_st, 16)
                wait(pool, ds_s, l + 1)
                wait(pool, tok0, l * 16 + 16)
                for k in range(2):
                    for t in range(NT):
                        pool.indirect_dma_start(tok_d, bass.IndirectOffsetOnAxis(dest[:, k, t:t + 1], 0),
                                                tok_i[:, k, t, :], None, bounds_check=E * SEQ - 1,
                                                oob_is_err=False).then_inc(tk_s, 16)
                wait(pool, tk_s, l * 128 + 128)
                wait(pool, xn_st, l * 64 + 64)

                def gather(e_abs, e_row, b, n_wait):
                    if n_wait is not None:
                        wait(pool, tr_r, n_wait)
                    pool.dma_start(idx[:, b, :], tok_d[bass.ds(e_row, P), :]).then_inc(ix_s, 16)
                    wait(pool, ix_s, e_abs * 16 + 16)
                    pool.indirect_dma_start(xg[:, b, :], None, xn_d, bass.IndirectOffsetOnAxis(idx[:, b, 0:1], 0),
                                            bounds_check=SEQ - 1, oob_is_err=False).then_inc(xg_s[b], 16)

                def scatter(e_abs, e_row, b):
                    pool.dma_start(idy[:, b, :], tok_d[bass.ds(e_row, P), :]).then_inc(iy_s, 16)
                    wait(pool, iy_s, e_abs * 16 + 16)
                    wait(pool, y_e, e_abs * 2 + 2)
                    pool.indirect_dma_start(ys_d, bass.IndirectOffsetOnAxis(idy[:, b, 1:2], 0), ysb[:, b, :], None,
                                            bounds_check=2 * SEQ - 1, oob_is_err=False).then_inc(ys_st[b], 16)

                wait(pool, x1, l * 8 + 8)
                gather(l * E, 0, 0, None)
                gather(l * E + 1, SEQ, 1, None)
                gather(l * E + 2, 2 * SEQ, 0, l * TR + (TR_X0 + 2))
                with pool.Fori(0, 6) as i:
                    for r in range(2):
                        f = 2 * i + r
                        gather(l * E + f + 3, (f + 3) * SEQ, (3 + r) % 2, l * TR + (TR_X0 + 4) + f * 3)
                        scatter(l * E + f, f * SEQ, r)
                gather(l * E + 15, 15 * SEQ, 1, l * TR + (TR_X0 + 4 + 12 * 3))
                for f in range(12, E):
                    scatter(l * E + f, f * SEQ, f % 2)

                def body(e, first, n):
                    wait(pool, ov_free, n + 1)
                    pool.dma_start(idx[:, 2, :], tok_d[bass.ds(e * SEQ + first, P), :]).then_inc(ov_i, 16)
                    wait(pool, ov_i, n * 16 + 16)
                    pool.indirect_dma_start(xg[:, 0, :], None, xn_d, bass.IndirectOffsetOnAxis(idx[:, 2, 0:1], 0),
                                            bounds_check=SEQ - 1, oob_is_err=False).then_inc(ov_x, 16)
                    wait(pool, ov_ye, n * 2 + 2)
                    pool.indirect_dma_start(ys_d, bass.IndirectOffsetOnAxis(idx[:, 2, 1:2], 0), ysb[:, 0, :], None,
                                            bounds_check=2 * SEQ - 1, oob_is_err=False).then_inc(ov_st, 16)
                    wait(pool, ov_st, n * 16 + 16)
                    pool.sem_inc(ov_free, 1)
                for b in range(2):
                    wait(pool, ys_st[b], l * 128 + 128)
                extra_blocks(pool, n_ov, body)
                pool.sem_inc(ov_all, 1)

                for t in range(NT):
                    if t >= 2:
                        wait(pool, x2, l * NT + NT + t - 1)
                    pool.dma_start(cy[:, t % 2, :, :].rearrange("p k n -> p (k n)"),
                                   ys_d.rearrange("(t p k) n -> t p (k n)", p=P, k=2)[t]).then_inc(cg_s[t % 2], 16)

        @block.scalar
        def _(act):
            A = act.activation
            act.wait_ge(cond_in, 16)
            A(cond[:, 1, :], cond[:, 0, :], ACT.Sigmoid).then_inc(cond_e, 1)
            with act.Fori(0, DEPTH) as l:
                with act.Fori(0, ADA_Q // R) as g:
                    for r in range(R):
                        act.dma_start(reg_b[0:1, 512 * r:512 * (r + 1)],
                                      b_ada.rearrange("l (q o n) -> l q o n", n=512, o=1)[l, g * R + r]).then_inc(b_in, 16)
                    for r in range(R):
                        act.wait_ge(ada_ev, l * ADA_Q + g * R + (R + r + 1))
                        act.dma_start(mod_d.rearrange("l (q o n) -> l q o n", n=512, o=1)[l, g * R + r],
                                      reg_b[0:1, 512 * r:512 * (r + 1)]).then_inc(mod_st, 16)
                    act.wait_ge(mod_st, (l * ADA_Q + g * R + R) * 16)

            n_ov = act.alloc_register("n_ov_act")
            act.reg_mov(n_ov, 0)

            def norm_sums(base, src_sem, at):
                for t in range(NT):
                    act.wait_ge(src_sem, at)
                    if t >= 1:
                        act.wait_ge(sq_s, base * NT + t)
                    A(sq_j, x[:, t, :], ACT.Square, accum_out=ssq[:, t:t + 1]).then_inc(sq_s, 1)
                act.wait_ge(ms_s, base + 1)
                A(ssq[:, :], ssq[:, :], ACT.Sqrt).then_inc(rt_s, 1)

            def evac(l, g, dst, **kw):
                act.wait_ge(tr_r, l * TR + (g + 1))
                A(dst, bank[g % 2][0:dst.shape[0], 0:SEQ], ACT.Identity, **kw).then_inc(tr_e, 1)

            with act.Fori(0, DEPTH) as l:
                norm_sums(l * 2, x2, l * NT + NT)
                act.wait_ge(cur_s, l + 1)
                for c in range(NC):
                    evac(l, TR_N1 + c, hT[:, c, :], scale=scale1(c), bias=shift1(c))
                for i, (at, n) in enumerate(Z_ITEMS):
                    for t in range(NT):
                        k = i * NT + t
                        act.wait_ge(z_r, l * 16 + (k + 1))
                        src = bank[2 + k % 4]
                        if i == 1:
                            A(va[:, t, :], src[:, P:2 * P], ACT.Copy)
                            A(z[:, t, at:at + P], src[:, 0:P], ACT.Copy).then_inc(z_e, 1)
                        elif i == 0:
                            A(z[:, t, 0:512].rearrange("p (j s d) -> p s j d", s=2, j=4),
                              src[:, :].rearrange("p (s j d) -> p s j d", s=2, j=4), ACT.Copy).then_inc(z_e, 1)
                        else:
                            A(z[:, t, at:at + n], src[:, 0:n], ACT.Copy).then_inc(z_e, 1)
                for t in range(NT):
                    act.wait_ge(z_e, l * 16 + 12 + t + 1)
                    if t >= 2:
                        act.wait_ge(zst_s, l * NT + t - 1)
                    if t >= 1:
                        act.wait_ge(zsq_s, l * NT + t)
                    A(reg_f[:, 1280:1280 + QL], z[:, t, Z_QL:Z_QL + QL], ACT.Square, accum_out=stz[:, t, 10:11])
                    A(reg_f[:, 1664:1664 + KVL], z[:, t, Z_KVL:Z_KVL + KVL], ACT.Square, accum_out=stz[:, t, 11:12])
                    A(zsq[:, t % 2, :], z[:, t, 0:640], ACT.Square).then_inc(zsq_s, 1)
                act.wait_ge(zms_s, l + 1)
                A(stz[:, :, :], stz[:, :, :], ACT.Sqrt).then_inc(zrt_s, 1)
                for j in range(4):
                    evac(l, TR_QK + j, qaT[:, j, :])
                evac(l, TR_QK + 4, kaT)
                act.wait_ge(gl_s, l * 64 + 64)
                for c in range(5):
                    evac(l, TR_LAT + c, (qlT[:, c, :] if c < 3 else kvlT[:, c - 3, :]), scale=gain_l[:, c:c + 1])

                def attend(u0, n):
                    for k in range(n + 2):
                        if k < n:
                            u = u0 + k
                            act.wait_ge(mx_s, l * UNITS + (u + 1))
                            if u >= 2:
                                act.wait_ge(pt_r, l * UNITS + (u - 1))
                            A(prob[:, u % 2, :], bank[4 + u % 2][:, :], ACT.Exp, bias=nmax[:, u % 4:u % 4 + 1],
                              accum_out=lsum[:, u % 4:u % 4 + 1]).then_inc(ex_s, 1)
                        if k >= 2:
                            u = u0 + k - 2
                            act.wait_ge(pt_r, l * UNITS + (u + 1))
                            if u >= 2:
                                act.wait_ge(o_r, l * UNITS + (u - 1))
                            A(probT[:, u % 2, :, :], bank[2 + u % 2][:, :], ACT.Copy).then_inc(pt_e, 1)
                attend(0, 32)
                for hf in range(2):
                    for g in range(2 * NT):
                        t = g % NT
                        act.wait_ge(nat_r, l * 16 + (hf * 8 + g + 1))
                        src = bank[6 + g % 2]
                        if g < NT:
                            A(qn[:, t, :, :], src[:, 0:384], ACT.Copy, scale=float(KD) ** -0.5).then_inc(nat_e, 1)
                        else:
                            kv = src[:, :].rearrange("p (h n) -> p h n", h=4)
                            A(vb[:, t, :].rearrange("p (h n) -> p h n", h=4), kv[:, :, HD:2 * HD], ACT.Copy)
                            A(kn[:, t, :, 0:HD], kv[:, :, 0:HD], ACT.Copy).then_inc(nat_e, 1)
                    for h in range(4):
                        evac(l, TR_MLA + 8 * hf + h, qbT[0:KD, h, :])
                    for h in range(4):
                        evac(l, TR_MLA + 8 * hf + 4 + h, kbT[0:KD, h, :])
                    attend(32 + 16 * hf, 16)
                for j in range(NC):
                    if j >= 2:
                        act.wait_ge(m_s, l * NC + (j - 1))
                    else:
                        act.wait_ge(o_e, l * UNITS + UNITS)
                    act.wait_ge(ga_r, l * NC + (j + 1))
                    A(sg_m[:, j % 2, 0, :], bank[4 * (j % 2)][:, :], ACT.Sigmoid)
                    act.wait_ge(gb_r, l * NC + (j + 1))
                    A(sg_m[:, j % 2, 1, :], bank[4 * (j % 2) + 1][:, :], ACT.Sigmoid).then_inc(sig_s, 1)
                norm_sums(l * 2 + 1, x1, l * 8 + 8)
                for c in range(NC):
                    evac(l, TR_N2 + c, hT[:, c, :], scale=scale2(c), bias=shift2(c))
                act.wait_ge(lg_r, l + 1)
                A(reg_f[:, 0:64], bank[2][:, 0:64], ACT.Sigmoid).then_inc(sc_s, 1)

                def tokens_out(g, b, p0):
                    for k in range(2):
                        act.wait_ge(tr_r, g + (k + 1))
                        for c in range(4):
                            cc = 4 * k + c
                            ins = A(xsT[:, b, cc, :], bank[(p0 + k) % 2][:, c * P:(c + 1) * P], ACT.Identity,
                                    scale=scale2(cc), bias=shift2(cc))
                        ins.then_inc(tr_e, 1)

                def expert(e, p, g, first=False, last=False):
                    act.wait_ge(h1_r, l * E + e + 1)
                    A(sg_e, bank[4][:, :], ACT.Sigmoid).then_inc(sge_s, 1)
                    if not last:
                        tokens_out(g, 1 - p, p)
                    if not first:
                        put_out(e - 1, 1 - p, first_use=False)
                    gu = g if last else g + 2
                    act.wait_ge(tr_r, gu + 1)
                    A(uT[:, :, :], bank[(p if not last else 1)][:, :], ACT.Copy).then_inc(tr_e, 1)

                def put_out(f, p, first_use):
                    for n in range(2):
                        act.wait_ge(y_r, (l * E + f) * 2 + (n + 1))
                        if n == 0 and not first_use:
                            wait_store(f, p)
                        A(ysb[:, p, n * 512:(n + 1) * 512], bank[6 + n][:, :], ACT.Copy).then_inc(y_e, 1)

                def wait_store(f, p):
                    if isinstance(f, int):
                        if f // 2 >= 1:
                            act.wait_ge(ys_st[p], l * 128 + (f // 2) * 16)
                    else:
                        act.wait_ge(ys_st[p], l * 128 + stored[0])

                stored = [None]
                tokens_out(l * TR + TR_X0, 0, 0)
                expert(0, 0, l * TR + TR_X0 + 2, first=True)
                for e in (1, 2):
                    expert(e, e % 2, l * TR + (TR_X0 + 2 + 3 * e))
                with act.Fori(0, 6) as i:
                    for r in range(2):
                        e = 2 * i + (3 + r)
                        stored[0] = i * 16 + 16
                        expert(e, (3 + r) % 2, l * TR + (TR_X0 + 2 + 9 + 3 * r) + i * 6)
                expert(15, 1, l * TR + (TR_X0 + 2 + 45), last=True)
                put_out(15, 1, first_use=False)

                def body(e, first, n):
                    for k in range(2):
                        act.wait_ge(ov_t, n * 3 + (k + 1))
                        for c in range(4):
                            cc = 4 * k + c
                            ins = A(xsT[:, 0, cc, :], bank[k][:, c * P:(c + 1) * P], ACT.Identity,
                                    scale=scale2(cc), bias=shift2(cc))
                        ins.then_inc(ov_te, 1)
                    act.wait_ge(ov_h, n * 2 + 1)
                    A(sg_e, bank[4][:, :], ACT.Sigmoid).then_inc(ov_g, 1)
                    act.wait_ge(ov_t, n * 3 + 3)
                    A(uT[:, :, :], bank[0][:, :], ACT.Copy).then_inc(ov_te, 1)
                    for h in range(2):
                        act.wait_ge(ov_y, n * 2 + (h + 1))
                        A(ysb[:, 0, h * 512:(h + 1) * 512], bank[6 + h][:, :], ACT.Copy).then_inc(ov_ye, 1)
                act.wait_ge(ys_st[0], l * 128 + 128)
                wait(act, ds_s, l + 1)
                extra_blocks(act, n_ov, body)
            norm_sums(2 * DEPTH, x2, NT * (DEPTH + 1))

        @block.vector
        def _(v):
            TT, TS, STT = v.tensor_tensor, v.tensor_scalar, v.scalar_tensor_tensor
            n_ov = v.alloc_register("n_ov_dve")
            v.reg_mov(n_ov, 0)
            v.sem_inc(ada_ps, R)
            v.sem_inc(ada_ev, R)
            v.sem_inc(ov_free, 1)
            v.wait_ge(cond_e, 1)
            TT(cond[:, 0, :], cond[:, 0, :], cond[:, 1, :], ALU.mult).then_inc(cond_s, 1)
            with v.Fori(0, DEPTH) as l:
                with v.Fori(0, ADA_Q // R) as g:
                    for r in range(R):
                        v.wait_ge(b_in, (l * ADA_Q + g * R + R) * 16)
                        v.wait_ge(ada_ps, l * ADA_Q + g * R + (R + r + 1))
                        row = reg_b[0:1, 512 * r:512 * (r + 1)]
                        TT(row, bank[r][0:1, :], row, ALU.add).then_inc(ada_ev, 1)
            v.wait_ge(x_in_s, 16 * NT)
            v.sem_inc(x2, NT)
            v.wait_ge(c_in_s, 16 * 5)
            v.wait_ge(mod_ld, 16)
            for l in range(DEPTH):
                for w in range(2):
                    STT(modc(l, 3 * w + 1), modc(l, 3 * w + 1), 1.0, gain_n[:, w * DEPTH + l, :], ALU.add, ALU.mult)
            for k in range(2):
                v.tensor_copy(tok_i[:, k, :, 0], cst[:, C_TK:C_TK + NT])
                TS(tok_i[:, k, :, 1], cst[:, C_TK:C_TK + NT], 2.0, float(k), ALU.mult, ALU.add).then_inc(mod_s, 1)
            v.drain()

            def normed(base, n0):
                v.wait_ge(sq_s, base * NT + NT)
                TS(ssq[:, :], ssq[:, :], 1.0 / D, EPS, ALU.mult, ALU.add).then_inc(ms_s, 1)
                v.wait_ge(rt_s, base + 1)
                v.reciprocal(rstd[:, :], ssq[:, :])
                v.drain()
                for t in range(NT):
                    TS(xn[:, t, :], x[:, t, :], rstd[:, t:t + 1], None, ALU.mult).then_inc(xn_s, 1)

            def rotate(x1v, x2v, cos, sin, ta, tb):
                TT(ta, x2v, sin, ALU.mult)
                TT(tb, x1v, sin, ALU.mult)
                v.drain()
                TT(x1v, x1v, cos, ALU.mult)
                TT(x2v, x2v, cos, ALU.mult)
                v.drain()
                TT(x1v, x1v, ta, ALU.subtract)
                return TT(x2v, x2v, tb, ALU.add)

            with v.Fori(0, DEPTH) as l:
                v.tensor_copy(cur[:, :, :], mod_c[:, bass.ds(l * NMOD, NMOD), :]).then_inc(cur_s, 1)
                normed(l * 2, 0)
                for t in range(NT):
                    v.wait_ge(zsq_s, l * NT + (t + 1))
                    v.tensor_reduce(stz[:, t, 0:10], zsq[:, t % 2, :].rearrange("p (h n) -> p h n", n=HD), X, ALU.add).then_inc(zst_s, 1)
                v.drain()
                TS(stz[:, :, 0:10], stz[:, :, 0:10], 1.0 / HD, EPS, ALU.mult, ALU.add)
                TS(stz[:, :, 10:11], stz[:, :, 10:11], 1.0 / QL, EPS, ALU.mult, ALU.add)
                TS(stz[:, :, 11:12], stz[:, :, 11:12], 1.0 / KVL, EPS, ALU.mult, ALU.add).then_inc(zms_s, 1)
                v.wait_ge(gl_s, l * 64 + 64)
                TS(gain_qk[:, 0, :], gain_qk[:, 0, :], float(HD) ** -0.5, None, ALU.mult)
                v.wait_ge(zrt_s, l + 1)
                v.reciprocal(stz[:, :, :], stz[:, :, :])
                v.drain()
                for t in range(NT):
                    heads = z[:, t, 0:640].rearrange("p (h n) -> p h n", n=HD)
                    TT(heads, heads, stz[:, t, 0:10].unsqueeze(2).broadcast_to([P, QK_HEADS, HD]), ALU.mult)
                    TS(z[:, t, Z_QL:Z_QL + QL], z[:, t, Z_QL:Z_QL + QL], stz[:, t, 10:11], None, ALU.mult)
                    TS(z[:, t, Z_KVL:Z_KVL + KVL], z[:, t, Z_KVL:Z_KVL + KVL], stz[:, t, 11:12], None, ALU.mult)
                    v.drain()
                    TT(heads[:, 0:8, :], heads[:, 0:8, :], gain_qk[:, 0:1, :].broadcast_to([P, 8, HD]), ALU.mult)
                    TT(heads[:, 8:10, :], heads[:, 8:10, :], gain_qk[:, 1:2, :].broadcast_to([P, 2, HD]), ALU.mult)
                    v.drain()
                    rr = [rot[:, k, :].rearrange("p (h n) -> p h n", n=32) for k in range(2)]
                    rotate(heads[:, :, 0:32], heads[:, :, 32:64],
                           cos_a[:, t:t + 1, :].broadcast_to([P, QK_HEADS, 32]),
                           sin_a[:, t:t + 1, :].broadcast_to([P, QK_HEADS, 32]), rr[0], rr[1]).then_inc(qk_s, 1)
                v.drain()
                krv = z[:, :, Z_KR:Z_KR + RD]
                rk2 = [rot[:, k, 0:64].rearrange("p (t n) -> p t n", t=NT) for k in range(2)]
                rotate(krv[:, :, 0:16], krv[:, :, 16:32], cos_b, sin_b, rk2[0], rk2[1])
                v.drain()
                v.tensor_copy(kr[:, :, :], krv).then_inc(qk_s, 1)

                def attend(u0, n, heads):
                    for k in range(n + 3):
                        if k < n:
                            u = u0 + k
                            v.wait_ge(s_r, l * UNITS + (u + 1))
                            v.tensor_reduce(nmax[:, u % 4:u % 4 + 1], bank[4 + u % 2][:, :], X, ALU.max, negate=True).then_inc(mx_s, 1)
                        if 1 <= k < n + 1:
                            u = u0 + k - 1
                            v.wait_ge(ex_s, l * UNITS + (u + 1))
                            v.reciprocal(linv[:, u % 4:u % 4 + 1], lsum[:, u % 4:u % 4 + 1])
                            v.drain()
                            TS(prob[:, u % 2, :], prob[:, u % 2, :], linv[:, u % 4:u % 4 + 1], None, ALU.mult).then_inc(pn_s, 1)
                        if k >= 3:
                            u = u0 + k - 3
                            hd, t = heads[k - 3]
                            v.wait_ge(o_r, l * UNITS + (u + 1))
                            v.tensor_copy(oT[(hd % 2) * HD:(hd % 2 + 1) * HD, hd // 2, t * P:(t + 1) * P],
                                          bank[6 + u % 2][0:HD, 0:P]).then_inc(o_e, 1)
                attend(0, 32, GQA_UNITS)
                for hf in range(2):
                    v.wait_ge(nat_e, l * 16 + (hf * 8 + 4))
                    r4 = [rot_b[:, k, :].rearrange("p (t h n) -> p t h n", t=NT, h=4) for k in range(2)]
                    cb = cos_b.unsqueeze(2).broadcast_to([P, NT, 4, 16])
                    sn = sin_b.unsqueeze(2).broadcast_to([P, NT, 4, 16])
                    rotate(qn[:, :, :, HD:HD + 16], qn[:, :, :, HD + 16:KD], cb, sn, r4[0], r4[1]).then_inc(rope_s, 1)
                    v.wait_ge(nat_e, l * 16 + (hf * 8 + 8))
                    v.tensor_copy(kn[:, :, :, HD:KD], kr[:, :, :].unsqueeze(2).broadcast_to([P, NT, 4, RD])).then_inc(rope_s, 1)
                    attend(32 + 16 * hf, 16, [(8 + 4 * hf + h, t) for h in range(4) for t in range(NT)])
                for j in range(NC):
                    v.wait_ge(sig_s, l * NC + (j + 1))
                    v.wait_ge(ya_r, l * NC + (j + 1))
                    TT(mT[:, j, :], bank[4 * (j % 2) + 2][:, :], sg_m[:, j % 2, 0, :], ALU.mult)
                    v.wait_ge(yb_r, l * NC + (j + 1))
                    TT(sg_m[:, j % 2, 1, :], bank[4 * (j % 2) + 3][:, :], sg_m[:, j % 2, 1, :], ALU.mult)
                    v.drain()
                    TT(mT[:, j, :], mT[:, j, :], sg_m[:, j % 2, 1, :], ALU.add).then_inc(m_s, 1)
                v.wait_ge(row_ld, l * 48 + 48)
                for k in range(8):
                    n, t = k // NT, k % NT
                    v.wait_ge(wo_r, l * 8 + (k + 1))
                    TT(wo_t[:, k % 2, :], bank[4 + k % 4][:, :], g1_row[:, n * 512:(n + 1) * 512], ALU.mult)
                    v.drain()
                    xs = x[:, t, n * 512:(n + 1) * 512]
                    TT(xs, xs, wo_t[:, k % 2, :], ALU.add).then_inc(x1, 1)
                normed(l * 2 + 1, 0)

                def top1(vals, ramp, onehot, tmp, mx):
                    n = vals.shape[2]
                    v.tensor_reduce(mx, vals, X, ALU.max)
                    v.drain()
                    TT(tmp, vals, mx.unsqueeze(2).broadcast_to([P, NT, n]), ALU.is_equal)
                    v.drain()
                    TT(tmp, tmp, ramp.unsqueeze(1).broadcast_to([P, NT, n]), ALU.mult)
                    v.drain()
                    v.tensor_reduce(mx, tmp, X, ALU.max)
                    v.drain()
                    TT(onehot, tmp, mx.unsqueeze(2).broadcast_to([P, NT, n]), ALU.is_equal)
                    v.drain()
                v.wait_ge(sc_s, l + 1)
                TT(biased, score, rbias[:, :].unsqueeze(1).broadcast_to([P, NT, E]), ALU.add)
                v.drain()
                bg = biased.rearrange("p t (g e) -> p (t g) e", g=EG)
                ps = reg_f[:, 640:736].rearrange("p (g k) -> p g k", k=6)
                TT(ps[:, :, 0:3], bg[:, :, 0:3], bg[:, :, 1:4], ALU.add)
                TT(ps[:, :, 3:5], bg[:, :, 0:2], bg[:, :, 2:4], ALU.add)
                TT(ps[:, :, 5:6], bg[:, :, 0:1], bg[:, :, 3:4], ALU.add)
                v.drain()
                gs = r_s[:, 0:16].rearrange("p (t g) -> p t g", t=NT)
                gt = r_s[:, 16:32].rearrange("p (t g) -> p t g", t=NT)
                gh = r_s[:, 32:48].rearrange("p (t g) -> p t g", t=NT)
                mx = r_s[:, 48:52]
                v.tensor_reduce(r_s[:, 0:16], ps, X, ALU.max)
                v.drain()
                top1(gs, cst[:, C_GW:C_GW + EG], gh, gt, mx)
                sel = r_s[:, 32:48].unsqueeze(2).broadcast_to([P, NT * EG, EG])
                ra_g = r_a.rearrange("p t (g e) -> p (t g) e", g=EG)
                TT(ra_g, bg, sel, ALU.mult)
                TS(r_s[:, 64:80], r_s[:, 32:48], 1.0, BIG, ALU.subtract, ALU.mult)
                v.drain()
                TT(ra_g, ra_g, r_s[:, 64:80].unsqueeze(2).broadcast_to([P, NT * EG, EG]), ALU.add)
                v.drain()
                ew = cst[:, C_EW:C_EW + E]
                top1(r_a, ew, oh1, r_b, mx)
                TT(r_b, r_a, oh1, ALU.mult)
                v.drain()
                TT(r_a, r_a, r_b, ALU.subtract)
                v.drain()
                STT(r_a, oh1, -BIG, r_a, ALU.mult, ALU.add)
                v.drain()
                top1(r_a, ew, oh2, r_b, mx)
                TT(r_a, oh1, oh2, ALU.add).then_inc(oh_s, 1)
                TT(r_b, oh1, score, ALU.mult)
                v.drain()
                v.tensor_reduce(gw[:, 0, :], r_b, X, ALU.add)
                v.drain()
                TT(r_b, oh2, score, ALU.mult)
                v.drain()
                v.tensor_reduce(gw[:, 1, :], r_b, X, ALU.add)
                v.drain()
                TT(r_s[:, 52:56], gw[:, 0, :], gw[:, 1, :], ALU.add)
                v.drain()
                v.reciprocal(r_s[:, 56:60], r_s[:, 52:56])
                v.drain()
                for k in range(2):
                    TT(gw[:, k, :], gw[:, k, :], r_s[:, 56:60], ALU.mult)
                v.wait_ge(rk_r, l + 1)
                v.tensor_copy(cnt_i[:, :], bank[3][:, 64:80])
                TT(rank, bank[3][:, 0:64].rearrange("p (t e) -> p t e", t=NT),
                   cst[:, C_EO:C_EO + E].unsqueeze(1).broadcast_to([P, NT, E]), ALU.add)
                v.drain()
                for k, oh in ((0, oh1), (1, oh2)):
                    TT(r_b, oh, rank, ALU.mult)
                    v.drain()
                    v.tensor_reduce(r_s[:, 60:64], r_b, X, ALU.add)
                    v.drain()
                    ins = v.tensor_copy(dest[:, k, :], r_s[:, 60:64])
                ins.then_inc(ds_s, 1)

                def hidden(at):
                    v.wait_ge(sge_s, at + 1)
                    TT(u_s, bank[4][:, :], sg_e, ALU.mult)
                    v.drain()
                    v.wait_ge(h3_r, at + 1)
                    TT(u_s, bank[5][:, :], u_s, ALU.mult).then_inc(u_s_s, 1)
                with v.Fori(0, E) as e:
                    hidden(l * E + e)

                def body(e, first, n):
                    v.wait_ge(ov_g, n + 1)
                    TT(u_s, bank[4][:, :], sg_e, ALU.mult)
                    v.drain()
                    v.wait_ge(ov_h, n * 2 + 2)
                    TT(u_s, bank[5][:, :], u_s, ALU.mult).then_inc(ov_u, 1)
                wait(v, ds_s, l + 1)
                extra_blocks(v, n_ov, body)

                for t in range(NT):
                    v.wait_ge(cg_s[t % 2], l * 32 + (t // 2 + 1) * 16)
                    a, b = cy[:, t % 2, 0, :], cy[:, t % 2, 1, :]
                    TS(a, a, gw[:, 0, t:t + 1], None, ALU.mult)
                    v.drain()
                    STT(a, b, gw[:, 1, t:t + 1], a, ALU.mult, ALU.add)
                    v.drain()
                    TT(a, a, g2_row, ALU.mult)
                    v.drain()
                    TT(x[:, t, :], x[:, t, :], a, ALU.add).then_inc(x2, 1)
            normed(2 * DEPTH, 0)
            v.drain()
            for t in range(NT):
                TT(xn[:, t, :], xn[:, t, :], nf_row, ALU.mult).then_inc(out_s, 1)

        @block.tensor
        def _(pe):
            n_ov = pe.alloc_register("n_ov_pe")
            pe.reg_mov(n_ov, 0)
            pe.wait_ge(cond_s, 1)
            with pe.Fori(0, DEPTH) as l:
                with pe.Fori(0, ADA_Q // R) as g:
                    for r in range(R):
                        pe.wait_ge(w_rdy[r], (l * (ADA_Q // R) + g + 1) * 16)
                        pe.wait_ge(ada_ev, l * ADA_Q + g * R + (r + 1))
                        for c in range(NC):
                            ins = pe.matmul(bank[r][0:1, :], cond[:, 0, c:c + 1], slot(r, NC, 512)[:, c, :],
                                            start=c == 0, stop=c == NC - 1)
                        ins.then_inc(ada_ps, 1)
            pe.wait_ge(ones_s, 1)
            pe.wait_ge(c_in_s, 16 * 5)
            pe.wait_ge(mod_s, 1)

            with pe.Fori(0, DEPTH) as l:
                def weights(k):
                    pe.wait_ge(w_rdy[k % R], l * (16 * ITEMS // R) + 16 * (ADA_ITEMS // R + k // R + 1))

                def transposes(g, srcs, rows=P):
                    if g >= 2:
                        pe.wait_ge(tr_e, l * TR + (g - 1))
                    for t, src in enumerate(srcs):
                        ins = pe.transpose(bank[g % 2][0:rows, t * P:(t + 1) * P], src, ident)
                    ins.then_inc(tr_r, 1)

                def norm_transposes(g0, n0):
                    pe.wait_ge(xn_s, l * 2 * NT + (n0 + NT))
                    xv = xn.rearrange("p t (q c) -> p t c q", c=NC)
                    for c in range(NC):
                        transposes(g0 + c, [xv[:, t, c, :] for t in range(NT)])

                norm_transposes(TR_N1, 0)
                pe.wait_ge(tr_e, l * TR + TR_QK)
                for i, (at, n) in enumerate(Z_ITEMS):
                    weights(i)
                    w = slot(i, NC, n)
                    for t in range(NT):
                        k = i * NT + t
                        if k >= 4:
                            pe.wait_ge(z_e, l * 16 + (k - 3))
                        for c in range(NC):
                            ins = pe.matmul(bank[2 + k % 4][:, 0:n], hT[:, c, t * P:(t + 1) * P], w[:, c, :],
                                            start=c == 0, stop=c == NC - 1)
                        ins.then_inc(z_r, 1)
                pe.wait_ge(qk_s, l * 5 + 5)
                for j in range(4):
                    transposes(TR_QK + j, [z[:, t, j * P:(j + 1) * P] for t in range(NT)])
                transposes(TR_QK + 4, [z[:, t, 512:640] for t in range(NT)])
                for c in range(5):
                    at = Z_QL + c * P
                    transposes(TR_LAT + c, [z[:, t, at:at + P] for t in range(NT)])
                pe.wait_ge(tr_e, l * TR + TR_MLA)

                def attend(u0, n, q_of, k_of, v_of):
                    for k in range(n + 3):
                        if k < n:
                            u = u0 + k
                            if u >= 2:
                                pe.wait_ge(ex_s, l * UNITS + (u - 1))
                            pe.matmul(bank[4 + u % 2][:, :], q_of(k), k_of(k), start=True, stop=True).then_inc(s_r, 1)
                        if 2 <= k < n + 2:
                            u = u0 + k - 2
                            pe.wait_ge(pn_s, l * UNITS + (u + 1))
                            if u >= 2:
                                pe.wait_ge(pt_e, l * UNITS + (u - 1))
                            for kc in range(NT):
                                ins = pe.transpose(bank[2 + u % 2][:, kc * P:(kc + 1) * P],
                                                   prob[:, u % 2, kc * P:(kc + 1) * P], ident)
                            ins.then_inc(pt_r, 1)
                        if k >= 3:
                            u = u0 + k - 3
                            pe.wait_ge(pt_e, l * UNITS + (u + 1))
                            if u >= 2:
                                pe.wait_ge(o_e, l * UNITS + (u - 1))
                            for kc in range(NT):
                                ins = pe.matmul(bank[6 + u % 2][0:HD, 0:P], v_of(k - 3, kc), probT[:, u % 2, kc, :],
                                                start=kc == 0, stop=kc == NT - 1)
                            ins.then_inc(o_r, 1)

                def gqa(k):
                    hd, t = GQA_UNITS[k]
                    return hd // 4, hd % 4, t
                attend(0, 32,
                       lambda k: qaT[gqa(k)[0] * HD:(gqa(k)[0] + 1) * HD, gqa(k)[1], gqa(k)[2] * P:(gqa(k)[2] + 1) * P],
                       lambda k: kaT[gqa(k)[0] * HD:(gqa(k)[0] + 1) * HD, :],
                       lambda k, kc: va[:, kc, gqa(k)[0] * HD:(gqa(k)[0] + 1) * HD])
                for hf in range(2):
                    pe.wait_ge(o_e, l * UNITS + (32 + 16 * hf))
                    for g in range(2 * NT):
                        t = g % NT
                        lat, nk, n, k = (qlT, 3, 384, 4) if g < NT else (kvlT, 2, 512, 5)
                        if t == 0:
                            weights(k + 2 * hf)
                        if g >= 2:
                            pe.wait_ge(nat_e, l * 16 + (hf * 8 + g - 1))
                        w = slot((k + 2 * hf) % R, nk, n)
                        for c in range(nk):
                            ins = pe.matmul(bank[6 + g % 2][:, 0:n], lat[:, c, t * P:(t + 1) * P], w[:, c, :],
                                            start=c == 0, stop=c == nk - 1)
                        ins.then_inc(nat_r, 1)
                    pe.wait_ge(rope_s, l * 4 + (2 * hf + 1))
                    for h in range(4):
                        transposes(TR_MLA + 8 * hf + h, [qn[:, t, h, :] for t in range(NT)], KD)
                    pe.wait_ge(rope_s, l * 4 + (2 * hf + 2))
                    for h in range(4):
                        transposes(TR_MLA + 8 * hf + 4 + h, [kn[:, t, h, :] for t in range(NT)], KD)
                    pe.wait_ge(tr_e, l * TR + (TR_MLA + 8 * hf + 8))
                    attend(32 + 16 * hf, 16,
                           lambda k: qbT[0:KD, k // NT, (k % NT) * P:(k % NT + 1) * P],
                           lambda k: kbT[0:KD, k // NT, :],
                           lambda k, kc: vb[:, kc, (k // NT) * HD:(k // NT + 1) * HD])
                pe.wait_ge(o_e, l * UNITS + UNITS)
                for j in range(NC):
                    h = j // 4
                    b0 = 4 * (j % 2)
                    cols = slice((j % 4) * P, (j % 4 + 1) * P)
                    if j >= 2:
                        pe.wait_ge(m_s, l * NC + (j - 1))
                    for q, (item, src, nk, s) in enumerate((((8, 12)[h], hT, NC, ga_r), ((9, 13)[h], hT, NC, gb_r),
                                                           ((10, 14)[h], oT, 4, ya_r), ((11, 15)[h], oT, 4, yb_r))):
                        if j % 4 == 0:
                            weights(item)
                        w = slot(item % R, nk, 512)
                        for c in range(nk):
                            ins = pe.matmul(bank[b0 + q][:, :], w[:, c, cols], src[:, c + (4 if q == 3 else 0), :],
                                            start=c == 0, stop=c == nk - 1)
                        ins.then_inc(s, 1)
                pe.wait_ge(m_s, l * NC + NC)
                for k in range(8):
                    n, t = k // NT, k % NT
                    if t == 0:
                        weights(16 + n)
                    if k >= 4:
                        pe.wait_ge(x1, l * 8 + (k - 3))
                    w = slot((16 + n) % R, NC, 512)
                    for c in range(NC):
                        ins = pe.matmul(bank[4 + k % 4][:, :], mT[:, c, t * P:(t + 1) * P], w[:, c, :],
                                        start=c == 0, stop=c == NC - 1)
                    ins.then_inc(wo_r, 1)
                norm_transposes(TR_N2, NT)
                pe.wait_ge(tr_e, l * TR + TR_X0)
                for t in range(NT):
                    for c in range(NC):
                        ins = pe.matmul(bank[2][:, t * E:(t + 1) * E], hT[:, c, t * P:(t + 1) * P], wr[:, c, :],
                                        start=c == 0, stop=c == NC - 1)
                ins.then_inc(lg_r, 1)
                pe.wait_ge(oh_s, l + 1)
                for t in range(NT + 1):
                    last = min(t, NT - 1)
                    for j in range(last + 1):
                        ins = pe.matmul(bank[3][:, t * E:(t + 1) * E], utri if j == t else ones[:, :], r_a[:, j, :],
                                        start=j == 0, stop=j == last)
                ins.then_inc(rk_r, 1)

                def token_transposes(g, p0, b, first=False):
                    xv = xg[:, b, :].rearrange("p (q c) -> p c q", c=NC)
                    for k in range(2):
                        pe.wait_ge(tr_e, g + (k - 1))
                        for c in range(4):
                            ins = pe.transpose(bank[(p0 + k) % 2][:, c * P:(c + 1) * P], xv[:, 4 * k + c, :], ident)
                        ins.then_inc(tr_r, 1)

                def up(tokens, w1s, w3s, s1, s3):
                    for s, bk, done in ((w1s, 4, s1), (w3s, 5, s3)):
                        w = slot(s, NC, F)
                        for c in range(NC):
                            ins = pe.matmul(bank[bk][:, :], tokens[:, c, :], w[:, c, :], start=c == 0, stop=c == NC - 1)
                        ins.then_inc(done, 1)

                def down(s, done):
                    w = slot(s, 4, D)
                    for n in range(2):
                        for c in range(4):
                            ins = pe.matmul(bank[6 + n][:, :], uT[:, c, :], w[:, c, n * 512:(n + 1) * 512],
                                            start=c == 0, stop=c == 3)
                        ins.then_inc(done, 1)

                def hidden_transposes(b):
                    for c in range(4):
                        ins = pe.transpose(bank[b][:, c * P:(c + 1) * P], u_s[:, c * P:(c + 1) * P], ident)
                    return ins

                def loaded(s, n):
                    pe.wait_ge(w_rdy[s], l * (16 * ITEMS // R) + n * 16)

                N0 = ADA_ITEMS // R + 1

                def expert(e, p, g, slots, loads, gat, first=False, last=False):
                    loaded(slots[0], loads[0])
                    pe.wait_ge(tr_e, g if first else g - 1)
                    for s, n, bk, done in ((slots[0], loads[0], 4, h1_r), (slots[1], loads[1], 5, h3_r)):
                        loaded(s, n)
                        wv = slot(s, NC, F)
                        for c in range(NC):
                            ins = pe.matmul(bank[bk][:, :], xsT[:, p, c, :], wv[:, c, :], start=c == 0, stop=c == NC - 1)
                        ins.then_inc(done, 1)
                    if not last:
                        pe.wait_ge(xg_s[1 - p], l * 128 + gat)
                        token_transposes(g, p, 1 - p)
                    if not first:
                        loaded(slots[2], loads[2])
                        pe.wait_ge(tr_e, g)
                        if not (isinstance(e, int) and e == 1):
                            pe.wait_ge(y_e, (l * E + e - 1) * 2)
                        down(slots[2], y_r)
                    pe.wait_ge(u_s_s, l * E + e + 1)
                    gu = g if last else g + 2
                    pe.wait_ge(tr_e, gu - 1)
                    hidden_transposes(1 if last else p).then_inc(tr_r, 1)

                pe.wait_ge(xg_s[0], l * 128 + 16)
                token_transposes(l * TR + TR_X0, 0, 0)
                expert(0, 0, l * TR + (TR_X0 + 2), (0, 1), (3 + N0, 3 + N0), 16, first=True)

                def items(e):
                    return [MIX_ITEMS + 2 + 3 * (e - 1) + q for q in range(3)]
                for e in (1, 2):
                    it = items(e)
                    expert(e, e % 2, l * TR + (TR_X0 + 2 + 3 * e), [k % R for k in it], [k // R + N0 for k in it],
                           16 * ((e + 1) // 2 + 1))
                with pe.Fori(0, 6) as i:
                    for r in range(2):
                        it = items(3 + r)
                        expert(2 * i + (3 + r), (3 + r) % 2, l * TR + (TR_X0 + 2 + 9 + 3 * r) + i * 6,
                               [k % R for k in it], [i + (k // R + N0) for k in it],
                               i * 16 + 16 * ((4 + r) // 2 + 1))
                it = items(15)
                expert(15, 1, l * TR + (TR_X0 + 2 + 45), [k % R for k in it], [k // R + N0 for k in it], 0, last=True)
                loaded(65 % R, 65 // R + N0)
                pe.wait_ge(tr_e, l * TR + TR)
                pe.wait_ge(y_e, (l * E + 15) * 2)
                down(65 % R, y_r)

                def body(e, first, n):
                    pe.wait_ge(ov_w, n * 48 + 48)
                    pe.wait_ge(ov_x, n * 16 + 16)
                    xv = xg[:, 0, :].rearrange("p (q c) -> p c q", c=NC)
                    for k in range(2):
                        for c in range(4):
                            ins = pe.transpose(bank[k][:, c * P:(c + 1) * P], xv[:, 4 * k + c, :], ident)
                        ins.then_inc(ov_t, 1)
                    pe.wait_ge(ov_te, n * 3 + 2)
                    up(xsT[:, 0, :, :], 0, 1, ov_h, ov_h)
                    pe.wait_ge(ov_u, n + 1)
                    hidden_transposes(0).then_inc(ov_t, 1)
                    pe.wait_ge(ov_te, n * 3 + 3)
                    down(2, ov_y)
                pe.wait_ge(y_e, l * 2 * E + 2 * E)
                wait(pe, ds_s, l + 1)
                extra_blocks(pe, n_ov, body)


def kernel(**inputs):
    import concourse.bacc as bacc
    from concourse.bass_utils import run_bass_kernel_spmd

    names = ["x", "c", "w_ada", "b_ada", "norm1", "w_in", "q_norm_a", "k_norm_a", "q_a_norm", "kv_norm",
             "w_q_b", "w_kv_b", "w_proj_a", "w_proj_b", "w_o", "norm2", "w_router", "router_bias",
             "w1", "w3", "w2", "norm_f"]
    nc = bacc.Bacc("TRN2", target_bir_lowering=False, num_devices=1)
    arrays = {f"in_{n}": np.ascontiguousarray(inputs[n]) for n in names}
    arrays["in_constants"] = constants()
    args = [nc.dram_tensor(n, a.shape, mybir.dt.from_np(a.dtype), kind="ExternalInput").ap() for n, a in arrays.items()]
    out = nc.dram_tensor("out_0", (1, SEQ, D), mybir.dt.float32, kind="ExternalOutput").ap()
    trunk(nc, *args, out)
    r = run_bass_kernel_spmd(nc, [arrays], core_ids=[0])
    return r.results[0]["out_0"]
```

```python
from contextlib import ExitStack

import numpy as np
import concourse.bass as bass
from concourse import mybir

P = 128
D = 1024
SEQ = 512
NT = SEQ // P
NC = D // P
DEPTH = 2
NMOD = 6
GRID_W = 64
THETA = 10000.0
EPS = 1e-6
HD = 64
RD = 32
KD = HD + RD
QL, KVL = 384, 256
QK_HEADS = 10
ZC = 1440
Z_ITEMS = ((0, 512), (512, 256), (768, 384), (1152, 288))
Z_V, Z_QL, Z_KVL, Z_KR = 640, 768, 1152, 1408
E = 16
EG = 4
F = 512
BIG = 3.0e38
R = 6
NONE = 2 * SEQ
MIX_ITEMS = 24
ITEMS = MIX_ITEMS + 3 * E
LOADS = [2 if k in (8, 11) else 1 for k in range(ITEMS)]
ADA_A, ADA_B = (4, 5, 6, 7), (9, 10, 12, 13)
ADA_ITEM = ADA_A + ADA_B
ADA_PRE = 4
ADA_IN = 8
TR = 98
UNITS = 64
TR_N1, TR_QK, TR_LAT, TR_N2, TR_X0 = 0, 8, 13, 42, 50
TR_MLA = (21, 31)
TR_ADA = (18, 19, 20, 29, 30, 39, 40, 41)
C_ID, C_UT, C_CA, C_SA, C_CB, C_SB, C_GW, C_EW, C_TK, C_RW, C_IO = 0, 128, 256, 384, 512, 576, 640, 644, 660, 664, 672
C_N = 800
GQA_UNITS = [(4 * s + j, t) for j in range(4) for s in range(2) for t in range(NT)]


def slot_loads(k):
    return sum(LOADS[j] for j in range(k % R, k + 1, R))


PRE = [DEPTH if s < ADA_PRE else 0 for s in range(R)]


def slot_total(s):
    return sum(LOADS[s::R])


def constants():
    c = np.zeros((P, C_N), np.float32)
    c[:, C_ID:C_ID + P] = np.eye(P, dtype=np.float32)
    c[:, C_UT:C_UT + P] = np.triu(np.ones((P, P), np.float32), 1)
    pos = np.arange(SEQ)
    row, col = (pos // GRID_W).astype(np.float32), (pos % GRID_W).astype(np.float32)
    for width, cc, cs in ((HD, C_CA, C_SA), (RD, C_CB, C_SB)):
        n = width // 4
        inv = (np.float32(1.0) / np.power(np.float32(THETA), np.arange(n, dtype=np.float32) / np.float32(n))).astype(np.float32)
        ang = np.concatenate([row[:, None] * inv, col[:, None] * inv], axis=-1).astype(np.float32)
        for at, f in ((cc, np.cos), (cs, np.sin)):
            t = f(ang.astype(np.float64)).astype(np.float32).reshape(NT, P, width // 2)
            c[:, at:at + NT * width // 2] = t.transpose(1, 0, 2).reshape(P, -1)
    c[:, C_GW:C_GW + EG] = EG - np.arange(EG)
    c[:, C_EW:C_EW + E] = E - np.arange(E)
    token = np.arange(NT)[None, :] * P + np.arange(P)[:, None]
    c[:, C_TK:C_TK + NT] = token
    for k in range(2):
        c[:, C_RW + k * NT:C_RW + (k + 1) * NT] = 2 * token + k - NONE
    c[:, C_IO:C_IO + P] = np.arange(P)
    return c


def trunk(nc, x_in, c_in, w_ada, b_ada, norm1, w_in, q_norm_a, k_norm_a, q_a_norm, kv_norm, w_q_b,
          w_kv_b, w_proj_a, w_proj_b, w_o, norm2, w_router, router_bias, w1, w3, w2, norm_f, consts, out):
    f32, i32 = mybir.dt.float32, mybir.dt.int32
    ALU = mybir.AluOpType
    ACT = mybir.ActivationFunctionType
    X = mybir.AxisListType.X

    b_ada_v = b_ada.rearrange("l (q o n) -> l q o n", n=512, o=1)
    mod_d = nc.dram_tensor("mod_d", [DEPTH, NMOD * D], f32, kind="Internal").ap()
    xn_d = nc.dram_tensor("xn_d", [SEQ, D], f32, kind="Internal").ap()
    ys_d = nc.dram_tensor("ys_d", [SEQ * 2, D], f32, kind="Internal").ap()

    mod_v = mod_d.rearrange("l (q o n) -> l q o n", n=512, o=1)

    ada_v = w_ada.rearrange("l (p c) (q n) -> l q p c n", c=NC, n=512)
    in_v = w_in.rearrange("l (p c) n -> l p c n", c=NC)
    qb_v = w_q_b.rearrange("l (c p) n -> l p c n", p=P)
    kvb_v = w_kv_b.rearrange("l (c p) n -> l p c n", p=P)
    pa_v = w_proj_a.rearrange("l (c p) n -> l p c n", p=P)
    pb_v = w_proj_b.rearrange("l (c p) n -> l p c n", p=P)
    wo_v = w_o.rearrange("l (c p) n -> l p c n", p=P)
    w1_v = w1.rearrange("l e (p c) f -> (l e) p c f", c=NC)
    w3_v = w3.rearrange("l e (p c) f -> (l e) p c f", c=NC)
    w2_v = w2.rearrange("l e (c p) n -> (l e) p c n", p=P)

    with ExitStack() as ctx:
        def sb(name, shape, dt=f32):
            return ctx.enter_context(nc.sbuf_tensor(name, shape, dt))

        def sem(name):
            return ctx.enter_context(nc.semaphore(name))

        ring = sb("ring", [P, R, 4096])
        x = sb("x", [P, NT, D])
        hT = sb("hT", [P, NC, SEQ])
        reg_a = sb("reg_a", [P, 4096])
        reg_b = sb("reg_b", [P, 5760])
        reg_c = sb("reg_c", [P, 3072])
        reg_d = sb("reg_d", [P, 2560])
        vb = sb("vb", [P, NT, 4 * HD])
        reg_f = sb("reg_f", [P, 2048])
        cst = sb("cst", [P, C_N])
        ones = sb("ones", [P, P])
        gain_qk = sb("gain_qk", [P, 2, HD])
        gain_l = sb("gain_l", [P, 5])
        gain_n = sb("gain_n", [P, 2 * DEPTH, NC])
        mod_c = sb("mod_c", [P, DEPTH * 2, NC])
        wr = sb("wr", [P, NC, E])
        rbias = sb("rbias", [P, E])
        kr = sb("kr", [P, NT, RD])
        ssq = sb("ssq", [P, NT])
        rstd = sb("rstd", [P, NT])
        stz = sb("stz", [P, NT, 12])
        nmax = sb("nmax", [P, 4])
        lsum = sb("lsum", [P, 4])
        linv = sb("linv", [P, 4])
        cur = sb("cur", [P, 4, NC])
        gain1, gain2 = sb("gain1", [P, NC]), sb("gain2", [P, NC])
        flag_i = sb("flag_i", [1, 1], i32)
        cond = sb("cond", [P, 2, NC])
        gw = sb("gw", [P, 2, NT])
        table = sb("table", [P, 2 * E], i32)
        cnt_i = sb("cnt_i", [P, E], i32)
        idx = sb("idx", [P, 2], i32)
        idy = sb("idy", [P, 2], i32)

        ident = cst[:, C_ID:C_ID + P]
        utri = cst[:, C_UT:C_UT + P]
        cos_a = cst[:, C_CA:C_CA + 128].rearrange("p (t n) -> p t n", t=NT)
        sin_a = cst[:, C_SA:C_SA + 128].rearrange("p (t n) -> p t n", t=NT)
        cos_b = cst[:, C_CB:C_CB + 64].rearrange("p (t n) -> p t n", t=NT)
        sin_b = cst[:, C_SB:C_SB + 64].rearrange("p (t n) -> p t n", t=NT)
        xn = reg_a[:, :].rearrange("p (t n) -> p t n", t=NT)
        oT = reg_a[:, :].rearrange("p (c n) -> p c n", c=8)
        cy = [r.rearrange("p (b k n) -> p b k n", b=2, k=2)[:, b] for r in (reg_a[:, :], hT[:, :, :].rearrange("p c n -> p (c n)")) for b in range(2)]
        z = reg_b[:, :].rearrange("p (t n) -> p t n", t=NT)
        qbT = reg_b[:, 0:2048].rearrange("p (h n) -> p h n", h=4)
        kbT = reg_b[:, 2048:4096].rearrange("p (h n) -> p h n", h=4)
        mT = reg_b[:, 0:4096].rearrange("p (c n) -> p c n", c=NC)
        xg = reg_b[:, 0:2048].rearrange("p (b n) -> p b n", b=2)
        xsT = reg_b[:, 2048:4096].rearrange("p (b c n) -> p b c n", b=2, c=NC)
        u_s = reg_b[:, 4096:4608]
        sg_e = reg_b[:, 4608:5120]
        uT = reg_b[:, 5120:5632].rearrange("p (c n) -> p c n", c=4)
        acc = reg_b[:, 4096:5120].rearrange("p (b n) -> p b n", b=2)
        mod_row = reg_b[0:1, 5120:5632]
        mod_bias = reg_b[32:33, 5120:5632]
        qaT = reg_c[:, 0:2048].rearrange("p (j n) -> p j n", j=4)
        kaT = reg_c[:, 2048:2560]
        va = reg_c[:, 2560:3072].rearrange("p (t n) -> p t n", t=NT)
        qn = reg_c[:, 0:1536].rearrange("p (t h n) -> p t h n", t=NT, h=4)
        kn = reg_c[:, 1536:3072].rearrange("p (t h n) -> p t h n", t=NT, h=4)
        g1_row, g2_row, nf_row = (reg_c[:, k * D:(k + 1) * D] for k in range(3))
        qlT = reg_d[:, 0:1536].rearrange("p (c n) -> p c n", c=3)
        kvlT = reg_d[:, 1536:2560].rearrange("p (c n) -> p c n", c=2)
        ysb = reg_d[:, 0:2048].rearrange("p (b n) -> p b n", b=2)
        prob = reg_f[:, 0:1024].rearrange("p (b n) -> p b n", b=2)
        probT = reg_f[:, 1024:2048].rearrange("p (b k n) -> p b k n", b=2, k=NT)
        zsq = reg_f[:, 0:1280].rearrange("p (b n) -> p b n", b=2)
        rot = reg_f[:, 1280:1920].rearrange("p (b n) -> p b n", b=2)
        rot_b = reg_f[:, 0:512].rearrange("p (b n) -> p b n", b=2)
        sg_m = reg_f[:, :].rearrange("p (b g n) -> p b g n", b=2, g=2)
        wo_t = reg_f[:, 0:1024].rearrange("p (b n) -> p b n", b=2)
        sq_j = reg_f[:, 1024:2048]

        def rt(k):
            return reg_f[:, k * 64:(k + 1) * 64].rearrange("p (t e) -> p t e", t=NT)
        score, biased, oh1, oh2, r_a, r_b, rank = (rt(k) for k in range(7))
        r_s = reg_f[:, 448:640]
        rank_k = reg_f[:, 736:744].rearrange("p (k t) -> p k t", k=2)
        chosen = reg_f[:, 768:1024].rearrange("p (k t n) -> p k t n", k=2, t=NT)
        slot_of = reg_f[:, 1024:2048].rearrange("p (q n) -> p q n", n=P)

        def scale1(c):
            return cur[:, 1, c:c + 1]

        def shift1(c):
            return cur[:, 0, c:c + 1]

        def scale2(c):
            return cur[:, 3, c:c + 1]

        def shift2(c):
            return cur[:, 2, c:c + 1]

        def slot(s, a, n):
            return ring[:, s, 0:a * n].rearrange("p (a n) -> p a n", a=a)

        def heads_q(k):
            return ring[:, k % R, 0:3 * 384].rearrange("p (a n) -> p a n", a=3)

        def heads_kv(k):
            return ring[:, k % R, 3 * 384:3 * 384 + 2 * 512].rearrange("p (a n) -> p a n", a=2)

        bank = [ctx.enter_context(nc.psum_tensor(f"bank{k}", [P, 512], f32)) for k in range(8)]

        c_in_s = sem("consts_loaded")
        x_in_s = sem("x_loaded")
        cond_in = sem("cond_loaded")
        cond_s = sem("cond_ready")
        ones_s = sem("ones_ready")
        cond_e = sem("cond_sigmoid")
        b_in = sem("ada_bias_loaded")
        ada_ps = sem("ada_psum_ready")
        ada_ev = sem("ada_psum_read")
        aa_s = sem("mod_chunks_summed")
        mb_s = sem("mod_bias_loaded")
        cur2_ld = sem("shift2_scale2_loaded")
        cur2_s = sem("scale2_ready")
        mod_st = sem("mod_stored")
        mod_ld = sem("mod_columns_loaded")
        cur_s = sem("layer_mod_ready")
        w_rdy = [sem(f"slot{k}_loaded") for k in range(R)]
        x2 = sem("x_after_moe")
        x1 = sem("x_after_mixer")
        sq_s = sem("square_sums")
        ms_s = sem("mean_squares")
        rt_s = sem("roots")
        xn_s = sem("normed")
        tr_r = sem("transposes_ready")
        tr_e = sem("transposes_read")
        z_r = sem("z_psum_ready")
        z_e = sem("z_psum_read")
        zsq_s = sem("z_squares")
        zl_s = sem("latent_square_sums")
        zst_s = sem("z_square_sums_reduced")
        zms_s = sem("z_mean_squares")
        zrt_s = sem("z_roots")
        qk_s = sem("heads_rotated")
        lat_s = sem("latents_normed_then_rotated_key")
        gl_s = sem("layer_gains_loaded")
        s_r = sem("scores_ready")
        mx_s = sem("row_max")
        ex_s = sem("exp_done")
        pn_s = sem("probs_normed")
        pt_r = sem("probsT_ready")
        pt_e = sem("probsT_read")
        o_r = sem("head_out_ready")
        o_e = sem("head_out_read")
        nat_r = sem("mla_psum_ready")
        nat_e = sem("mla_psum_read")
        rope_s = sem("mla_rotated")
        ga_r, gb_r, ya_r, yb_r = (sem(n) for n in ("gate_a_ready", "gate_b_ready", "proj_a_ready", "proj_b_ready"))
        sig_s = sem("gates_sigmoid")
        m_s = sem("merged")
        wo_r = sem("mixer_out_ready")
        row_ld = sem("gate_rows_loaded")
        xn_st = sem("normed_stored")
        lg_r = sem("logits_ready")
        sc_s = sem("router_scores")
        oh_s = sem("one_hots")
        rk_r = sem("ranks_ready")
        ds_s = sem("counts_and_slots")
        tp_r = sem("slot_table_psum_ready")
        tb_s = sem("slot_table_ready")
        ix_s = sem("gather_index_ready")
        iy_s = sem("scatter_index_ready")
        xg_s = [sem(f"tokens_gathered{k}") for k in range(2)]
        h1_r, h3_r = sem("h1_ready"), sem("h3_ready")
        sge_s = sem("h1_sigmoid")
        u_s_s = sem("expert_hidden")
        y_r, y_e = sem("expert_out_ready"), sem("expert_out_read")
        ys_st = [sem(f"expert_out_stored{k}") for k in range(2)]
        cg_s = [sem(f"token_outputs_loaded{t}") for t in range(NT)]
        ov_free = sem("extra_block_done")
        ov_w = sem("extra_weights_loaded")
        ov_sl = sem("extra_slots_of_tokens")
        ov_tp = sem("extra_table_psum_ready")
        ov_tb = sem("extra_table_ready")
        ov_i = sem("extra_indices_ready")
        ov_x = sem("extra_tokens_gathered")
        ov_t = sem("extra_transposed")
        ov_te = sem("extra_transposes_read")
        ov_h = sem("extra_h_ready")
        ov_g = sem("extra_sigmoid")
        ov_u = sem("extra_hidden")
        ov_y = sem("extra_out_ready")
        ov_ye = sem("extra_out_read")
        ov_st = sem("extra_out_stored")
        ov_all = sem("extra_pass_done")
        out_s = sem("out_ready")
        out_st = sem("out_stored")

        ticks = sem("ticks")

        block = ctx.enter_context(nc.Block())

        def wait(eng, s, value):
            eng.wait_ge(s, value)
            eng.sem_inc(ticks, 1)

        def extra_blocks(eng, blocks, tables, body, new_table=None):
            most = eng.value_load(flag_i[0:1, 0:1], min_val=0, max_val=SEQ)
            with eng.If(most > P):
                with eng.Fori(1, eng.snap((most + (P - 1)) >> 7)) as b:
                    if new_table is not None:
                        new_table(eng.snap(blocks), eng.snap(tables))
                    eng.reg_add(tables, tables, 1)
                    with eng.Fori(0, E) as e:
                        n = eng.value_load(cnt_i[0:1, bass.ds(e, 1)], min_val=0, max_val=SEQ)
                        with eng.If(n > b * P):
                            body(e, eng.snap(blocks))
                            eng.reg_add(blocks, blocks, 1)

        @block.sync
        def _(sp):
            sp.dma_start(cond[:, 0, :], c_in[0].rearrange("(p c) -> p c", c=NC)).then_inc(cond_in, 16)

            with sp.Fori(0, DEPTH) as l:
                for r in range(ADA_PRE):
                    wait(sp, ada_ps, l * ADA_PRE + (r + 1))
                    sp.dma_start(slot(r, NC, 512), ada_v[l, r]).then_inc(w_rdy[r], 16)

            n_ov, n_tab = sp.alloc_register("extra_blocks_sp"), sp.alloc_register("extra_tables_sp")
            sp.reg_mov(n_ov, 0)
            sp.reg_mov(n_tab, 0)
            wait(sp, ada_ps, ADA_PRE * (DEPTH + 1))
            wait(sp, mod_ld, 16 * DEPTH)
            with sp.Fori(0, DEPTH) as l:
                def load(k, dst_shape, src):
                    a, n = dst_shape
                    sp.dma_start(slot(k % R, a, n), src).then_inc(w_rdy[k % R], 16)

                def load_ada(i):
                    load(ADA_ITEM[i], (NC, 512), ada_v[l, ADA_PRE + i])

                def load_heads(k, hf):
                    sp.dma_start(heads_q(k), qb_v[l, :, :, hf * 384:(hf + 1) * 384]).then_inc(w_rdy[k % R], 16)
                    sp.dma_start(heads_kv(k), kvb_v[l, :, :, hf * 512:(hf + 1) * 512]).then_inc(w_rdy[k % R], 16)

                for i, (at, n) in enumerate(Z_ITEMS):
                    load(i, (NC, n), in_v[l, :, :, at:at + n])
                load_ada(0)
                load_ada(1)
                wait(sp, z_r, l * 16 + 4)
                load_ada(2)
                wait(sp, z_r, l * 16 + 8)
                load_ada(3)
                wait(sp, z_r, l * 16 + 12)
                load_heads(8, 0)
                wait(sp, z_r, l * 16 + 16)
                load_ada(4)
                wait(sp, aa_s, l * ADA_IN + 1)
                load_ada(5)
                wait(sp, aa_s, l * ADA_IN + 2)
                load_heads(11, 1)
                wait(sp, aa_s, l * ADA_IN + 3)
                load_ada(6)
                wait(sp, aa_s, l * ADA_IN + 4)
                load_ada(7)
                wait(sp, nat_r, l * 16 + 8)
                load(14, (NC, 512), in_v[l, :, :, ZC:ZC + 512])
                wait(sp, aa_s, l * ADA_IN + 5)
                load(15, (NC, 512), in_v[l, :, :, ZC + D:ZC + D + 512])
                wait(sp, aa_s, l * ADA_IN + 6)
                load(16, (4, 512), pa_v[l, :, :, 0:512])
                wait(sp, nat_r, l * 16 + 16)
                load(17, (4, 512), pb_v[l, :, :, 0:512])
                wait(sp, aa_s, l * ADA_IN + 7)
                load(18, (NC, 512), in_v[l, :, :, ZC + 512:ZC + D])
                wait(sp, aa_s, l * ADA_IN + 8)
                load(19, (NC, 512), in_v[l, :, :, ZC + D + 512:ZC + 2 * D])
                wait(sp, ga_r, l * 8 + 4)
                load(20, (4, 512), pa_v[l, :, :, 512:D])
                wait(sp, gb_r, l * 8 + 4)
                load(21, (4, 512), pb_v[l, :, :, 512:D])
                for n, s in ((0, ya_r), (1, yb_r)):
                    wait(sp, s, l * 8 + 4)
                    load(22 + n, (NC, 512), wo_v[l, :, :, n * 512:(n + 1) * 512])
                wait(sp, ga_r, l * 8 + 8)
                load(24, (NC, F), w1_v[l * E])
                wait(sp, gb_r, l * 8 + 8)
                load(25, (NC, F), w3_v[l * E])
                wait(sp, ya_r, l * 8 + 8)
                load(26, (NC, F), w1_v[l * E + 1])
                wait(sp, yb_r, l * 8 + 8)
                load(27, (NC, F), w3_v[l * E + 1])
                wait(sp, wo_r, l * 8 + 8)
                load(28, (4, D), w2_v[l * E])
                load(29, (NC, F), w1_v[l * E + 2])
                wait(sp, h1_r, l * E + 1)
                load(30, (NC, F), w3_v[l * E + 2])
                wait(sp, h3_r, l * E + 1)
                load(31, (4, D), w2_v[l * E + 1])
                with sp.Fori(0, 6) as i:
                    e0 = l * E + 2 * i
                    for r in range(2):
                        k = 32 + 3 * r
                        wait(sp, h1_r, e0 + (r + 2))
                        load(k, (NC, F), w1_v[e0 + (r + 3)])
                        wait(sp, h3_r, e0 + (r + 2))
                        load(k + 1, (NC, F), w3_v[e0 + (r + 3)])
                        wait(sp, y_r, (e0 + (r + 1)) * 2)
                        load(k + 2, (4, D), w2_v[e0 + (r + 2)])
                wait(sp, h1_r, l * E + 14)
                load(68, (NC, F), w1_v[l * E + 15])
                wait(sp, h3_r, l * E + 14)
                load(69, (NC, F), w3_v[l * E + 15])
                wait(sp, y_r, l * 2 * E + 26)
                load(70, (4, D), w2_v[l * E + 14])
                wait(sp, h1_r, l * E + 15)
                load(71, (4, D), w2_v[l * E + 15])
                wait(sp, y_r, l * 2 * E + 2 * E)

                def body(e, n):
                    wait(sp, ov_free, n + 1)
                    sp.dma_start(slot(0, NC, F), w1_v[l * E + e]).then_inc(ov_w, 16)
                    sp.dma_start(slot(1, NC, F), w3_v[l * E + e]).then_inc(ov_w, 16)
                    sp.dma_start(slot(2, 4, D), w2_v[l * E + e]).then_inc(ov_w, 16)
                wait(sp, ds_s, l + 1)
                extra_blocks(sp, n_ov, n_tab, body)
                for b in range(2):
                    wait(sp, ys_st[b], l * 128 + 128)
                wait(sp, ov_all, l + 1)
                for t in range(NT):
                    sp.dma_start(cy[t].rearrange("p k n -> p (k n)"), ys_d.rearrange("(t p k) n -> t p (k n)", p=P, k=2)[t]).then_inc(cg_s[t], 16)
            for t in range(NT):
                wait(sp, out_s, t + 1)
                sp.dma_start(out[0, t * P:(t + 1) * P, :], xn[:, t, :]).then_inc(out_st, 16)
            wait(sp, out_st, 16 * NT)

        @block.gpsimd
        def _(pool):
            pool.dma_start(cst[:, :], consts).then_inc(c_in_s, 16)
            pool.memset(ones[:, :], 1.0).then_inc(ones_s, 1)
            for t in range(NT):
                pool.dma_start(x[:, t, :], x_in[0, t * P:(t + 1) * P, :]).then_inc(x_in_s, 16)
            pool.dma_start(wr[:, :, :], w_router.rearrange("(p c) e -> p c e", c=NC)).then_inc(c_in_s, 16)
            pool.dma_start(rbias[:, :], router_bias.partition_broadcast(P)).then_inc(c_in_s, 16)
            for w, g in ((0, norm1), (1, norm2)):
                pool.dma_start(gain_n[:, w * DEPTH:(w + 1) * DEPTH, :], g.rearrange("l (p c) -> p l c", c=NC)).then_inc(c_in_s, 16)
            wait(pool, ones_s, 1)
            wait(pool, c_in_s, 16 * 5)
            wait(pool, mod_st, 16 * ADA_PRE * DEPTH)
            for l in range(DEPTH):
                pool.dma_start(mod_c[:, 2 * l:2 * l + 2, :],
                               mod_d[l, 0:2 * D].rearrange("(m p c) -> p m c", m=2, c=NC)).then_inc(mod_ld, 16)

            n_ov, n_tab = pool.alloc_register("extra_blocks_pool"), pool.alloc_register("extra_tables_pool")
            pool.reg_mov(n_ov, 0)
            pool.reg_mov(n_tab, 0)
            with pool.Fori(0, DEPTH) as l:
                wait(pool, x2, l * NT + NT)
                pool.dma_start(gain_qk[:, 0, :], q_norm_a[l].partition_broadcast(P)).then_inc(gl_s, 16)
                pool.dma_start(gain_qk[:, 1, :], k_norm_a[l].partition_broadcast(P)).then_inc(gl_s, 16)
                pool.dma_start(gain_l[:, 0:3], q_a_norm[l].rearrange("(c p) -> p c", p=P), allow_slow_non_contiguous=True).then_inc(gl_s, 16)
                pool.dma_start(gain_l[:, 3:5], kv_norm[l].rearrange("(c p) -> p c", p=P), allow_slow_non_contiguous=True).then_inc(gl_s, 16)
                for i in range(ADA_IN):
                    wait(pool, tr_r, l * TR + ((TR_ADA[i - 1] + 1) if i else TR_LAT + 5))
                    pool.dma_start(mod_bias, b_ada_v[l, ADA_PRE + i]).then_inc(mb_s, 16)
                    if i == ADA_IN - 1:
                        wait(pool, mod_st, (l * ADA_IN + (DEPTH * ADA_PRE + 6)) * 16)
                        pool.dma_start(cur[:, 2:4, :], mod_d[l, 3 * D:5 * D].rearrange("(m p c) -> p m c", m=2, c=NC)).then_inc(cur2_ld, 16)
                wait(pool, mod_st, (l * ADA_IN + (DEPTH * ADA_PRE + ADA_IN)) * 16)
                wait(pool, o_e, l * UNITS + UNITS)
                pool.dma_start(g1_row, mod_d[l, 2 * D:3 * D].partition_broadcast(P)).then_inc(row_ld, 16)
                pool.dma_start(g2_row, mod_d[l, 5 * D:6 * D].partition_broadcast(P)).then_inc(row_ld, 16)
                pool.dma_start(nf_row, norm_f.partition_broadcast(P)).then_inc(row_ld, 16)
                for t in range(NT):
                    wait(pool, xn_s, l * 2 * NT + NT + t + 1)
                    pool.dma_start(xn_d[t * P:(t + 1) * P, :], xn[:, t, :]).then_inc(xn_st, 16)
                wait(pool, xn_st, l * 64 + 64)

                def gather(e, b, n_wait):
                    if n_wait is not None:
                        wait(pool, tr_r, n_wait)
                    pool.tensor_copy(idx[:, b:b + 1], table[:, bass.ds(e, 1)]).then_inc(ix_s, 1)
                    wait(pool, ix_s, l * E + e + 1)
                    pool.indirect_dma_start(xg[:, b, :], None, xn_d, bass.IndirectOffsetOnAxis(idx[:, b:b + 1], 0),
                                            bounds_check=SEQ - 1, oob_is_err=False).then_inc(xg_s[b], 16)

                def scatter(e, b):
                    wait(pool, y_e, (l * E + e) * 2 + 2)
                    pool.tensor_copy(idy[:, b:b + 1], table[:, bass.ds(e + E, 1)]).then_inc(iy_s, 1)
                    wait(pool, iy_s, l * E + e + 1)
                    pool.indirect_dma_start(ys_d, bass.IndirectOffsetOnAxis(idy[:, b:b + 1], 0), ysb[:, b, :], None,
                                            bounds_check=2 * SEQ - 1, oob_is_err=False).then_inc(ys_st[b], 16)

                wait(pool, tb_s, l + 1)
                wait(pool, x1, l * 8 + 8)
                gather(0, 0, None)
                gather(1, 1, None)
                gather(2, 0, l * TR + (TR_X0 + 2))
                with pool.Fori(0, 6) as i:
                    for r in range(2):
                        f = 2 * i + r
                        gather(f + 3, (3 + r) % 2, l * TR + (TR_X0 + 4) + f * 3)
                        scatter(f, r)
                gather(15, 1, l * TR + (TR_X0 + 4 + 12 * 3))
                for f in range(12, E):
                    scatter(f, f % 2)

                def body(e, n):
                    wait(pool, ov_free, n + 1)
                    pool.tensor_copy(idx[:, 0:1], table[:, bass.ds(e, 1)]).then_inc(ov_i, 1)
                    pool.tensor_copy(idy[:, 0:1], table[:, bass.ds(e + E, 1)]).then_inc(ov_i, 1)
                    wait(pool, ov_i, n * 2 + 2)
                    pool.indirect_dma_start(xg[:, 0, :], None, xn_d, bass.IndirectOffsetOnAxis(idx[:, 0:1], 0),
                                            bounds_check=SEQ - 1, oob_is_err=False).then_inc(ov_x, 16)
                    wait(pool, ov_ye, n * 2 + 2)
                    pool.indirect_dma_start(ys_d, bass.IndirectOffsetOnAxis(idy[:, 0:1], 0), ysb[:, 0, :], None,
                                            bounds_check=2 * SEQ - 1, oob_is_err=False).then_inc(ov_st, 16)
                    wait(pool, ov_st, n * 16 + 16)
                    pool.sem_inc(ov_free, 1)
                for b in range(2):
                    wait(pool, ys_st[b], l * 128 + 128)
                extra_blocks(pool, n_ov, n_tab, body, lambda n, m: wait(pool, ov_tb, m + 1))
                pool.sem_inc(ov_all, 1)

        @block.scalar
        def _(act):
            A = act.activation
            act.wait_ge(cond_in, 16)
            A(cond[:, 1, :], cond[:, 0, :], ACT.Sigmoid).then_inc(cond_e, 1)
            with act.Fori(0, DEPTH) as l:
                for r in range(ADA_PRE):
                    act.dma_start(reg_b[0:1, 512 * r:512 * (r + 1)], b_ada_v[l, r]).then_inc(b_in, 16)
                for r in range(ADA_PRE):
                    wait(act, ada_ev, l * ADA_PRE + (ADA_PRE + r + 1))
                    act.dma_start(mod_v[l, r], reg_b[0:1, 512 * r:512 * (r + 1)]).then_inc(mod_st, 16)
                wait(act, mod_st, (l * ADA_PRE + ADA_PRE) * 16)

            n_ov, n_tab = act.alloc_register("extra_blocks_act"), act.alloc_register("extra_tables_act")
            act.reg_mov(n_ov, 0)
            act.reg_mov(n_tab, 0)

            def square(base, t):
                if t >= 1:
                    act.wait_ge(sq_s, base * NT + t)
                A(sq_j, x[:, t, :], ACT.Square, accum_out=ssq[:, t:t + 1]).then_inc(sq_s, 1)

            def root(base, t):
                act.wait_ge(ms_s, base * NT + (t + 1))
                A(ssq[:, t:t + 1], ssq[:, t:t + 1], ACT.Sqrt).then_inc(rt_s, 1)

            def modulated(l, g0, t, scale, shift):
                for k in range(2):
                    act.wait_ge(tr_r, l * TR + (g0 + 2 * t + k + 1))
                    for c in range(4):
                        cc = 4 * k + c
                        ins = A(hT[:, cc, t * P:(t + 1) * P], bank[(g0 + k) % 2][:, c * P:(c + 1) * P], ACT.Identity,
                                scale=scale(cc), bias=shift(cc))
                    ins.then_inc(tr_e, 1)

            def evac(l, g, dst, **kw):
                act.wait_ge(tr_r, l * TR + (g + 1))
                A(dst, bank[g % 2][0:dst.shape[0], 0:SEQ], ACT.Identity, **kw).then_inc(tr_e, 1)

            with act.Fori(0, DEPTH) as l:
                for t in range(NT):
                    act.wait_ge(x2, l * NT + (t + 1))
                    square(l * 2, t)
                for t in range(NT):
                    root(l * 2, t)
                act.wait_ge(cur_s, l + 1)
                for t in range(NT):
                    modulated(l, TR_N1, t, scale1, shift1)
                for i, (at, n) in enumerate(Z_ITEMS):
                    if i == 2:
                        for t in range(NT):
                            act.wait_ge(z_e, l * 16 + NT + t + 1)
                            if t >= 2:
                                act.wait_ge(zst_s, l * NT + t - 1)
                            A(zsq[:, t % 2, :], z[:, t, 0:640], ACT.Square).then_inc(zsq_s, 1)
                        act.wait_ge(zms_s, l * 2 + 1)
                        A(stz[:, :, 0:10], stz[:, :, 0:10], ACT.Sqrt).then_inc(zrt_s, 1)
                    for t in range(NT):
                        k = i * NT + t
                        act.wait_ge(z_r, l * 16 + (k + 1))
                        src = bank[2 + k % 4]
                        if i == 1:
                            A(va[:, t, :], src[:, P:2 * P], ACT.Copy)
                            A(z[:, t, at:at + P], src[:, 0:P], ACT.Copy).then_inc(z_e, 1)
                        elif i == 0:
                            A(z[:, t, 0:512].rearrange("p (j s d) -> p s j d", s=2, j=4),
                              src[:, :].rearrange("p (s j d) -> p s j d", s=2, j=4), ACT.Copy).then_inc(z_e, 1)
                        else:
                            A(z[:, t, at:at + n], src[:, 0:n], ACT.Copy).then_inc(z_e, 1)
                for t in range(NT):
                    act.wait_ge(z_e, l * 16 + 12 + t + 1)
                    if t >= 1:
                        act.wait_ge(zl_s, l * NT + t)
                    A(reg_f[:, 0:QL], z[:, t, Z_QL:Z_QL + QL], ACT.Square, accum_out=stz[:, t, 10:11])
                    A(reg_f[:, 512:512 + KVL], z[:, t, Z_KVL:Z_KVL + KVL], ACT.Square, accum_out=stz[:, t, 11:12]).then_inc(zl_s, 1)
                act.wait_ge(zms_s, l * 2 + 2)
                A(stz[:, :, 10:12], stz[:, :, 10:12], ACT.Sqrt).then_inc(zrt_s, 1)
                for j in range(4):
                    evac(l, TR_QK + j, qaT[:, j, :])
                evac(l, TR_QK + 4, kaT)
                act.wait_ge(gl_s, l * 64 + 64)
                for c in range(5):
                    evac(l, TR_LAT + c, (qlT[:, c, :] if c < 3 else kvlT[:, c - 3, :]), scale=gain_l[:, c:c + 1])

                def put_mod(i):
                    act.wait_ge(mod_st, (l * ADA_IN + (DEPTH * ADA_PRE + i)) * 16)
                    act.wait_ge(tr_r, l * TR + (TR_ADA[i] + 1))
                    A(mod_row, bank[TR_ADA[i] % 2][0:1, :], ACT.Copy).then_inc(tr_e, 1)
                    wait(act, tr_e, l * TR + (TR_ADA[i] + 1))
                    act.dma_start(mod_v[l, ADA_PRE + i], mod_row).then_inc(mod_st, 16)

                def attend(u0, n):
                    for k in range(n + 2):
                        if k < n:
                            u = u0 + k
                            act.wait_ge(mx_s, l * UNITS + (u + 1))
                            if u >= 2:
                                act.wait_ge(pt_r, l * UNITS + (u - 1))
                            A(prob[:, u % 2, :], bank[4 + u % 2][:, :], ACT.Exp, bias=nmax[:, u % 4:u % 4 + 1],
                              accum_out=lsum[:, u % 4:u % 4 + 1]).then_inc(ex_s, 1)
                        if k >= 2:
                            u = u0 + k - 2
                            act.wait_ge(pt_r, l * UNITS + (u + 1))
                            if u >= 2:
                                act.wait_ge(o_r, l * UNITS + (u - 1))
                            A(probT[:, u % 2, :, :], bank[2 + u % 2][:, :], ACT.Copy).then_inc(pt_e, 1)
                        if k < n and (u0 + k) % 8 == 5 and u0 + k >= 8:
                            put_mod((u0 + k) // 8 - 1)
                attend(0, 32)
                for hf in range(2):
                    for g in range(2 * NT):
                        t = g % NT
                        act.wait_ge(nat_r, l * 16 + (hf * 8 + g + 1))
                        src = bank[6 + g % 2]
                        if g < NT:
                            A(qn[:, t, :, :], src[:, 0:384], ACT.Copy, scale=float(KD) ** -0.5).then_inc(nat_e, 1)
                        else:
                            kv = src[:, :].rearrange("p (h n) -> p h n", h=4)
                            A(vb[:, t, :].rearrange("p (h n) -> p h n", h=4), kv[:, :, HD:2 * HD], ACT.Copy)
                            A(kn[:, t, :, 0:HD], kv[:, :, 0:HD], ACT.Copy).then_inc(nat_e, 1)
                    for h in range(4):
                        evac(l, TR_MLA[hf] + h, qbT[0:KD, h, :])
                    for h in range(4):
                        evac(l, TR_MLA[hf] + 4 + h, kbT[0:KD, h, :])
                    attend(32 + 16 * hf, 16)
                put_mod(7)
                for j in range(NC):
                    if j >= 2:
                        act.wait_ge(m_s, l * NC + (j - 1))
                    else:
                        act.wait_ge(o_e, l * UNITS + UNITS)
                    act.wait_ge(ga_r, l * NC + (j + 1))
                    A(sg_m[:, j % 2, 0, :], bank[4 * (j % 2)][:, :], ACT.Sigmoid)
                    act.wait_ge(gb_r, l * NC + (j + 1))
                    A(sg_m[:, j % 2, 1, :], bank[4 * (j % 2) + 1][:, :], ACT.Sigmoid).then_inc(sig_s, 1)
                act.wait_ge(cur2_s, l + 1)
                for t in range(NT):
                    act.wait_ge(x1, l * 8 + 2 * (t + 1))
                    square(l * 2 + 1, t)
                    root(l * 2 + 1, t)
                    modulated(l, TR_N2, t, scale2, shift2)
                act.wait_ge(lg_r, l + 1)
                A(reg_f[:, 0:64], bank[2][:, 0:64], ACT.Sigmoid).then_inc(sc_s, 1)

                def tokens_out(g, b, p0):
                    for k in range(2):
                        act.wait_ge(tr_r, g + (k + 1))
                        for c in range(4):
                            cc = 4 * k + c
                            ins = A(xsT[:, b, cc, :], bank[(p0 + k) % 2][:, c * P:(c + 1) * P], ACT.Identity,
                                    scale=scale2(cc), bias=shift2(cc))
                        ins.then_inc(tr_e, 1)

                def expert(e, p, g, first=False, last=False):
                    act.wait_ge(h1_r, l * E + e + 1)
                    A(sg_e, bank[4][:, :], ACT.Sigmoid).then_inc(sge_s, 1)
                    if not last:
                        tokens_out(g, 1 - p, p)
                    gu = g if last else g + 2
                    act.wait_ge(tr_r, gu + 1)
                    A(uT[:, :, :], bank[(p if not last else 1)][:, :], ACT.Copy).then_inc(tr_e, 1)

                tokens_out(l * TR + TR_X0, 0, 0)
                expert(0, 0, l * TR + TR_X0 + 2, first=True)
                for e in (1, 2):
                    expert(e, e % 2, l * TR + (TR_X0 + 2 + 3 * e))
                with act.Fori(0, 6) as i:
                    for r in range(2):
                        e = 2 * i + (3 + r)
                        expert(e, (3 + r) % 2, l * TR + (TR_X0 + 2 + 9 + 3 * r) + i * 6)
                expert(15, 1, l * TR + (TR_X0 + 2 + 45), last=True)

                def body(e, n):
                    for k in range(2):
                        act.wait_ge(ov_t, n * 3 + (k + 1))
                        for c in range(4):
                            cc = 4 * k + c
                            ins = A(xsT[:, 0, cc, :], bank[k][:, c * P:(c + 1) * P], ACT.Identity,
                                    scale=scale2(cc), bias=shift2(cc))
                        ins.then_inc(ov_te, 1)
                    act.wait_ge(ov_h, n * 2 + 1)
                    A(sg_e, bank[4][:, :], ACT.Sigmoid).then_inc(ov_g, 1)
                    act.wait_ge(ov_t, n * 3 + 3)
                    A(uT[:, :, :], bank[0][:, :], ACT.Copy).then_inc(ov_te, 1)
                wait(act, ds_s, l + 1)
                extra_blocks(act, n_ov, n_tab, body)
            for t in range(NT):
                act.wait_ge(x2, DEPTH * NT + t + 1)
                square(2 * DEPTH, t)
            for t in range(NT):
                root(2 * DEPTH, t)

        @block.vector
        def _(v):
            TT, TS, STT = v.tensor_tensor, v.tensor_scalar, v.scalar_tensor_tensor
            n_ov, n_tab = v.alloc_register("extra_blocks_dve"), v.alloc_register("extra_tables_dve")
            v.reg_mov(n_ov, 0)
            v.reg_mov(n_tab, 0)
            v.sem_inc(ada_ps, ADA_PRE)
            v.sem_inc(ada_ev, ADA_PRE)
            v.sem_inc(ov_free, 1)
            v.wait_ge(cond_e, 1)
            TT(cond[:, 0, :], cond[:, 0, :], cond[:, 1, :], ALU.mult).then_inc(cond_s, 1)
            with v.Fori(0, DEPTH) as l:
                for r in range(ADA_PRE):
                    v.wait_ge(b_in, (l * ADA_PRE + ADA_PRE) * 16)
                    v.wait_ge(ada_ps, l * ADA_PRE + (ADA_PRE + r + 1))
                    row = reg_b[0:1, 512 * r:512 * (r + 1)]
                    TT(row, bank[r][0:1, :], row, ALU.add).then_inc(ada_ev, 1)
            v.wait_ge(x_in_s, 16 * NT)
            v.sem_inc(x2, NT)
            v.wait_ge(c_in_s, 16 * 5)

            def mean_square(base, t):
                v.wait_ge(sq_s, base * NT + (t + 1))
                TS(ssq[:, t:t + 1], ssq[:, t:t + 1], 1.0 / D, EPS, ALU.mult, ALU.add).then_inc(ms_s, 1)

            def scaled(base, t):
                v.wait_ge(rt_s, base * NT + (t + 1))
                v.reciprocal(rstd[:, t:t + 1], ssq[:, t:t + 1])
                v.drain()
                return TS(xn[:, t, :], x[:, t, :], rstd[:, t:t + 1], None, ALU.mult).then_inc(xn_s, 1)

            def rotate(x1v, x2v, cos, sin, ta, tb):
                TT(ta, x2v, sin, ALU.mult)
                TT(tb, x1v, sin, ALU.mult)
                v.drain()
                TT(x1v, x1v, cos, ALU.mult)
                TT(x2v, x2v, cos, ALU.mult)
                v.drain()
                TT(x1v, x1v, ta, ALU.subtract)
                return TT(x2v, x2v, tb, ALU.add)

            with v.Fori(0, DEPTH) as l:
                v.tensor_copy(gain2[:, :], gain_n[:, bass.ds(l + DEPTH, 1), :].rearrange("p o c -> p (o c)"))
                v.tensor_copy(gain1[:, :], gain_n[:, bass.ds(l, 1), :].rearrange("p o c -> p (o c)"))
                for t in range(NT):
                    mean_square(l * 2, t)
                for t in range(NT):
                    scaled(l * 2, t)
                v.wait_ge(mod_ld, 16 * DEPTH)
                v.tensor_copy(cur[:, 0:2, :], mod_c[:, bass.ds(l * 2, 2), :])
                v.drain()
                STT(cur[:, 1, :], cur[:, 1, :], 1.0, gain1[:, :], ALU.add, ALU.mult).then_inc(cur_s, 1)
                for t in range(NT):
                    v.wait_ge(zsq_s, l * NT + (t + 1))
                    v.tensor_reduce(stz[:, t, 0:10], zsq[:, t % 2, :].rearrange("p (h n) -> p h n", n=HD), X, ALU.add).then_inc(zst_s, 1)
                v.drain()
                TS(stz[:, :, 0:10], stz[:, :, 0:10], 1.0 / HD, EPS, ALU.mult, ALU.add).then_inc(zms_s, 1)
                v.wait_ge(gl_s, l * 64 + 64)
                TS(gain_qk[:, 0, :], gain_qk[:, 0, :], float(HD) ** -0.5, None, ALU.mult)
                v.wait_ge(zrt_s, l * 2 + 1)
                v.reciprocal(stz[:, :, 0:10], stz[:, :, 0:10])
                v.drain()
                for t in range(NT):
                    heads = z[:, t, 0:640].rearrange("p (h n) -> p h n", n=HD)
                    TT(heads, heads, stz[:, t, 0:10].unsqueeze(2).broadcast_to([P, QK_HEADS, HD]), ALU.mult)
                    v.drain()
                    TT(heads[:, 0:8, :], heads[:, 0:8, :], gain_qk[:, 0:1, :].broadcast_to([P, 8, HD]), ALU.mult)
                    TT(heads[:, 8:10, :], heads[:, 8:10, :], gain_qk[:, 1:2, :].broadcast_to([P, 2, HD]), ALU.mult)
                    v.drain()
                    rr = [rot[:, k, :].rearrange("p (h n) -> p h n", n=32) for k in range(2)]
                    rotate(heads[:, :, 0:32], heads[:, :, 32:64],
                           cos_a[:, t:t + 1, :].broadcast_to([P, QK_HEADS, 32]),
                           sin_a[:, t:t + 1, :].broadcast_to([P, QK_HEADS, 32]), rr[0], rr[1]).then_inc(qk_s, 1)
                v.wait_ge(zl_s, l * NT + NT)
                TS(stz[:, :, 10:11], stz[:, :, 10:11], 1.0 / QL, EPS, ALU.mult, ALU.add)
                TS(stz[:, :, 11:12], stz[:, :, 11:12], 1.0 / KVL, EPS, ALU.mult, ALU.add).then_inc(zms_s, 1)
                v.wait_ge(zrt_s, l * 2 + 2)
                v.reciprocal(stz[:, :, 10:12], stz[:, :, 10:12])
                v.drain()
                for t in range(NT):
                    TS(z[:, t, Z_QL:Z_QL + QL], z[:, t, Z_QL:Z_QL + QL], stz[:, t, 10:11], None, ALU.mult)
                    ins = TS(z[:, t, Z_KVL:Z_KVL + KVL], z[:, t, Z_KVL:Z_KVL + KVL], stz[:, t, 11:12], None, ALU.mult)
                ins.then_inc(lat_s, 1)
                krv = z[:, :, Z_KR:Z_KR + RD]
                rk2 = [rot[:, k, 0:64].rearrange("p (t n) -> p t n", t=NT) for k in range(2)]
                rotate(krv[:, :, 0:16], krv[:, :, 16:32], cos_b, sin_b, rk2[0], rk2[1])
                v.drain()
                v.tensor_copy(kr[:, :, :], krv).then_inc(lat_s, 1)
                v.drain()

                def mod_chunk(u):
                    i, c = u // 8, u % 8
                    k = ADA_ITEM[i]
                    w = slot(k % R, NC, 512)[:, c, :]
                    if c == 0:
                        v.wait_ge(w_rdy[k % R], l * (16 * slot_total(k % R)) + 16 * (PRE[k % R] + slot_loads(k)))
                        if i >= 2:
                            v.wait_ge(tr_r, l * TR + (TR_ADA[i - 2] + 1))
                        return TS(acc[:, i % 2, :], w, cond[:, 0, c:c + 1], None, ALU.mult)
                    return STT(acc[:, i % 2, :], w, cond[:, 0, c:c + 1], acc[:, i % 2, :], ALU.mult, ALU.add)

                def attend(u0, n, heads):
                    for k in range(n + 3):
                        if k < n:
                            u = u0 + k
                            v.wait_ge(s_r, l * UNITS + (u + 1))
                            v.tensor_reduce(nmax[:, u % 4:u % 4 + 1], bank[4 + u % 2][:, :], X, ALU.max, negate=True).then_inc(mx_s, 1)
                        if 1 <= k < n + 1:
                            u = u0 + k - 1
                            v.wait_ge(ex_s, l * UNITS + (u + 1))
                            v.reciprocal(linv[:, u % 4:u % 4 + 1], lsum[:, u % 4:u % 4 + 1])
                            v.drain()
                            TS(prob[:, u % 2, :], prob[:, u % 2, :], linv[:, u % 4:u % 4 + 1], None, ALU.mult).then_inc(pn_s, 1)
                        if k < n:
                            ins = mod_chunk(u0 + k)
                            if (u0 + k) % 8 == 7:
                                ins.then_inc(aa_s, 1)
                        if k >= 3:
                            u = u0 + k - 3
                            hd, t = heads[k - 3]
                            v.wait_ge(o_r, l * UNITS + (u + 1))
                            v.tensor_copy(oT[(hd % 2) * HD:(hd % 2 + 1) * HD, hd // 2, t * P:(t + 1) * P],
                                          bank[6 + u % 2][0:HD, 0:P]).then_inc(o_e, 1)
                attend(0, 32, GQA_UNITS)
                for hf in range(2):
                    v.wait_ge(nat_e, l * 16 + (hf * 8 + 4))
                    r4 = [rot_b[:, k, :].rearrange("p (t h n) -> p t h n", t=NT, h=4) for k in range(2)]
                    cb = cos_b.unsqueeze(2).broadcast_to([P, NT, 4, 16])
                    sn = sin_b.unsqueeze(2).broadcast_to([P, NT, 4, 16])
                    rotate(qn[:, :, :, HD:HD + 16], qn[:, :, :, HD + 16:KD], cb, sn, r4[0], r4[1]).then_inc(rope_s, 1)
                    v.wait_ge(nat_e, l * 16 + (hf * 8 + 8))
                    v.tensor_copy(kn[:, :, :, HD:KD], kr[:, :, :].unsqueeze(2).broadcast_to([P, NT, 4, RD])).then_inc(rope_s, 1)
                    attend(32 + 16 * hf, 16, [(8 + 4 * hf + h, t) for h in range(4) for t in range(NT)])
                v.wait_ge(cur2_ld, l * 16 + 16)
                STT(cur[:, 3, :], cur[:, 3, :], 1.0, gain2[:, :], ALU.add, ALU.mult).then_inc(cur2_s, 1)
                for j in range(NC):
                    v.wait_ge(sig_s, l * NC + (j + 1))
                    v.wait_ge(ya_r, l * NC + (j + 1))
                    TT(mT[:, j, :], bank[4 * (j % 2) + 2][:, :], sg_m[:, j % 2, 0, :], ALU.mult)
                    v.wait_ge(yb_r, l * NC + (j + 1))
                    TT(sg_m[:, j % 2, 1, :], bank[4 * (j % 2) + 3][:, :], sg_m[:, j % 2, 1, :], ALU.mult)
                    v.drain()
                    TT(mT[:, j, :], mT[:, j, :], sg_m[:, j % 2, 1, :], ALU.add).then_inc(m_s, 1)
                v.wait_ge(row_ld, l * 48 + 48)
                for k in range(8):
                    t, n = k // 2, k % 2
                    v.wait_ge(wo_r, l * 8 + (k + 1))
                    TT(wo_t[:, k % 2, :], bank[4 + k % 4][:, :], g1_row[:, n * 512:(n + 1) * 512], ALU.mult)
                    v.drain()
                    xs = x[:, t, n * 512:(n + 1) * 512]
                    TT(xs, xs, wo_t[:, k % 2, :], ALU.add).then_inc(x1, 1)
                    if n == 1:
                        mean_square(l * 2 + 1, t)
                        scaled(l * 2 + 1, t)

                def top1(vals, ramp, onehot, tmp, mx):
                    n = vals.shape[2]
                    v.tensor_reduce(mx, vals, X, ALU.max)
                    v.drain()
                    TT(tmp, vals, mx.unsqueeze(2).broadcast_to([P, NT, n]), ALU.is_equal)
                    v.drain()
                    TT(tmp, tmp, ramp.unsqueeze(1).broadcast_to([P, NT, n]), ALU.mult)
                    v.drain()
                    v.tensor_reduce(mx, tmp, X, ALU.max)
                    v.drain()
                    TT(onehot, tmp, mx.unsqueeze(2).broadcast_to([P, NT, n]), ALU.is_equal)
                    v.drain()
                v.wait_ge(sc_s, l + 1)
                TT(biased, score, rbias[:, :].unsqueeze(1).broadcast_to([P, NT, E]), ALU.add)
                v.drain()
                bg = biased.rearrange("p t (g e) -> p (t g) e", g=EG)
                ps = reg_f[:, 640:736].rearrange("p (g k) -> p g k", k=6)
                TT(ps[:, :, 0:3], bg[:, :, 0:3], bg[:, :, 1:4], ALU.add)
                TT(ps[:, :, 3:5], bg[:, :, 0:2], bg[:, :, 2:4], ALU.add)
                TT(ps[:, :, 5:6], bg[:, :, 0:1], bg[:, :, 3:4], ALU.add)
                v.drain()
                gs = r_s[:, 0:16].rearrange("p (t g) -> p t g", t=NT)
                gt = r_s[:, 16:32].rearrange("p (t g) -> p t g", t=NT)
                gh = r_s[:, 32:48].rearrange("p (t g) -> p t g", t=NT)
                mx = r_s[:, 48:52]
                v.tensor_reduce(r_s[:, 0:16], ps, X, ALU.max)
                v.drain()
                top1(gs, cst[:, C_GW:C_GW + EG], gh, gt, mx)
                sel = r_s[:, 32:48].unsqueeze(2).broadcast_to([P, NT * EG, EG])
                ra_g = r_a.rearrange("p t (g e) -> p (t g) e", g=EG)
                TT(ra_g, bg, sel, ALU.mult)
                TS(r_s[:, 64:80], r_s[:, 32:48], 1.0, BIG, ALU.subtract, ALU.mult)
                v.drain()
                TT(ra_g, ra_g, r_s[:, 64:80].unsqueeze(2).broadcast_to([P, NT * EG, EG]), ALU.add)
                v.drain()
                ew = cst[:, C_EW:C_EW + E]
                top1(r_a, ew, oh1, r_b, mx)
                TT(r_b, r_a, oh1, ALU.mult)
                v.drain()
                TT(r_a, r_a, r_b, ALU.subtract)
                v.drain()
                STT(r_a, oh1, -BIG, r_a, ALU.mult, ALU.add)
                v.drain()
                top1(r_a, ew, oh2, r_b, mx)
                TT(r_a, oh1, oh2, ALU.add).then_inc(oh_s, 1)
                TT(r_b, oh1, score, ALU.mult)
                v.drain()
                v.tensor_reduce(gw[:, 0, :], r_b, X, ALU.add)
                v.drain()
                TT(r_b, oh2, score, ALU.mult)
                v.drain()
                v.tensor_reduce(gw[:, 1, :], r_b, X, ALU.add)
                v.drain()
                TT(r_s[:, 52:56], gw[:, 0, :], gw[:, 1, :], ALU.add)
                v.drain()
                v.reciprocal(r_s[:, 56:60], r_s[:, 52:56])
                v.drain()
                for k in range(2):
                    TT(gw[:, k, :], gw[:, k, :], r_s[:, 56:60], ALU.mult)
                v.wait_ge(rk_r, l + 1)
                v.tensor_copy(cnt_i[:, :], bank[3][:, 64:80])
                v.tensor_reduce(r_s[0:1, 160:161], bank[3][0:1, 64:80], X, ALU.max)
                v.tensor_copy(rank, bank[3][:, 0:64].rearrange("p (t e) -> p t e", t=NT))
                v.drain()
                v.tensor_copy(flag_i[:, :], r_s[0:1, 160:161])
                for k, oh, tmp in ((0, oh1, r_b), (1, oh2, biased)):
                    TT(tmp, oh, rank, ALU.mult)
                    TT(chosen[:, k, :, 0:E], oh, cst[:, C_TK:C_TK + NT].unsqueeze(2).broadcast_to([P, NT, E]), ALU.mult)
                    TT(chosen[:, k, :, E:2 * E], oh,
                       cst[:, C_RW + k * NT:C_RW + (k + 1) * NT].unsqueeze(2).broadcast_to([P, NT, E]), ALU.mult)
                v.drain()
                v.tensor_reduce(rank_k[:, 0, :], r_b, X, ALU.add)
                v.tensor_reduce(rank_k[:, 1, :], biased, X, ALU.add)
                v.drain()

                def slots_of_tokens(done):
                    for q in range(2 * NT):
                        ins = TS(slot_of[:, q, :], cst[:, C_IO:C_IO + P], rank_k[:, q // NT, q % NT:q % NT + 1], None, ALU.is_equal)
                    ins.then_inc(done, 1)

                def take_table(done):
                    v.tensor_copy(table[:, 0:E], bank[3][:, P:P + E])
                    TS(table[:, E:2 * E], bank[3][:, P + E:P + 2 * E], float(NONE), None, ALU.add).then_inc(done, 1)
                slots_of_tokens(ds_s)
                v.wait_ge(tp_r, l + 1)
                take_table(tb_s)

                def hidden(at):
                    v.wait_ge(sge_s, at + 1)
                    TT(u_s, bank[4][:, :], sg_e, ALU.mult)
                    v.drain()
                    v.wait_ge(h3_r, at + 1)
                    TT(u_s, bank[5][:, :], u_s, ALU.mult).then_inc(u_s_s, 1)

                def put_out(f, p):
                    for n in range(2):
                        v.wait_ge(y_r, (l * E + f) * 2 + (n + 1))
                        cols = slice(n * 512, (n + 1) * 512)
                        TT(ysb[:, p, cols], bank[6 + n][:, :], g2_row[:, cols], ALU.mult).then_inc(y_e, 1)
                for e in range(3):
                    hidden(l * E + e)
                    if e:
                        put_out(e - 1, (e - 1) % 2)
                with v.Fori(0, 6) as i:
                    for r in range(2):
                        hidden(l * E + 2 * i + (3 + r))
                        v.wait_ge(ys_st[r], l * 128 + (i * 16 + 16))
                        put_out(2 * i + (2 + r), r)
                hidden(l * E + 15)
                for f in (14, 15):
                    v.wait_ge(ys_st[f % 2], l * 128 + 112)
                    put_out(f, f % 2)

                def body(e, n):
                    v.wait_ge(ov_g, n + 1)
                    TT(u_s, bank[4][:, :], sg_e, ALU.mult)
                    v.drain()
                    v.wait_ge(ov_h, n * 2 + 2)
                    TT(u_s, bank[5][:, :], u_s, ALU.mult).then_inc(ov_u, 1)
                    for h in range(2):
                        v.wait_ge(ov_y, n * 2 + (h + 1))
                        cols = slice(h * 512, (h + 1) * 512)
                        TT(ysb[:, 0, cols], bank[6 + h][:, :], g2_row[:, cols], ALU.mult).then_inc(ov_ye, 1)

                def new_table(n, m):
                    v.wait_ge(ov_free, n + 1)
                    TS(rank_k, rank_k, -float(P), None, ALU.add)
                    v.drain()
                    slots_of_tokens(ov_sl)
                    v.wait_ge(ov_tp, m + 1)
                    take_table(ov_tb)
                v.wait_ge(ys_st[0], l * 128 + 128)
                v.wait_ge(ys_st[1], l * 128 + 128)
                wait(v, ds_s, l + 1)
                extra_blocks(v, n_ov, n_tab, body, new_table)

                for t in range(NT):
                    v.wait_ge(cg_s[t], l * 16 + 16)
                    a, b = cy[t][:, 0, :], cy[t][:, 1, :]
                    STT(x[:, t, :], a, gw[:, 0, t:t + 1], x[:, t, :], ALU.mult, ALU.add)
                    v.drain()
                    STT(x[:, t, :], b, gw[:, 1, t:t + 1], x[:, t, :], ALU.mult, ALU.add).then_inc(x2, 1)
            for t in range(NT):
                mean_square(2 * DEPTH, t)
            for t in range(NT):
                scaled(2 * DEPTH, t)
                v.drain()
                TT(xn[:, t, :], xn[:, t, :], nf_row, ALU.mult).then_inc(out_s, 1)

        @block.tensor
        def _(pe):
            n_ov, n_tab = pe.alloc_register("extra_blocks_pe"), pe.alloc_register("extra_tables_pe")
            pe.reg_mov(n_ov, 0)
            pe.reg_mov(n_tab, 0)
            pe.wait_ge(cond_s, 1)
            with pe.Fori(0, DEPTH) as l:
                for r in range(ADA_PRE):
                    pe.wait_ge(w_rdy[r], l * 16 + 16)
                    pe.wait_ge(ada_ev, l * ADA_PRE + (r + 1))
                    for c in range(NC):
                        ins = pe.matmul(bank[r][0:1, :], cond[:, 0, c:c + 1], slot(r, NC, 512)[:, c, :],
                                        start=c == 0, stop=c == NC - 1)
                    ins.then_inc(ada_ps, 1)
            pe.wait_ge(ones_s, 1)
            pe.wait_ge(c_in_s, 16 * 5)

            with pe.Fori(0, DEPTH) as l:
                def weights(k):
                    pe.wait_ge(w_rdy[k % R], l * (16 * slot_total(k % R)) + 16 * (PRE[k % R] + slot_loads(k)))

                def transposes(g, srcs, rows=P):
                    if g >= 2:
                        pe.wait_ge(tr_e, l * TR + (g - 1))
                    for t, src in enumerate(srcs):
                        ins = pe.transpose(bank[g % 2][0:rows, t * P:(t + 1) * P], src, ident)
                    ins.then_inc(tr_r, 1)

                def norm_transposes(g0, n0, t):
                    pe.wait_ge(xn_s, l * 2 * NT + (n0 + t + 1))
                    xv = xn[:, t, :].rearrange("p (q c) -> p c q", c=NC)
                    for k in range(2):
                        transposes(g0 + 2 * t + k, [xv[:, 4 * k + c, :] for c in range(4)])

                for t in range(NT):
                    norm_transposes(TR_N1, 0, t)
                for i, (at, n) in enumerate(Z_ITEMS):
                    weights(i)
                    w = slot(i, NC, n)
                    for t in range(NT):
                        k = i * NT + t
                        if i == 0:
                            pe.wait_ge(tr_e, l * TR + (TR_N1 + 2 * t + 2))
                        if k >= 4:
                            pe.wait_ge(z_e, l * 16 + (k - 3))
                        for c in range(NC):
                            ins = pe.matmul(bank[2 + k % 4][:, 0:n], hT[:, c, t * P:(t + 1) * P], w[:, c, :],
                                            start=c == 0, stop=c == NC - 1)
                        ins.then_inc(z_r, 1)
                pe.wait_ge(qk_s, l * 4 + 4)
                for j in range(4):
                    transposes(TR_QK + j, [z[:, t, j * P:(j + 1) * P] for t in range(NT)])
                transposes(TR_QK + 4, [z[:, t, 512:640] for t in range(NT)])
                pe.wait_ge(lat_s, l * 2 + 1)
                for c in range(5):
                    at = Z_QL + c * P
                    transposes(TR_LAT + c, [z[:, t, at:at + P] for t in range(NT)])
                pe.wait_ge(tr_e, l * TR + TR_ADA[0])

                def mod_sum(i):
                    g = TR_ADA[i]
                    pe.wait_ge(aa_s, l * ADA_IN + (i + 1))
                    pe.wait_ge(mb_s, l * (16 * ADA_IN) + 16 * (i + 1))
                    pe.wait_ge(tr_e, l * TR + (g - 1))
                    pe.matmul(bank[g % 2][0:1, :], ones[:, 0:1], acc[:, i % 2, :], start=True, stop=False)
                    pe.matmul(bank[g % 2][0:1, :], ones[32:33, 0:1], mod_bias, start=False, stop=True).then_inc(tr_r, 1)

                def attend(u0, n, q_of, k_of, v_of):
                    for k in range(n + 3):
                        if k < n:
                            u = u0 + k
                            if u >= 2:
                                pe.wait_ge(ex_s, l * UNITS + (u - 1))
                            pe.matmul(bank[4 + u % 2][:, :], q_of(k), k_of(k), start=True, stop=True).then_inc(s_r, 1)
                        if 2 <= k < n + 2:
                            u = u0 + k - 2
                            pe.wait_ge(pn_s, l * UNITS + (u + 1))
                            if u >= 2:
                                pe.wait_ge(pt_e, l * UNITS + (u - 1))
                            for kc in range(NT):
                                ins = pe.transpose(bank[2 + u % 2][:, kc * P:(kc + 1) * P],
                                                   prob[:, u % 2, kc * P:(kc + 1) * P], ident)
                            ins.then_inc(pt_r, 1)
                        if k >= 3:
                            u = u0 + k - 3
                            pe.wait_ge(pt_e, l * UNITS + (u + 1))
                            if u >= 2:
                                pe.wait_ge(o_e, l * UNITS + (u - 1))
                            for kc in range(NT):
                                ins = pe.matmul(bank[6 + u % 2][0:HD, 0:P], v_of(k - 3, kc), probT[:, u % 2, kc, :],
                                                start=kc == 0, stop=kc == NT - 1)
                            ins.then_inc(o_r, 1)
                        if k < n and (u0 + k) % 8 == 3 and u0 + k >= 8:
                            mod_sum((u0 + k) // 8 - 1)

                def gqa(k):
                    hd, t = GQA_UNITS[k]
                    return hd // 4, hd % 4, t
                attend(0, 32,
                       lambda k: qaT[gqa(k)[0] * HD:(gqa(k)[0] + 1) * HD, gqa(k)[1], gqa(k)[2] * P:(gqa(k)[2] + 1) * P],
                       lambda k: kaT[gqa(k)[0] * HD:(gqa(k)[0] + 1) * HD, :],
                       lambda k, kc: va[:, kc, gqa(k)[0] * HD:(gqa(k)[0] + 1) * HD])
                for hf in range(2):
                    pe.wait_ge(o_e, l * UNITS + (32 + 16 * hf))
                    for g in range(2 * NT):
                        t = g % NT
                        item = (8, 11)[hf]
                        lat, nk, n, w = (qlT, 3, 384, heads_q(item)) if g < NT else (kvlT, 2, 512, heads_kv(item))
                        if g == 0:
                            weights(item)
                        if g >= 2:
                            pe.wait_ge(nat_e, l * 16 + (hf * 8 + g - 1))
                        for c in range(nk):
                            ins = pe.matmul(bank[6 + g % 2][:, 0:n], lat[:, c, t * P:(t + 1) * P], w[:, c, :],
                                            start=c == 0, stop=c == nk - 1)
                        ins.then_inc(nat_r, 1)
                    pe.wait_ge(rope_s, l * 4 + (2 * hf + 1))
                    for h in range(4):
                        transposes(TR_MLA[hf] + h, [qn[:, t, h, :] for t in range(NT)], KD)
                    pe.wait_ge(rope_s, l * 4 + (2 * hf + 2))
                    for h in range(4):
                        transposes(TR_MLA[hf] + 4 + h, [kn[:, t, h, :] for t in range(NT)], KD)
                    pe.wait_ge(tr_e, l * TR + (TR_MLA[hf] + 8))
                    attend(32 + 16 * hf, 16,
                           lambda k: qbT[0:KD, k // NT, (k % NT) * P:(k % NT + 1) * P],
                           lambda k: kbT[0:KD, k // NT, :],
                           lambda k, kc: vb[:, kc, (k // NT) * HD:(k // NT + 1) * HD])
                mod_sum(7)
                pe.wait_ge(o_e, l * UNITS + UNITS)
                pe.wait_ge(tr_e, l * TR + TR_N2)
                for j in range(NC):
                    h = j // 4
                    b0 = 4 * (j % 2)
                    cols = slice((j % 4) * P, (j % 4 + 1) * P)
                    if j >= 2:
                        pe.wait_ge(m_s, l * NC + (j - 1))
                    for q, (item, src, nk, s) in enumerate((((14, 18)[h], hT, NC, ga_r), ((15, 19)[h], hT, NC, gb_r),
                                                           ((16, 20)[h], oT, 4, ya_r), ((17, 21)[h], oT, 4, yb_r))):
                        if j % 4 == 0:
                            weights(item)
                        w = slot(item % R, nk, 512)
                        for c in range(nk):
                            ins = pe.matmul(bank[b0 + q][:, :], w[:, c, cols], src[:, c + (4 if q == 3 else 0), :],
                                            start=c == 0, stop=c == nk - 1)
                        ins.then_inc(s, 1)
                pe.wait_ge(m_s, l * NC + NC)
                def logits(t):
                    pe.wait_ge(tr_e, l * TR + (TR_N2 + 2 * t + 2))
                    for c in range(NC):
                        ins = pe.matmul(bank[2][:, t * E:(t + 1) * E], hT[:, c, t * P:(t + 1) * P], wr[:, c, :],
                                        start=c == 0, stop=c == NC - 1)
                    return ins

                weights(22)
                weights(23)
                for k in range(8):
                    t, n = k // 2, k % 2
                    if k >= 4:
                        pe.wait_ge(x1, l * 8 + (k - 3))
                    w = slot((22 + n) % R, NC, 512)
                    for c in range(NC):
                        ins = pe.matmul(bank[4 + k % 4][:, :], mT[:, c, t * P:(t + 1) * P], w[:, c, :],
                                        start=c == 0, stop=c == NC - 1)
                    ins.then_inc(wo_r, 1)
                    if n == 1 and t >= 1:
                        norm_transposes(TR_N2, NT, t - 1)
                        if t >= 2:
                            logits(t - 2)
                logits(NT - 2)
                norm_transposes(TR_N2, NT, NT - 1)
                logits(NT - 1).then_inc(lg_r, 1)
                pe.wait_ge(oh_s, l + 1)
                for t in range(NT + 1):
                    last = min(t, NT - 1)
                    for j in range(last + 1):
                        ins = pe.matmul(bank[3][:, t * E:(t + 1) * E], utri if j == t else ones[:, :], r_a[:, j, :],
                                        start=j == 0, stop=j == last)
                ins.then_inc(rk_r, 1)

                def slot_table(done):
                    for q in range(2 * NT):
                        ins = pe.matmul(bank[3][:, P:P + 2 * E], slot_of[:, q, :], chosen[:, q // NT, q % NT, :],
                                        start=q == 0, stop=q == 2 * NT - 1)
                    ins.then_inc(done, 1)
                pe.wait_ge(ds_s, l + 1)
                slot_table(tp_r)

                def token_transposes(g, p0, b, first=False):
                    xv = xg[:, b, :].rearrange("p (q c) -> p c q", c=NC)
                    for k in range(2):
                        pe.wait_ge(tr_e, g + (k - 1))
                        for c in range(4):
                            ins = pe.transpose(bank[(p0 + k) % 2][:, c * P:(c + 1) * P], xv[:, 4 * k + c, :], ident)
                        ins.then_inc(tr_r, 1)

                def up(tokens, w1s, w3s, s1, s3):
                    for s, bk, done in ((w1s, 4, s1), (w3s, 5, s3)):
                        w = slot(s, NC, F)
                        for c in range(NC):
                            ins = pe.matmul(bank[bk][:, :], tokens[:, c, :], w[:, c, :], start=c == 0, stop=c == NC - 1)
                        ins.then_inc(done, 1)

                def down(s, done):
                    w = slot(s, 4, D)
                    for n in range(2):
                        for c in range(4):
                            ins = pe.matmul(bank[6 + n][:, :], uT[:, c, :], w[:, c, n * 512:(n + 1) * 512],
                                            start=c == 0, stop=c == 3)
                        ins.then_inc(done, 1)

                def hidden_transposes(b):
                    for c in range(4):
                        ins = pe.transpose(bank[b][:, c * P:(c + 1) * P], u_s[:, c * P:(c + 1) * P], ident)
                    return ins

                def loaded(s, n):
                    pe.wait_ge(w_rdy[s], l * (16 * slot_total(s)) + n * 16)

                def nth(k):
                    return PRE[k % R] + slot_loads(k)

                def expert(e, p, g, slots, loads, gat, first=False, last=False):
                    loaded(slots[0], loads[0])
                    pe.wait_ge(tr_e, g if first else g - 1)
                    for s, n, bk, done in ((slots[0], loads[0], 4, h1_r), (slots[1], loads[1], 5, h3_r)):
                        loaded(s, n)
                        wv = slot(s, NC, F)
                        for c in range(NC):
                            ins = pe.matmul(bank[bk][:, :], xsT[:, p, c, :], wv[:, c, :], start=c == 0, stop=c == NC - 1)
                        ins.then_inc(done, 1)
                    if not last:
                        pe.wait_ge(xg_s[1 - p], l * 128 + gat)
                        token_transposes(g, p, 1 - p)
                    if not first:
                        loaded(slots[2], loads[2])
                        pe.wait_ge(tr_e, g)
                        if not (isinstance(e, int) and e == 1):
                            pe.wait_ge(y_e, (l * E + e - 1) * 2)
                        down(slots[2], y_r)
                    pe.wait_ge(u_s_s, l * E + e + 1)
                    gu = g if last else g + 2
                    pe.wait_ge(tr_e, gu - 1)
                    hidden_transposes(1 if last else p).then_inc(tr_r, 1)

                pe.wait_ge(xg_s[0], l * 128 + 16)
                token_transposes(l * TR + TR_X0, 0, 0)
                expert(0, 0, l * TR + (TR_X0 + 2), (0, 1), (nth(MIX_ITEMS), nth(MIX_ITEMS + 1)), 16, first=True)

                def items(e):
                    return [MIX_ITEMS + 2 + 3 * (e - 1) + q for q in range(3)]
                for e in (1, 2):
                    it = items(e)
                    expert(e, e % 2, l * TR + (TR_X0 + 2 + 3 * e), [k % R for k in it], [nth(k) for k in it],
                           16 * ((e + 1) // 2 + 1))
                with pe.Fori(0, 6) as i:
                    for r in range(2):
                        it = items(3 + r)
                        expert(2 * i + (3 + r), (3 + r) % 2, l * TR + (TR_X0 + 2 + 9 + 3 * r) + i * 6,
                               [k % R for k in it], [i + nth(k) for k in it],
                               i * 16 + 16 * ((4 + r) // 2 + 1))
                it = items(15)
                expert(15, 1, l * TR + (TR_X0 + 2 + 45), [k % R for k in it], [nth(k) for k in it], 0, last=True)
                loaded((ITEMS - 1) % R, nth(ITEMS - 1))
                pe.wait_ge(tr_e, l * TR + TR)
                pe.wait_ge(y_e, (l * E + 15) * 2)
                down((ITEMS - 1) % R, y_r)

                def body(e, n):
                    pe.wait_ge(ov_w, n * 48 + 48)
                    pe.wait_ge(ov_x, n * 16 + 16)
                    xv = xg[:, 0, :].rearrange("p (q c) -> p c q", c=NC)
                    for k in range(2):
                        for c in range(4):
                            ins = pe.transpose(bank[k][:, c * P:(c + 1) * P], xv[:, 4 * k + c, :], ident)
                        ins.then_inc(ov_t, 1)
                    pe.wait_ge(ov_te, n * 3 + 2)
                    up(xsT[:, 0, :, :], 0, 1, ov_h, ov_h)
                    pe.wait_ge(ov_u, n + 1)
                    hidden_transposes(0).then_inc(ov_t, 1)
                    pe.wait_ge(ov_te, n * 3 + 3)
                    down(2, ov_y)
                pe.wait_ge(y_e, l * 2 * E + 2 * E)
                wait(pe, ds_s, l + 1)

                def new_table(n, m):
                    pe.wait_ge(ov_sl, m + 1)
                    slot_table(ov_tp)
                extra_blocks(pe, n_ov, n_tab, body, new_table)


def kernel(**inputs):
    import concourse.bacc as bacc
    from concourse.bass_utils import run_bass_kernel_spmd

    names = ["x", "c", "w_ada", "b_ada", "norm1", "w_in", "q_norm_a", "k_norm_a", "q_a_norm", "kv_norm",
             "w_q_b", "w_kv_b", "w_proj_a", "w_proj_b", "w_o", "norm2", "w_router", "router_bias",
             "w1", "w3", "w2", "norm_f"]
    nc = bacc.Bacc("TRN2", target_bir_lowering=False, num_devices=1)
    arrays = {f"in_{n}": np.ascontiguousarray(inputs[n]) for n in names}
    arrays["in_constants"] = constants()
    args = [nc.dram_tensor(n, a.shape, mybir.dt.from_np(a.dtype), kind="ExternalInput").ap() for n, a in arrays.items()]
    out = nc.dram_tensor("out_0", (1, SEQ, D), mybir.dt.float32, kind="ExternalOutput").ap()
    trunk(nc, *args, out)
    r = run_bass_kernel_spmd(nc, [arrays], core_ids=[0])
    return r.results[0]["out_0"]
```

```python
from contextlib import ExitStack

import numpy as np
import concourse.bass as bass
from concourse import mybir

P = 128
D = 1024
SEQ = 512
NT = SEQ // P
NC = D // P
DEPTH = 2
NMOD = 6
GRID_W = 64
THETA = 10000.0
EPS = 1e-6
HD = 64
RD = 32
KD = HD + RD
QL, KVL = 384, 256
QK_HEADS = 10
ZC = 1440
Z_ITEMS = ((0, 512), (512, 256), (768, 384), (1152, 288))
Z_V, Z_QL, Z_KVL, Z_KR = 640, 768, 1152, 1408
E = 16
EG = 4
F = 512
BIG = 3.0e38
R = 6
NONE = 2 * SEQ
MIX_ITEMS = 24
ITEMS = MIX_ITEMS + 3 * E
LOADS = [2 if k in (8, 11) else 1 for k in range(ITEMS)]
ADA_ITEM = (4, 5, 6, 7, 9, 10, 12, 13)
ADA_PRE = 4
FIRST_PARTS = ((0, 2), (2, 4), (4, NC))
NX = 2 * D // P
ADA_IN = 8
TR = 98
UNITS = 64
TR_N1, TR_QK, TR_LAT, TR_N2, TR_X0 = 0, 8, 13, 42, 50
TR_MLA = (21, 31)
TR_ADA = (18, 19, 20, 29, 30, 39, 40, 41)
C_ID, C_UT, C_CA, C_SA, C_CB, C_SB, C_GW, C_EW, C_TK, C_RW, C_IO = 0, 128, 256, 384, 512, 576, 640, 644, 660, 664, 672
C_N = 800
GQA_UNITS = [(4 * s + j, t) for j in range(4) for s in range(2) for t in range(NT)]


def slot_loads(k):
    return sum(LOADS[j] for j in range(k % R, k + 1, R))


PRE = [1 if s < ADA_PRE else 0 for s in range(R)]


def slot_total(s):
    return sum(LOADS[s::R])


def constants():
    c = np.zeros((P, C_N), np.float32)
    c[:, C_ID:C_ID + P] = np.eye(P, dtype=np.float32)
    c[:, C_UT:C_UT + P] = np.triu(np.ones((P, P), np.float32), 1)
    pos = np.arange(SEQ)
    row, col = (pos // GRID_W).astype(np.float32), (pos % GRID_W).astype(np.float32)
    for width, cc, cs in ((HD, C_CA, C_SA), (RD, C_CB, C_SB)):
        n = width // 4
        inv = (np.float32(1.0) / np.power(np.float32(THETA), np.arange(n, dtype=np.float32) / np.float32(n))).astype(np.float32)
        ang = np.concatenate([row[:, None] * inv, col[:, None] * inv], axis=-1).astype(np.float32)
        for at, f in ((cc, np.cos), (cs, np.sin)):
            t = f(ang.astype(np.float64)).astype(np.float32).reshape(NT, P, width // 2)
            c[:, at:at + NT * width // 2] = t.transpose(1, 0, 2).reshape(P, -1)
    c[:, C_GW:C_GW + EG] = EG - np.arange(EG)
    c[:, C_EW:C_EW + E] = E - np.arange(E)
    token = np.arange(NT)[None, :] * P + np.arange(P)[:, None]
    c[:, C_TK:C_TK + NT] = token
    for k in range(2):
        c[:, C_RW + k * NT:C_RW + (k + 1) * NT] = 2 * token + k - NONE
    c[:, C_IO:C_IO + P] = np.arange(P)
    return c


def trunk(nc, x_in, c_in, w_ada, b_ada, norm1, w_in, q_norm_a, k_norm_a, q_a_norm, kv_norm, w_q_b,
          w_kv_b, w_proj_a, w_proj_b, w_o, norm2, w_router, router_bias, w1, w3, w2, norm_f, consts, out):
    f32, i32 = mybir.dt.float32, mybir.dt.int32
    ALU = mybir.AluOpType
    ACT = mybir.ActivationFunctionType
    X = mybir.AxisListType.X

    b_ada_v = b_ada.rearrange("l (q o n) -> l q o n", n=512, o=1)
    mod_d = nc.dram_tensor("mod_d", [DEPTH, NMOD * D], f32, kind="Internal").ap()
    xn_d = nc.dram_tensor("xn_d", [SEQ, D], f32, kind="Internal").ap()
    ys_d = nc.dram_tensor("ys_d", [SEQ * 2, D], f32, kind="Internal").ap()

    nx_v = w_ada.rearrange("l (p c) (q n) -> l q p c n", c=NC, n=P)
    mod_v = mod_d.rearrange("l (q o n) -> l q o n", n=512, o=1)

    ada_v = w_ada.rearrange("l (p c) (q n) -> l q p c n", c=NC, n=512)
    in_v = w_in.rearrange("l (p c) n -> l p c n", c=NC)
    qb_v = w_q_b.rearrange("l (c p) n -> l p c n", p=P)
    kvb_v = w_kv_b.rearrange("l (c p) n -> l p c n", p=P)
    pa_v = w_proj_a.rearrange("l (c p) n -> l p c n", p=P)
    pb_v = w_proj_b.rearrange("l (c p) n -> l p c n", p=P)
    wo_v = w_o.rearrange("l (c p) n -> l p c n", p=P)
    w1_v = w1.rearrange("l e (p c) f -> (l e) p c f", c=NC)
    w3_v = w3.rearrange("l e (p c) f -> (l e) p c f", c=NC)
    w2_v = w2.rearrange("l e (c p) n -> (l e) p c n", p=P)

    with ExitStack() as ctx:
        def sb(name, shape, dt=f32):
            return ctx.enter_context(nc.sbuf_tensor(name, shape, dt))

        def sem(name):
            return ctx.enter_context(nc.semaphore(name))

        ring = sb("ring", [P, R, 4096])
        x = sb("x", [P, NT, D])
        hT = sb("hT", [P, NC, SEQ])
        reg_a = sb("reg_a", [P, 4096])
        reg_b = sb("reg_b", [P, 5760])
        reg_c = sb("reg_c", [P, 3072])
        reg_d = sb("reg_d", [P, 2560])
        vb = sb("vb", [P, NT, 4 * HD])
        reg_f = sb("reg_f", [P, 2048])
        cst = sb("cst", [P, C_N])
        ones = sb("ones", [P, P])
        gain_qk = sb("gain_qk", [P, 2, HD])
        gain_l = sb("gain_l", [P, 5])
        gain_n = sb("gain_n", [P, 2 * DEPTH, NC])
        mod_c = sb("mod_c", [P, 2, NC])
        bias_c = sb("bias_c", [P, 2, NC])
        wr = sb("wr", [P, NC, E])
        rbias = sb("rbias", [P, E])
        kr = sb("kr", [P, NT, RD])
        ssq = sb("ssq", [P, NT])
        warm = sb("warm", [P, 1])
        rstd = sb("rstd", [P, NT])
        stz = sb("stz", [P, NT, 12])
        nmax = sb("nmax", [P, 4])
        lsum = sb("lsum", [P, 4])
        linv = sb("linv", [P, 4])
        cur = sb("cur", [P, 4, NC])
        gain1, gain2 = sb("gain1", [P, NC]), sb("gain2", [P, NC])
        flag_i = sb("flag_i", [1, 1], i32)
        cond = sb("cond", [P, 2, NC])
        gw = sb("gw", [P, 2, NT])
        table = sb("table", [P, 2 * E], i32)
        cnt_i = sb("cnt_i", [P, E], i32)
        idx = sb("idx", [P, 2], i32)
        idy = sb("idy", [P, 2], i32)

        ident = cst[:, C_ID:C_ID + P]
        utri = cst[:, C_UT:C_UT + P]
        cos_a = cst[:, C_CA:C_CA + 128].rearrange("p (t n) -> p t n", t=NT)
        sin_a = cst[:, C_SA:C_SA + 128].rearrange("p (t n) -> p t n", t=NT)
        cos_b = cst[:, C_CB:C_CB + 64].rearrange("p (t n) -> p t n", t=NT)
        sin_b = cst[:, C_SB:C_SB + 64].rearrange("p (t n) -> p t n", t=NT)
        xn = reg_a[:, :].rearrange("p (t n) -> p t n", t=NT)
        oT = reg_a[:, :].rearrange("p (c n) -> p c n", c=8)
        cy = [r.rearrange("p (b k n) -> p b k n", b=2, k=2)[:, b] for r in (reg_a[:, :], reg_b[:, 0:4096]) for b in range(2)]
        z = reg_b[:, :].rearrange("p (t n) -> p t n", t=NT)
        qbT = reg_b[:, 0:2048].rearrange("p (h n) -> p h n", h=4)
        kbT = reg_b[:, 2048:4096].rearrange("p (h n) -> p h n", h=4)
        mT = reg_b[:, 0:4096].rearrange("p (c n) -> p c n", c=NC)
        xg = reg_b[:, 0:2048].rearrange("p (b n) -> p b n", b=2)
        xsT = reg_b[:, 2048:4096].rearrange("p (b c n) -> p b c n", b=2, c=NC)
        u_s = reg_b[:, 4096:4608]
        sg_e = reg_b[:, 4608:5120]
        uT = reg_b[:, 5120:5632].rearrange("p (c n) -> p c n", c=4)
        acc = reg_b[:, 4096:5120].rearrange("p (b n) -> p b n", b=2)
        mod_row = reg_b[0:1, 5120:5632]
        mod_bias = reg_b[32:33, 5120:5632]
        qaT = reg_c[:, 0:2048].rearrange("p (j n) -> p j n", j=4)
        kaT = reg_c[:, 2048:2560]
        va = reg_c[:, 2560:3072].rearrange("p (t n) -> p t n", t=NT)
        qn = reg_c[:, 0:1536].rearrange("p (t h n) -> p t h n", t=NT, h=4)
        kn = reg_c[:, 1536:3072].rearrange("p (t h n) -> p t h n", t=NT, h=4)
        g1_row, g2_row, nf_row = (reg_c[:, k * D:(k + 1) * D] for k in range(3))
        qlT = reg_d[:, 0:1536].rearrange("p (c n) -> p c n", c=3)
        kvlT = reg_d[:, 1536:2560].rearrange("p (c n) -> p c n", c=2)
        ysb = reg_d[:, 0:2048].rearrange("p (b n) -> p b n", b=2)
        prob = reg_f[:, 0:1024].rearrange("p (b n) -> p b n", b=2)
        probT = reg_f[:, 1024:2048].rearrange("p (b k n) -> p b k n", b=2, k=NT)
        zsq = reg_f[:, 0:1280].rearrange("p (b n) -> p b n", b=2)
        rot = reg_f[:, 1280:1920].rearrange("p (b n) -> p b n", b=2)
        rot_b = reg_f[:, 0:512].rearrange("p (b n) -> p b n", b=2)
        sg_m = reg_f[:, :].rearrange("p (b g n) -> p b g n", b=2, g=2)
        nx_w = vb[:, :, :].rearrange("p t n -> p (t n)").rearrange("p (c n) -> p c n", c=NC)
        nx_acc = reg_d[:, 0:2048]
        wo_t = reg_f[:, 0:1024].rearrange("p (b n) -> p b n", b=2)
        sq_j = reg_f[:, 1024:2048]

        def rt(k):
            return reg_f[:, k * 64:(k + 1) * 64].rearrange("p (t e) -> p t e", t=NT)
        score, biased, oh1, oh2, r_a, r_b = (rt(k) for k in range(6))
        r_s = reg_f[:, 448:640]
        upto = r_s[:, 64:128].rearrange("p (t e) -> p t e", t=NT)
        rank_k = reg_f[:, 736:744].rearrange("p (k t) -> p k t", k=2)
        chosen = reg_f[:, 768:1024].rearrange("p (k t n) -> p k t n", k=2, t=NT)
        slot_of = reg_f[:, 1024:2048].rearrange("p (q n) -> p q n", n=P)

        def scale1(c):
            return cur[:, 1, c:c + 1]

        def shift1(c):
            return cur[:, 0, c:c + 1]

        def scale2(c):
            return cur[:, 3, c:c + 1]

        def shift2(c):
            return cur[:, 2, c:c + 1]

        def slot(s, a, n):
            return ring[:, s, 0:a * n].rearrange("p (a n) -> p a n", a=a)

        def heads_q(k):
            return ring[:, k % R, 0:3 * 384].rearrange("p (a n) -> p a n", a=3)

        def heads_kv(k):
            return ring[:, k % R, 3 * 384:3 * 384 + 2 * 512].rearrange("p (a n) -> p a n", a=2)

        bank = [ctx.enter_context(nc.psum_tensor(f"bank{k}", [P, 512], f32)) for k in range(8)]

        def wo_bank(k):
            return bank[3 if k == 0 else 4 + k % 4]

        c_in_s = sem("consts_loaded")
        x_in_s = sem("x_loaded")
        cond_in = sem("cond_loaded")
        cond_s = sem("cond_ready")
        ones_s = sem("ones_ready")
        cond_e = sem("cond_sigmoid")
        b_in = sem("ada_bias_loaded")
        first_s = [sem(f"first_piece_part{k}_loaded") for k in range(len(FIRST_PARTS) - 1)]
        ada_ps = sem("ada_psum_ready")
        ada_ev = sem("ada_psum_read")
        aa_s = sem("mod_chunks_summed")
        mb_s = sem("mod_bias_loaded")
        nb_s = sem("next_bias_loaded")
        nl_s = sem("next_piece_loaded")
        nu_s = sem("next_piece_summed_over_chunks")
        nm_r = sem("next_mod_psum_ready")
        cur2_ld = sem("shift2_scale2_loaded")
        cur2_s = sem("scale2_ready")
        mod_st = sem("mod_stored")
        col_r = sem("mod_columns_ready")
        cur_s = sem("layer_mod_ready")
        w_rdy = [sem(f"slot{k}_loaded") for k in range(R)]
        x2 = sem("x_after_moe")
        x1 = sem("x_after_mixer")
        sq_s = sem("square_sums")
        wm_s = sem("root_table_loaded")
        ms_s = sem("mean_squares")
        rt_s = sem("roots")
        xn_s = sem("normed")
        tr_r = sem("transposes_ready")
        tr_e = sem("transposes_read")
        z_r = sem("z_psum_ready")
        z_e = sem("z_psum_read")
        zsq_s = sem("z_squares")
        zl_s = sem("latent_square_sums")
        zst_s = sem("z_square_sums_reduced")
        zms_s = sem("z_mean_squares")
        zrt_s = sem("z_roots")
        qk_s = sem("heads_rotated")
        lat_s = sem("latents_normed_then_rotated_key")
        gl_s = sem("layer_gains_loaded")
        s_r = sem("scores_ready")
        mx_s = sem("row_max")
        ex_s = sem("exp_done")
        pn_s = sem("probs_normed")
        pt_r = sem("probsT_ready")
        pt_e = sem("probsT_read")
        o_r = sem("head_out_ready")
        o_e = sem("head_out_read")
        nat_r = sem("mla_psum_ready")
        nat_e = sem("mla_psum_read")
        rope_s = sem("mla_rotated")
        ga_r, gb_r, ya_r, yb_r = (sem(n) for n in ("gate_a_ready", "gate_b_ready", "proj_a_ready", "proj_b_ready"))
        sig_s = sem("gates_sigmoid")
        m_s = sem("merged")
        wo_r = sem("mixer_out_ready")
        row_ld = sem("gate_rows_loaded")
        xn_st = sem("normed_stored")
        lg_r = sem("logits_ready")
        sc_s = sem("router_scores")
        oh_s = sem("one_hots")
        rk_r = sem("ranks_ready")
        ds_s = sem("counts_and_slots")
        tp_r = sem("slot_table_psum_ready")
        tb_s = sem("slot_table_ready")
        ix_s = sem("gather_index_ready")
        iy_s = sem("scatter_index_ready")
        xg_s = [sem(f"tokens_gathered{k}") for k in range(2)]
        h1_r, h3_r = sem("h1_ready"), sem("h3_ready")
        sge_s = sem("h1_sigmoid")
        u_s_s = sem("expert_hidden")
        y_r, y_e = sem("expert_out_ready"), sem("expert_out_read")
        ys_st = [sem(f"expert_out_stored{k}") for k in range(2)]
        cg_s = [sem(f"token_outputs_loaded{t}") for t in range(NT)]
        ov_free = sem("extra_block_done")
        ov_w = sem("extra_weights_loaded")
        ov_sl = sem("extra_slots_of_tokens")
        ov_tp = sem("extra_table_psum_ready")
        ov_tb = sem("extra_table_ready")
        ov_i = sem("extra_indices_ready")
        ov_x = sem("extra_tokens_gathered")
        ov_t = sem("extra_transposed")
        ov_te = sem("extra_transposes_read")
        ov_h = sem("extra_h_ready")
        ov_g = sem("extra_sigmoid")
        ov_u = sem("extra_hidden")
        ov_y = sem("extra_out_ready")
        ov_ye = sem("extra_out_read")
        ov_st = sem("extra_out_stored")
        ov_all = sem("extra_pass_done")
        out_s = sem("out_ready")
        out_st = sem("out_stored")

        ticks = sem("ticks")

        block = ctx.enter_context(nc.Block())

        def wait(eng, s, value):
            eng.wait_ge(s, value)
            eng.sem_inc(ticks, 1)

        def after(l):
            return nc.s_assert_within(l + 1, 1, DEPTH - 1, skip_runtime_bounds_check_because="inside If(l < DEPTH - 1)")

        def extra_blocks(eng, blocks, tables, body, new_table=None):
            most = eng.value_load(flag_i[0:1, 0:1], min_val=0, max_val=SEQ)
            with eng.If(most > P):
                with eng.Fori(1, eng.snap((most + (P - 1)) >> 7)) as b:
                    if new_table is not None:
                        new_table(eng.snap(blocks), eng.snap(tables))
                    eng.reg_add(tables, tables, 1)
                    with eng.Fori(0, E) as e:
                        n = eng.value_load(cnt_i[0:1, bass.ds(e, 1)], min_val=0, max_val=SEQ)
                        with eng.If(n > b * P):
                            body(e, eng.snap(blocks))
                            eng.reg_add(blocks, blocks, 1)

        @block.sync
        def _(sp):
            sp.dma_start(cond[:, 0, :], c_in[0].rearrange("(p c) -> p c", c=NC)).then_inc(cond_in, 16)

            for (a, b), s in zip(FIRST_PARTS, first_s + [w_rdy[0]]):
                sp.dma_start(slot(0, NC, 512)[:, a:b, :], ada_v[0, 0][:, a:b, :]).then_inc(s, 16)
            for r in range(1, ADA_PRE):
                sp.dma_start(slot(r, NC, 512), ada_v[0, r]).then_inc(w_rdy[r], 16)
            for t in range(NT):
                sp.dma_start(x[:, t, :], x_in[0, t * P:(t + 1) * P, :]).then_inc(x_in_s, 16)

            n_ov, n_tab = sp.alloc_register("extra_blocks_sp"), sp.alloc_register("extra_tables_sp")
            sp.reg_mov(n_ov, 0)
            sp.reg_mov(n_tab, 0)

            def load(k, dst_shape, src):
                a, n = dst_shape
                sp.dma_start(slot(k % R, a, n), src).then_inc(w_rdy[k % R], 16)

            def load_z(layer, i):
                at, n = Z_ITEMS[i]
                load(i, (NC, n), in_v[layer, :, :, at:at + n])
            for i in range(3):
                wait(sp, ada_ps, i + 1)
                load_z(0, i)
            wait(sp, ada_ps, ADA_PRE)
            with sp.Fori(0, DEPTH) as l:

                def load_ada(i):
                    load(ADA_ITEM[i], (NC, 512), ada_v[l, ADA_PRE + i])

                def load_heads(k, hf):
                    sp.dma_start(heads_q(k), qb_v[l, :, :, hf * 384:(hf + 1) * 384]).then_inc(w_rdy[k % R], 16)
                    sp.dma_start(heads_kv(k), kvb_v[l, :, :, hf * 512:(hf + 1) * 512]).then_inc(w_rdy[k % R], 16)

                load_z(l, 3)
                load_ada(0)
                load_ada(1)
                wait(sp, z_r, l * 16 + 4)
                load_ada(2)
                wait(sp, z_r, l * 16 + 8)
                load_ada(3)
                wait(sp, z_r, l * 16 + 12)
                load_heads(8, 0)
                wait(sp, z_r, l * 16 + 16)
                load_ada(4)
                wait(sp, aa_s, l * ADA_IN + 1)
                load_ada(5)
                wait(sp, aa_s, l * ADA_IN + 2)
                load_heads(11, 1)
                wait(sp, aa_s, l * ADA_IN + 3)
                load_ada(6)
                wait(sp, aa_s, l * ADA_IN + 4)
                load_ada(7)
                wait(sp, nat_r, l * 16 + 8)
                load(14, (NC, 512), in_v[l, :, :, ZC:ZC + 512])
                wait(sp, aa_s, l * ADA_IN + 5)
                load(15, (NC, 512), in_v[l, :, :, ZC + D:ZC + D + 512])
                wait(sp, aa_s, l * ADA_IN + 6)
                load(16, (4, 512), pa_v[l, :, :, 0:512])
                wait(sp, nat_r, l * 16 + 16)
                load(17, (4, 512), pb_v[l, :, :, 0:512])
                wait(sp, aa_s, l * ADA_IN + 7)
                load(18, (NC, 512), in_v[l, :, :, ZC + 512:ZC + D])
                wait(sp, aa_s, l * ADA_IN + 8)
                load(19, (NC, 512), in_v[l, :, :, ZC + D + 512:ZC + 2 * D])
                wait(sp, ga_r, l * 8 + 4)
                load(20, (4, 512), pa_v[l, :, :, 512:D])
                wait(sp, gb_r, l * 8 + 4)
                load(21, (4, 512), pb_v[l, :, :, 512:D])
                for n, s in ((0, ya_r), (1, yb_r)):
                    wait(sp, s, l * 8 + 4)
                    load(22 + n, (NC, 512), wo_v[l, :, :, n * 512:(n + 1) * 512])
                wait(sp, ga_r, l * 8 + 8)
                load(24, (NC, F), w1_v[l * E])
                wait(sp, gb_r, l * 8 + 8)
                load(25, (NC, F), w3_v[l * E])
                wait(sp, ya_r, l * 8 + 8)
                load(26, (NC, F), w1_v[l * E + 1])
                wait(sp, yb_r, l * 8 + 8)
                load(27, (NC, F), w3_v[l * E + 1])
                wait(sp, wo_r, l * 8 + 8)
                load(28, (4, D), w2_v[l * E])
                load(29, (NC, F), w1_v[l * E + 2])
                wait(sp, h1_r, l * E + 1)
                load(30, (NC, F), w3_v[l * E + 2])
                wait(sp, h3_r, l * E + 1)
                load(31, (4, D), w2_v[l * E + 1])
                with sp.Fori(0, 6) as i:
                    e0 = l * E + 2 * i
                    for r in range(2):
                        k = 32 + 3 * r
                        wait(sp, h1_r, e0 + (r + 2))
                        load(k, (NC, F), w1_v[e0 + (r + 3)])
                        wait(sp, h3_r, e0 + (r + 2))
                        load(k + 1, (NC, F), w3_v[e0 + (r + 3)])
                        wait(sp, y_r, (e0 + (r + 1)) * 2)
                        load(k + 2, (4, D), w2_v[e0 + (r + 2)])
                wait(sp, h1_r, l * E + 14)
                load(68, (NC, F), w1_v[l * E + 15])
                wait(sp, h3_r, l * E + 14)
                load(69, (NC, F), w3_v[l * E + 15])
                wait(sp, y_r, l * 2 * E + 26)
                load(70, (4, D), w2_v[l * E + 14])
                wait(sp, h1_r, l * E + 15)
                load(71, (4, D), w2_v[l * E + 15])
                wait(sp, h3_r, l * E + 15)
                wait(sp, y_r, l * 2 * E + 28)
                wait(sp, h1_r, l * E + 16)
                with sp.If(l < DEPTH - 1):
                    for i in range(3):
                        load_z(after(l), i)
                wait(sp, y_r, l * 2 * E + 2 * E)

                def body(e, n):
                    wait(sp, ov_free, n + 1)
                    sp.dma_start(slot(3, NC, F), w1_v[l * E + e]).then_inc(ov_w, 16)
                    sp.dma_start(slot(4, NC, F), w3_v[l * E + e]).then_inc(ov_w, 16)
                    sp.dma_start(slot(5, 4, D), w2_v[l * E + e]).then_inc(ov_w, 16)
                wait(sp, ds_s, l + 1)
                extra_blocks(sp, n_ov, n_tab, body)
                for b in range(2):
                    wait(sp, ys_st[b], l * 128 + 128)
                wait(sp, ov_all, l + 1)
                for t in range(NT):
                    sp.dma_start(cy[t].rearrange("p k n -> p (k n)"), ys_d.rearrange("(t p k) n -> t p (k n)", p=P, k=2)[t]).then_inc(cg_s[t], 16)
            for t in range(NT):
                wait(sp, out_s, t + 1)
                sp.dma_start(out[0, t * P:(t + 1) * P, :], xn[:, t, :]).then_inc(out_st, 16)
            wait(sp, out_st, 16 * NT)

        @block.gpsimd
        def _(pool):
            pool.dma_start(cst[:, :], consts).then_inc(c_in_s, 16)
            pool.memset(ones[:, :], 1.0).then_inc(ones_s, 1)
            pool.dma_start(wr[:, :, :], w_router.rearrange("(p c) e -> p c e", c=NC)).then_inc(c_in_s, 16)
            pool.dma_start(rbias[:, :], router_bias.partition_broadcast(P)).then_inc(c_in_s, 16)
            for w, g in ((0, norm1), (1, norm2)):
                pool.dma_start(gain_n[:, w * DEPTH:(w + 1) * DEPTH, :], g.rearrange("l (p c) -> p l c", c=NC)).then_inc(c_in_s, 16)
            wait(pool, ones_s, 1)
            wait(pool, c_in_s, 16 * 5)

            n_ov, n_tab = pool.alloc_register("extra_blocks_pool"), pool.alloc_register("extra_tables_pool")
            pool.reg_mov(n_ov, 0)
            pool.reg_mov(n_tab, 0)
            with pool.Fori(0, DEPTH) as l:
                wait(pool, x2, l * NT + NT)
                pool.dma_start(gain_qk[:, 0, :], q_norm_a[l].partition_broadcast(P)).then_inc(gl_s, 16)
                pool.dma_start(gain_qk[:, 1, :], k_norm_a[l].partition_broadcast(P)).then_inc(gl_s, 16)
                pool.dma_start(gain_l[:, 0:3], q_a_norm[l].rearrange("(c p) -> p c", p=P), allow_slow_non_contiguous=True).then_inc(gl_s, 16)
                pool.dma_start(gain_l[:, 3:5], kv_norm[l].rearrange("(c p) -> p c", p=P), allow_slow_non_contiguous=True).then_inc(gl_s, 16)
                with pool.If(l < DEPTH - 1):
                    pool.dma_start(bias_c[:, :, :], b_ada[after(l), 0:2 * D].rearrange("(m p c) -> p m c", m=2, c=NC)).then_inc(nb_s, 16)
                for i in range(ADA_IN):
                    wait(pool, tr_r, l * TR + ((TR_ADA[i - 1] + 1) if i else TR_LAT + 5))
                    pool.dma_start(mod_bias, b_ada_v[l, ADA_PRE + i]).then_inc(mb_s, 16)
                    if i == ADA_IN - 1:
                        wait(pool, mod_st, (l * ADA_IN + 6) * 16)
                        pool.dma_start(cur[:, 2:4, :], mod_d[l, 3 * D:5 * D].rearrange("(m p c) -> p m c", m=2, c=NC)).then_inc(cur2_ld, 16)
                wait(pool, mod_st, (l * ADA_IN + ADA_IN) * 16)
                wait(pool, o_e, l * UNITS + UNITS)
                pool.dma_start(g1_row, mod_d[l, 2 * D:3 * D].partition_broadcast(P)).then_inc(row_ld, 16)
                pool.dma_start(g2_row, mod_d[l, 5 * D:6 * D].partition_broadcast(P)).then_inc(row_ld, 16)
                pool.dma_start(nf_row, norm_f.partition_broadcast(P)).then_inc(row_ld, 16)
                for t in range(NT):
                    wait(pool, xn_s, l * 2 * NT + NT + t + 1)
                    pool.dma_start(xn_d[t * P:(t + 1) * P, :], xn[:, t, :]).then_inc(xn_st, 16)
                wait(pool, xn_st, l * 64 + 64)

                def gather(e, b, n_wait):
                    if n_wait is not None:
                        wait(pool, tr_r, n_wait)
                    if isinstance(e, int):
                        tokens = table[:, e:e + 1]
                    else:
                        tokens = idx[:, b:b + 1]
                        pool.tensor_copy(tokens, table[:, bass.ds(e, 1)]).then_inc(ix_s, 1)
                        wait(pool, ix_s, l * 12 + (e - 2))
                    pool.indirect_dma_start(xg[:, b, :], None, xn_d, bass.IndirectOffsetOnAxis(tokens, 0),
                                            bounds_check=SEQ - 1, oob_is_err=False).then_inc(xg_s[b], 16)

                def scatter(e, b):
                    wait(pool, y_e, (l * E + e) * 2 + 2)
                    if isinstance(e, int):
                        rows = table[:, E + e:E + e + 1]
                    else:
                        rows = idy[:, b:b + 1]
                        pool.tensor_copy(rows, table[:, bass.ds(e + E, 1)]).then_inc(iy_s, 1)
                        wait(pool, iy_s, l * 12 + (e + 1))
                    pool.indirect_dma_start(ys_d, bass.IndirectOffsetOnAxis(rows, 0), ysb[:, b, :], None,
                                            bounds_check=2 * SEQ - 1, oob_is_err=False).then_inc(ys_st[b], 16)

                wait(pool, tb_s, l + 1)
                wait(pool, x1, l * 8 + 8)
                gather(0, 0, None)
                gather(1, 1, None)
                gather(2, 0, l * TR + (TR_X0 + 2))
                with pool.Fori(0, 6) as i:
                    for r in range(2):
                        f = 2 * i + r
                        gather(f + 3, (3 + r) % 2, l * TR + (TR_X0 + 4) + f * 3)
                        scatter(f, r)
                gather(15, 1, l * TR + (TR_X0 + 4 + 12 * 3))
                for f in range(12, E):
                    scatter(f, f % 2)

                def body(e, n):
                    wait(pool, ov_free, n + 1)
                    pool.tensor_copy(idx[:, 0:1], table[:, bass.ds(e, 1)]).then_inc(ov_i, 1)
                    pool.tensor_copy(idy[:, 0:1], table[:, bass.ds(e + E, 1)]).then_inc(ov_i, 1)
                    wait(pool, ov_i, n * 2 + 2)
                    pool.indirect_dma_start(xg[:, 0, :], None, xn_d, bass.IndirectOffsetOnAxis(idx[:, 0:1], 0),
                                            bounds_check=SEQ - 1, oob_is_err=False).then_inc(ov_x, 16)
                    wait(pool, ov_ye, n * 2 + 2)
                    pool.indirect_dma_start(ys_d, bass.IndirectOffsetOnAxis(idy[:, 0:1], 0), ysb[:, 0, :], None,
                                            bounds_check=2 * SEQ - 1, oob_is_err=False).then_inc(ov_st, 16)
                    wait(pool, ov_st, n * 16 + 16)
                    pool.sem_inc(ov_free, 1)

                def new_table(n, m):
                    for b in range(2):
                        wait(pool, ys_st[b], l * 128 + 128)
                    wait(pool, ov_tb, m + 1)
                extra_blocks(pool, n_ov, n_tab, body, new_table)
                pool.sem_inc(ov_all, 1)

        @block.scalar
        def _(act):
            A = act.activation
            act.wait_ge(cond_in, 16)
            A(cond[:, 1, :], cond[:, 0, :], ACT.Sigmoid).then_inc(cond_e, 1)
            for r in range(ADA_PRE):
                act.dma_start(reg_b[0:1, 512 * r:512 * (r + 1)], b_ada_v[0, r]).then_inc(b_in, 16)

            n_ov, n_tab = act.alloc_register("extra_blocks_act"), act.alloc_register("extra_tables_act")
            act.reg_mov(n_ov, 0)
            act.reg_mov(n_tab, 0)

            def square(base, t):
                if t >= 1:
                    act.wait_ge(sq_s, base * NT + t)
                A(sq_j, x[:, t, :], ACT.Square, accum_out=ssq[:, t:t + 1]).then_inc(sq_s, 1)

            def root(base, t):
                act.wait_ge(ms_s, base * NT + (t + 1))
                A(ssq[:, t:t + 1], ssq[:, t:t + 1], ACT.Sqrt).then_inc(rt_s, 1)

            def modulated(l, g0, t, scale, shift):
                for k in range(2):
                    act.wait_ge(tr_r, l * TR + (g0 + 2 * t + k + 1))
                    for c in range(4):
                        cc = 4 * k + c
                        ins = A(hT[:, cc, t * P:(t + 1) * P], bank[(g0 + k) % 2][:, c * P:(c + 1) * P], ACT.Identity,
                                scale=scale(cc), bias=shift(cc))
                    ins.then_inc(tr_e, 1)

            def evac(l, g, dst, **kw):
                act.wait_ge(tr_r, l * TR + (g + 1))
                A(dst, bank[g % 2][0:dst.shape[0], 0:SEQ], ACT.Identity, **kw).then_inc(tr_e, 1)

            def warm_root(n):
                if isinstance(n, int) and n == 0:
                    act.wait_ge(ones_s, 1)
                else:
                    act.wait_ge(wm_s, n)
                A(warm[:, :], ones[:, 0:1], ACT.Sqrt).then_inc(wm_s, 1)
            warm_root(0)
            with act.Fori(0, DEPTH) as l:
                warm_root(l + 1)
                for t in range(NT):
                    act.wait_ge(x2, l * NT + (t + 1))
                    square(l * 2, t)
                    root(l * 2, t)
                    if t == 1:
                        act.wait_ge(cur_s, l + 1)
                    if t:
                        modulated(l, TR_N1, t - 1, scale1, shift1)
                modulated(l, TR_N1, NT - 1, scale1, shift1)
                for i, (at, n) in enumerate(Z_ITEMS):
                    if i == 2:
                        for t in range(NT):
                            act.wait_ge(z_e, l * 16 + NT + t + 1)
                            if t >= 2:
                                act.wait_ge(zst_s, l * NT + t - 1)
                            A(zsq[:, t % 2, :], z[:, t, 0:640], ACT.Square).then_inc(zsq_s, 1)
                        act.wait_ge(zms_s, l * 2 + 1)
                        A(stz[:, :, 0:10], stz[:, :, 0:10], ACT.Sqrt).then_inc(zrt_s, 1)
                    for t in range(NT):
                        k = i * NT + t
                        act.wait_ge(z_r, l * 16 + (k + 1))
                        src = bank[2 + k % 4]
                        if i == 1:
                            A(va[:, t, :], src[:, P:2 * P], ACT.Copy)
                            A(z[:, t, at:at + P], src[:, 0:P], ACT.Copy).then_inc(z_e, 1)
                        elif i == 0:
                            A(z[:, t, 0:512].rearrange("p (j s d) -> p s j d", s=2, j=4),
                              src[:, :].rearrange("p (s j d) -> p s j d", s=2, j=4), ACT.Copy).then_inc(z_e, 1)
                        else:
                            A(z[:, t, at:at + n], src[:, 0:n], ACT.Copy).then_inc(z_e, 1)
                        if i == 3:
                            act.wait_ge(z_e, l * 16 + (k + 1))
                            if t:
                                act.wait_ge(zl_s, l * NT + t)
                            else:
                                act.wait_ge(zst_s, l * NT + NT)
                            A(reg_f[:, 0:QL], z[:, t, Z_QL:Z_QL + QL], ACT.Square, accum_out=stz[:, t, 10:11])
                            A(reg_f[:, QL:QL + KVL], z[:, t, Z_KVL:Z_KVL + KVL], ACT.Square, accum_out=stz[:, t, 11:12]).then_inc(zl_s, 1)
                act.wait_ge(zms_s, l * 2 + 2)
                A(stz[:, :, 10:12], stz[:, :, 10:12], ACT.Sqrt).then_inc(zrt_s, 1)
                for j in range(4):
                    evac(l, TR_QK + j, qaT[:, j, :])
                evac(l, TR_QK + 4, kaT)
                act.wait_ge(gl_s, l * 64 + 64)
                for c in range(5):
                    evac(l, TR_LAT + c, (qlT[:, c, :] if c < 3 else kvlT[:, c - 3, :]), scale=gain_l[:, c:c + 1])

                def put_mod(i):
                    act.wait_ge(mod_st, (l * ADA_IN + i) * 16)
                    act.wait_ge(tr_r, l * TR + (TR_ADA[i] + 1))
                    A(mod_row, bank[TR_ADA[i] % 2][0:1, :], ACT.Copy).then_inc(tr_e, 1)
                    wait(act, tr_e, l * TR + (TR_ADA[i] + 1))
                    act.dma_start(mod_v[l, ADA_PRE + i], mod_row).then_inc(mod_st, 16)

                def attend(u0, n):
                    for k in range(n + 2):
                        if k < n:
                            u = u0 + k
                            act.wait_ge(mx_s, l * UNITS + (u + 1))
                            if u >= 2:
                                act.wait_ge(pt_r, l * UNITS + (u - 1))
                            A(prob[:, u % 2, :], bank[4 + u % 2][:, :], ACT.Exp, bias=nmax[:, u % 4:u % 4 + 1],
                              accum_out=lsum[:, u % 4:u % 4 + 1]).then_inc(ex_s, 1)
                        if k >= 2:
                            u = u0 + k - 2
                            act.wait_ge(pt_r, l * UNITS + (u + 1))
                            if u >= 2:
                                act.wait_ge(o_r, l * UNITS + (u - 1))
                            A(probT[:, u % 2, :, :], bank[2 + u % 2][:, :], ACT.Copy).then_inc(pt_e, 1)
                        if k < n and (u0 + k) % 8 == 5 and u0 + k >= 8:
                            put_mod((u0 + k) // 8 - 1)
                attend(0, 32)
                for hf in range(2):
                    for g in range(2 * NT):
                        t = g % NT
                        if g == 2 * NT - 1:
                            for h in range(4):
                                evac(l, TR_MLA[hf] + h, qbT[0:KD, h, :])
                        act.wait_ge(nat_r, l * 16 + (hf * 8 + g + 1))
                        src = bank[4 + g % 2]
                        if g < NT:
                            A(qn[:, t, :, :], src[:, 0:384], ACT.Copy, scale=float(KD) ** -0.5).then_inc(nat_e, 1)
                        else:
                            kv = src[:, :].rearrange("p (h n) -> p h n", h=4)
                            A(vb[:, t, :].rearrange("p (h n) -> p h n", h=4), kv[:, :, HD:2 * HD], ACT.Copy)
                            A(kn[:, t, :, 0:HD], kv[:, :, 0:HD], ACT.Copy).then_inc(nat_e, 1)
                    for h in range(4):
                        evac(l, TR_MLA[hf] + 4 + h, kbT[0:KD, h, :])
                    attend(32 + 16 * hf, 16)
                put_mod(7)
                def next_piece(q):
                    with act.If(l < DEPTH - 1):
                        if q:
                            wait(act, nu_s, l * NX + q)
                        act.dma_start(nx_w, nx_v[after(l), q]).then_inc(nl_s, 16)
                wait(act, o_e, l * UNITS + UNITS)
                for j in range(NC):
                    next_piece(2 * j)
                    if j >= 2:
                        act.wait_ge(m_s, l * NC + (j - 1))
                    act.wait_ge(ga_r, l * NC + (j + 1))
                    A(sg_m[:, j % 2, 0, :], bank[4 * (j % 2)][:, :], ACT.Sigmoid)
                    act.wait_ge(gb_r, l * NC + (j + 1))
                    A(sg_m[:, j % 2, 1, :], bank[4 * (j % 2) + 1][:, :], ACT.Sigmoid).then_inc(sig_s, 1)
                    next_piece(2 * j + 1)
                act.wait_ge(cur2_s, l + 1)
                for t in range(NT):
                    act.wait_ge(x1, l * 8 + 2 * (t + 1))
                    square(l * 2 + 1, t)
                    root(l * 2 + 1, t)
                    modulated(l, TR_N2, t, scale2, shift2)
                act.wait_ge(lg_r, l + 1)
                A(reg_f[:, 0:64], bank[2][:, 0:64], ACT.Sigmoid).then_inc(sc_s, 1)

                def tokens_out(g, b, p0):
                    for k in range(2):
                        act.wait_ge(tr_r, g + (k + 1))
                        for c in range(4):
                            cc = 4 * k + c
                            ins = A(xsT[:, b, cc, :], bank[(p0 + k) % 2][:, c * P:(c + 1) * P], ACT.Identity,
                                    scale=scale2(cc), bias=shift2(cc))
                        ins.then_inc(tr_e, 1)

                def expert(e, p, g, last=False):
                    act.wait_ge(h1_r, l * E + e + 1)
                    A(sg_e, bank[4][:, :], ACT.Sigmoid).then_inc(sge_s, 1)
                    if not last:
                        tokens_out(g, 1 - p, p)
                    gu = g if last else g + 2
                    act.wait_ge(tr_r, gu + 1)
                    A(uT[:, :, :], bank[(p if not last else 1)][:, :], ACT.Copy).then_inc(tr_e, 1)

                tokens_out(l * TR + TR_X0, 0, 0)
                expert(0, 0, l * TR + TR_X0 + 2)
                for e in (1, 2):
                    expert(e, e % 2, l * TR + (TR_X0 + 2 + 3 * e))
                with act.Fori(0, 6) as i:
                    for r in range(2):
                        e = 2 * i + (3 + r)
                        expert(e, (3 + r) % 2, l * TR + (TR_X0 + 2 + 9 + 3 * r) + i * 6)
                expert(15, 1, l * TR + (TR_X0 + 2 + 45), last=True)

                def body(e, n):
                    for k in range(2):
                        act.wait_ge(ov_t, n * 3 + (k + 1))
                        for c in range(4):
                            cc = 4 * k + c
                            ins = A(xsT[:, 0, cc, :], bank[k][:, c * P:(c + 1) * P], ACT.Identity,
                                    scale=scale2(cc), bias=shift2(cc))
                        ins.then_inc(ov_te, 1)
                    act.wait_ge(ov_h, n * 2 + 1)
                    A(sg_e, bank[4][:, :], ACT.Sigmoid).then_inc(ov_g, 1)
                    act.wait_ge(ov_t, n * 3 + 3)
                    A(uT[:, :, :], bank[0][:, :], ACT.Copy).then_inc(ov_te, 1)
                wait(act, ds_s, l + 1)
                extra_blocks(act, n_ov, n_tab, body)
            warm_root(DEPTH + 1)
            for t in range(NT):
                act.wait_ge(x2, DEPTH * NT + t + 1)
                square(2 * DEPTH, t)
                root(2 * DEPTH, t)

        @block.vector
        def _(v):
            TT, TS, STT = v.tensor_tensor, v.tensor_scalar, v.scalar_tensor_tensor
            n_ov, n_tab = v.alloc_register("extra_blocks_dve"), v.alloc_register("extra_tables_dve")
            v.reg_mov(n_ov, 0)
            v.reg_mov(n_tab, 0)
            v.sem_inc(ov_free, 1)
            v.wait_ge(cond_e, 1)
            TT(cond[:, 0, :], cond[:, 0, :], cond[:, 1, :], ALU.mult).then_inc(cond_s, 1)
            v.wait_ge(x_in_s, 16 * NT)
            v.sem_inc(x2, NT)
            for r in range(ADA_PRE):
                v.wait_ge(b_in, ADA_PRE * 16)
                v.wait_ge(ada_ps, r + 1)
                row = reg_b[0:1, 512 * r:512 * (r + 1)]
                TT(row, bank[r][0:1, :], row, ALU.add).then_inc(ada_ev, 1)
            v.wait_ge(c_in_s, 16 * 5)

            def mean_square(base, t):
                v.wait_ge(sq_s, base * NT + (t + 1))
                TS(ssq[:, t:t + 1], ssq[:, t:t + 1], 1.0 / D, EPS, ALU.mult, ALU.add).then_inc(ms_s, 1)

            def scaled(base, t):
                v.wait_ge(rt_s, base * NT + (t + 1))
                v.reciprocal(rstd[:, t:t + 1], ssq[:, t:t + 1])
                v.drain()
                return TS(xn[:, t, :], x[:, t, :], rstd[:, t:t + 1], None, ALU.mult).then_inc(xn_s, 1)

            def combine(layer, t):
                v.wait_ge(cg_s[t], layer * 16 + 16)
                STT(x[:, t, :], cy[t][:, 0, :], gw[:, 0, t:t + 1], x[:, t, :], ALU.mult, ALU.add)
                v.drain()
                STT(x[:, t, :], cy[t][:, 1, :], gw[:, 1, t:t + 1], x[:, t, :], ALU.mult, ALU.add).then_inc(x2, 1)

            def rotate(x1v, x2v, cos, sin, ta, tb):
                TT(ta, x2v, sin, ALU.mult)
                TT(tb, x1v, sin, ALU.mult)
                v.drain()
                TT(x1v, x1v, cos, ALU.mult)
                TT(x2v, x2v, cos, ALU.mult)
                v.drain()
                TT(x1v, x1v, ta, ALU.subtract)
                return TT(x2v, x2v, tb, ALU.add)

            with v.Fori(0, DEPTH) as l:
                v.tensor_copy(gain2[:, :], gain_n[:, bass.ds(l + DEPTH, 1), :].rearrange("p o c -> p (o c)"))
                v.tensor_copy(gain1[:, :], gain_n[:, bass.ds(l, 1), :].rearrange("p o c -> p (o c)"))
                for t in range(NT):
                    with v.If(l > 0):
                        combine(l - 1, t)
                    mean_square(l * 2, t)
                    scaled(l * 2, t)
                    if t == 0:
                        with v.If(l < 1):
                            v.wait_ge(col_r, 2)
                            v.tensor_copy(mod_c[:, :, :].rearrange("p m c -> p (m c)"), bank[4][:, 0:2 * NC])
                        v.drain()
                        v.tensor_copy(cur[:, 0:2, :], mod_c[:, :, :])
                        v.drain()
                        STT(cur[:, 1, :], cur[:, 1, :], 1.0, gain1[:, :], ALU.add, ALU.mult).then_inc(cur_s, 1)
                for t in range(NT):
                    v.wait_ge(zsq_s, l * NT + (t + 1))
                    v.tensor_reduce(stz[:, t, 0:10], zsq[:, t % 2, :].rearrange("p (h n) -> p h n", n=HD), X, ALU.add).then_inc(zst_s, 1)
                v.drain()
                TS(stz[:, :, 0:10], stz[:, :, 0:10], 1.0 / HD, EPS, ALU.mult, ALU.add).then_inc(zms_s, 1)
                v.wait_ge(gl_s, l * 64 + 64)
                TS(gain_qk[:, 0, :], gain_qk[:, 0, :], float(HD) ** -0.5, None, ALU.mult)
                v.wait_ge(zrt_s, l * 2 + 1)
                v.reciprocal(stz[:, :, 0:10], stz[:, :, 0:10])
                v.drain()
                for t in range(NT):
                    heads = z[:, t, 0:640].rearrange("p (h n) -> p h n", n=HD)
                    TT(heads, heads, stz[:, t, 0:10].unsqueeze(2).broadcast_to([P, QK_HEADS, HD]), ALU.mult)
                    v.drain()
                    TT(heads[:, 0:8, :], heads[:, 0:8, :], gain_qk[:, 0:1, :].broadcast_to([P, 8, HD]), ALU.mult)
                    TT(heads[:, 8:10, :], heads[:, 8:10, :], gain_qk[:, 1:2, :].broadcast_to([P, 2, HD]), ALU.mult)
                    v.drain()
                    rr = [rot[:, k, :].rearrange("p (h n) -> p h n", n=32) for k in range(2)]
                    rotate(heads[:, :, 0:32], heads[:, :, 32:64],
                           cos_a[:, t:t + 1, :].broadcast_to([P, QK_HEADS, 32]),
                           sin_a[:, t:t + 1, :].broadcast_to([P, QK_HEADS, 32]), rr[0], rr[1]).then_inc(qk_s, 1)
                v.wait_ge(zl_s, l * NT + NT)
                TS(stz[:, :, 10:11], stz[:, :, 10:11], 1.0 / QL, EPS, ALU.mult, ALU.add)
                TS(stz[:, :, 11:12], stz[:, :, 11:12], 1.0 / KVL, EPS, ALU.mult, ALU.add).then_inc(zms_s, 1)
                v.wait_ge(zrt_s, l * 2 + 2)
                v.reciprocal(stz[:, :, 10:12], stz[:, :, 10:12])
                v.drain()
                for t in range(NT):
                    TS(z[:, t, Z_QL:Z_QL + QL], z[:, t, Z_QL:Z_QL + QL], stz[:, t, 10:11], None, ALU.mult)
                    ins = TS(z[:, t, Z_KVL:Z_KVL + KVL], z[:, t, Z_KVL:Z_KVL + KVL], stz[:, t, 11:12], None, ALU.mult)
                ins.then_inc(lat_s, 1)
                krv = z[:, :, Z_KR:Z_KR + RD]
                rk2 = [rot[:, k, 0:64].rearrange("p (t n) -> p t n", t=NT) for k in range(2)]
                rotate(krv[:, :, 0:16], krv[:, :, 16:32], cos_b, sin_b, rk2[0], rk2[1])
                v.drain()
                v.tensor_copy(kr[:, :, :], krv).then_inc(lat_s, 1)
                v.drain()

                def mod_chunk(u):
                    i, c = u // 8, u % 8
                    k = ADA_ITEM[i]
                    w = slot(k % R, NC, 512)[:, c, :]
                    if c == 0:
                        v.wait_ge(w_rdy[k % R], l * (16 * slot_total(k % R)) + 16 * (PRE[k % R] + slot_loads(k)))
                        if i >= 2:
                            v.wait_ge(tr_r, l * TR + (TR_ADA[i - 2] + 1))
                        return TS(acc[:, i % 2, :], w, cond[:, 0, c:c + 1], None, ALU.mult)
                    return STT(acc[:, i % 2, :], w, cond[:, 0, c:c + 1], acc[:, i % 2, :], ALU.mult, ALU.add)

                def attend(u0, n, heads):
                    for k in range(n + 3):
                        if k < n:
                            u = u0 + k
                            v.wait_ge(s_r, l * UNITS + (u + 1))
                            v.tensor_reduce(nmax[:, u % 4:u % 4 + 1], bank[4 + u % 2][:, :], X, ALU.max, negate=True).then_inc(mx_s, 1)
                        if 1 <= k < n + 1:
                            u = u0 + k - 1
                            v.wait_ge(ex_s, l * UNITS + (u + 1))
                            v.reciprocal(linv[:, u % 4:u % 4 + 1], lsum[:, u % 4:u % 4 + 1])
                            v.drain()
                            TS(prob[:, u % 2, :], prob[:, u % 2, :], linv[:, u % 4:u % 4 + 1], None, ALU.mult).then_inc(pn_s, 1)
                        if k < n:
                            ins = mod_chunk(u0 + k)
                            if (u0 + k) % 8 == 7:
                                ins.then_inc(aa_s, 1)
                        if k >= 3:
                            u = u0 + k - 3
                            hd, t = heads[k - 3]
                            v.wait_ge(o_r, l * UNITS + (u + 1))
                            v.tensor_copy(oT[(hd % 2) * HD:(hd % 2 + 1) * HD, hd // 2, t * P:(t + 1) * P],
                                          bank[6 + u % 2][0:HD, 0:P]).then_inc(o_e, 1)
                attend(0, 32, GQA_UNITS)
                for hf in range(2):
                    v.tensor_copy(kn[:, :, :, HD:KD], kr[:, :, :].unsqueeze(2).broadcast_to([P, NT, 4, RD]))
                    v.wait_ge(nat_e, l * 16 + (hf * 8 + 4))
                    r4 = [rot_b[:, k, :].rearrange("p (t h n) -> p t h n", t=NT, h=4) for k in range(2)]
                    cb = cos_b.unsqueeze(2).broadcast_to([P, NT, 4, 16])
                    sn = sin_b.unsqueeze(2).broadcast_to([P, NT, 4, 16])
                    rotate(qn[:, :, :, HD:HD + 16], qn[:, :, :, HD + 16:KD], cb, sn, r4[0], r4[1]).then_inc(rope_s, 1)
                    attend(32 + 16 * hf, 16, [(8 + 4 * hf + h, t) for h in range(4) for t in range(NT)])
                v.wait_ge(cur2_ld, l * 16 + 16)
                STT(cur[:, 3, :], cur[:, 3, :], 1.0, gain2[:, :], ALU.add, ALU.mult).then_inc(cur2_s, 1)
                def next_sum(q):
                    with v.If(l < DEPTH - 1):
                        dst = nx_acc[:, q * P:(q + 1) * P]
                        v.wait_ge(nl_s, l * (16 * NX) + 16 * (q + 1))
                        TS(dst, nx_w[:, 0, :], cond[:, 0, 0:1], None, ALU.mult)
                        for c in range(1, NC):
                            v.drain()
                            ins = STT(dst, nx_w[:, c, :], cond[:, 0, c:c + 1], dst, ALU.mult, ALU.add)
                        ins.then_inc(nu_s, 1)
                for j in range(NC):
                    next_sum(2 * j)
                    v.wait_ge(sig_s, l * NC + (j + 1))
                    v.wait_ge(ya_r, l * NC + (j + 1))
                    TT(mT[:, j, :], bank[4 * (j % 2) + 2][:, :], sg_m[:, j % 2, 0, :], ALU.mult)
                    v.wait_ge(yb_r, l * NC + (j + 1))
                    TT(sg_m[:, j % 2, 1, :], bank[4 * (j % 2) + 3][:, :], sg_m[:, j % 2, 1, :], ALU.mult)
                    v.drain()
                    TT(mT[:, j, :], mT[:, j, :], sg_m[:, j % 2, 1, :], ALU.add).then_inc(m_s, 1)
                    next_sum(2 * j + 1)
                v.wait_ge(row_ld, l * 48 + 48)
                for k in range(8):
                    t, n = k // 2, k % 2
                    v.wait_ge(wo_r, l * 8 + (k + 1))
                    TT(wo_t[:, k % 2, :], wo_bank(k)[:, :], g1_row[:, n * 512:(n + 1) * 512], ALU.mult)
                    v.drain()
                    xs = x[:, t, n * 512:(n + 1) * 512]
                    TT(xs, xs, wo_t[:, k % 2, :], ALU.add).then_inc(x1, 1)
                    if n == 1:
                        mean_square(l * 2 + 1, t)
                        scaled(l * 2 + 1, t)

                def top1(vals, ramp, onehot, tmp, mx):
                    n = vals.shape[2]
                    v.tensor_reduce(mx, vals, X, ALU.max)
                    v.drain()
                    TT(tmp, vals, mx.unsqueeze(2).broadcast_to([P, NT, n]), ALU.is_equal)
                    v.drain()
                    TT(tmp, tmp, ramp.unsqueeze(1).broadcast_to([P, NT, n]), ALU.mult)
                    v.drain()
                    v.tensor_reduce(mx, tmp, X, ALU.max)
                    v.drain()
                    TT(onehot, tmp, mx.unsqueeze(2).broadcast_to([P, NT, n]), ALU.is_equal)
                    v.drain()
                v.wait_ge(sc_s, l + 1)
                TT(biased, score, rbias[:, :].unsqueeze(1).broadcast_to([P, NT, E]), ALU.add)
                v.drain()
                bg = biased.rearrange("p t (g e) -> p (t g) e", g=EG)
                ps = reg_f[:, 640:736].rearrange("p (g k) -> p g k", k=6)
                TT(ps[:, :, 0:3], bg[:, :, 0:3], bg[:, :, 1:4], ALU.add)
                TT(ps[:, :, 3:5], bg[:, :, 0:2], bg[:, :, 2:4], ALU.add)
                TT(ps[:, :, 5:6], bg[:, :, 0:1], bg[:, :, 3:4], ALU.add)
                v.drain()
                gs = r_s[:, 0:16].rearrange("p (t g) -> p t g", t=NT)
                gt = r_s[:, 16:32].rearrange("p (t g) -> p t g", t=NT)
                gh = r_s[:, 32:48].rearrange("p (t g) -> p t g", t=NT)
                mx = r_s[:, 48:52]
                v.tensor_reduce(r_s[:, 0:16], ps, X, ALU.max)
                v.drain()
                top1(gs, cst[:, C_GW:C_GW + EG], gh, gt, mx)
                sel = r_s[:, 32:48].unsqueeze(2).broadcast_to([P, NT * EG, EG])
                ra_g = r_a.rearrange("p t (g e) -> p (t g) e", g=EG)
                TT(ra_g, bg, sel, ALU.mult)
                TS(r_s[:, 64:80], r_s[:, 32:48], 1.0, BIG, ALU.subtract, ALU.mult)
                v.drain()
                TT(ra_g, ra_g, r_s[:, 64:80].unsqueeze(2).broadcast_to([P, NT * EG, EG]), ALU.add)
                v.drain()
                ew = cst[:, C_EW:C_EW + E]
                top1(r_a, ew, oh1, r_b, mx)
                STT(r_a, oh1, -BIG, r_a, ALU.mult, ALU.add)
                v.drain()
                top1(r_a, ew, oh2, r_b, mx)
                TT(r_a, oh1, oh2, ALU.add)
                v.drain()
                v.tensor_copy(upto[:, 0, :], r_a[:, 0, :])
                TT(upto[:, 1, :], r_a[:, 0, :], r_a[:, 1, :], ALU.add)
                TT(upto[:, 3, :], r_a[:, 2, :], r_a[:, 3, :], ALU.add)
                v.drain()
                TT(upto[:, 2, :], upto[:, 1, :], r_a[:, 2, :], ALU.add)
                TT(upto[:, 3, :], upto[:, 1, :], upto[:, 3, :], ALU.add).then_inc(oh_s, 1)
                TT(r_b, oh1, score, ALU.mult)
                v.drain()
                v.tensor_reduce(gw[:, 0, :], r_b, X, ALU.add)
                v.drain()
                TT(r_b, oh2, score, ALU.mult)
                v.drain()
                v.tensor_reduce(gw[:, 1, :], r_b, X, ALU.add)
                v.drain()
                TT(r_s[:, 52:56], gw[:, 0, :], gw[:, 1, :], ALU.add)
                v.drain()
                v.reciprocal(r_s[:, 56:60], r_s[:, 52:56])
                v.drain()
                for k in range(2):
                    TT(gw[:, k, :], gw[:, k, :], r_s[:, 56:60], ALU.mult)
                with v.If(l < DEPTH - 1):
                    v.wait_ge(nb_s, l * 16 + 16)
                    v.wait_ge(nm_r, l + 1)
                    TT(mod_c[:, :, :].rearrange("p m c -> p (m c)"), bank[7][:, 0:2 * NC],
                       bias_c[:, :, :].rearrange("p m c -> p (m c)"), ALU.add)
                for k, oh in ((0, oh1), (1, oh2)):
                    TT(chosen[:, k, :, 0:E], oh, cst[:, C_TK:C_TK + NT].unsqueeze(2).broadcast_to([P, NT, E]), ALU.mult)
                    TT(chosen[:, k, :, E:2 * E], oh,
                       cst[:, C_RW + k * NT:C_RW + (k + 1) * NT].unsqueeze(2).broadcast_to([P, NT, E]), ALU.mult)
                v.wait_ge(rk_r, l + 1)
                rank = bank[3][:, 0:NT * E].rearrange("p (t e) -> p t e", t=NT)
                TT(r_b, oh1, rank, ALU.mult)
                TT(biased, oh2, rank, ALU.mult)
                v.drain()
                v.tensor_reduce(rank_k[:, 0, :], r_b, X, ALU.add)
                v.tensor_reduce(rank_k[:, 1, :], biased, X, ALU.add)
                v.tensor_copy(cnt_i[:, :], bank[3][:, NT * E:(NT + 1) * E])
                v.tensor_reduce(r_s[0:1, 160:161], bank[3][0:1, NT * E:(NT + 1) * E], X, ALU.max)
                v.drain()
                v.tensor_copy(flag_i[:, :], r_s[0:1, 160:161])

                def slots_of_tokens(done):
                    TT(slot_of, cst[:, C_IO:C_IO + P].unsqueeze(1).broadcast_to([P, 2 * NT, P]),
                       reg_f[:, 736:744].unsqueeze(2).broadcast_to([P, 2 * NT, P]), ALU.is_equal).then_inc(done, 1)

                def take_table(done):
                    v.tensor_copy(table[:, 0:E], bank[3][:, P:P + E])
                    TS(table[:, E:2 * E], bank[3][:, P + E:P + 2 * E], float(NONE), None, ALU.add).then_inc(done, 1)
                slots_of_tokens(ds_s)
                v.wait_ge(tp_r, l + 1)
                take_table(tb_s)

                def hidden(at):
                    v.wait_ge(sge_s, at + 1)
                    TT(u_s, bank[4][:, :], sg_e, ALU.mult)
                    v.drain()
                    v.wait_ge(h3_r, at + 1)
                    TT(u_s, bank[5][:, :], u_s, ALU.mult).then_inc(u_s_s, 1)

                def put_out(f, p):
                    for n in range(2):
                        v.wait_ge(y_r, (l * E + f) * 2 + (n + 1))
                        cols = slice(n * 512, (n + 1) * 512)
                        TT(ysb[:, p, cols], bank[6 + n][:, :], g2_row[:, cols], ALU.mult).then_inc(y_e, 1)
                for e in range(3):
                    hidden(l * E + e)
                    if e:
                        put_out(e - 1, (e - 1) % 2)
                with v.Fori(0, 6) as i:
                    for r in range(2):
                        hidden(l * E + 2 * i + (3 + r))
                        v.wait_ge(ys_st[r], l * 128 + (i * 16 + 16))
                        put_out(2 * i + (2 + r), r)
                hidden(l * E + 15)
                for f in (14, 15):
                    v.wait_ge(ys_st[f % 2], l * 128 + 112)
                    put_out(f, f % 2)

                def body(e, n):
                    v.wait_ge(ov_g, n + 1)
                    TT(u_s, bank[4][:, :], sg_e, ALU.mult)
                    v.drain()
                    v.wait_ge(ov_h, n * 2 + 2)
                    TT(u_s, bank[5][:, :], u_s, ALU.mult).then_inc(ov_u, 1)
                    for h in range(2):
                        v.wait_ge(ov_y, n * 2 + (h + 1))
                        cols = slice(h * 512, (h + 1) * 512)
                        TT(ysb[:, 0, cols], bank[6 + h][:, :], g2_row[:, cols], ALU.mult).then_inc(ov_ye, 1)

                def new_table(n, m):
                    v.wait_ge(ov_free, n + 1)
                    TS(rank_k, rank_k, -float(P), None, ALU.add)
                    v.drain()
                    slots_of_tokens(ov_sl)
                    v.wait_ge(ov_tp, m + 1)
                    take_table(ov_tb)
                v.wait_ge(ys_st[0], l * 128 + 128)
                v.wait_ge(ys_st[1], l * 128 + 128)
                wait(v, ds_s, l + 1)
                extra_blocks(v, n_ov, n_tab, body, new_table)

            for t in range(NT + 1):
                if t < NT:
                    combine(DEPTH - 1, t)
                if t:
                    u = t - 1
                    mean_square(2 * DEPTH, u)
                    v.wait_ge(rt_s, 2 * DEPTH * NT + (u + 1))
                    v.reciprocal(rstd[:, u:u + 1], ssq[:, u:u + 1])
                    v.drain()
                    STT(xn[:, u, :], x[:, u, :], rstd[:, u:u + 1], nf_row, ALU.mult, ALU.mult).then_inc(out_s, 1)

        @block.tensor
        def _(pe):
            n_ov, n_tab = pe.alloc_register("extra_blocks_pe"), pe.alloc_register("extra_tables_pe")
            pe.reg_mov(n_ov, 0)
            pe.reg_mov(n_tab, 0)
            pe.wait_ge(cond_s, 1)
            pe.wait_ge(ones_s, 1)

            def columns(m):
                pe.wait_ge(ada_ev, 2 * (m + 1))
                for c in range(NC):
                    ins = pe.transpose(bank[4][:, m * NC + c:m * NC + c + 1], reg_b[0:1, m * D + c:(m + 1) * D:NC],
                                       ones[0:1, 0:1])
                ins.then_inc(col_r, 1)
            for r in range(ADA_PRE):
                if r:
                    pe.wait_ge(w_rdy[r], 16)
                for c in range(NC):
                    if r == 0:
                        for (a, _), s in zip(FIRST_PARTS, first_s + [w_rdy[0]]):
                            if c == a:
                                pe.wait_ge(s, 16)
                    ins = pe.matmul(bank[r][0:1, :], cond[:, 0, c:c + 1], slot(r, NC, 512)[:, c, :],
                                    start=c == 0, stop=c == NC - 1)
                ins.then_inc(ada_ps, 1)
            columns(0)
            columns(1)
            pe.wait_ge(c_in_s, 16 * 5)

            with pe.Fori(0, DEPTH) as l:
                def weights(k):
                    pe.wait_ge(w_rdy[k % R], l * (16 * slot_total(k % R)) + 16 * (PRE[k % R] + slot_loads(k)))

                def transposes(g, srcs, rows=P):
                    if g >= 2:
                        pe.wait_ge(tr_e, l * TR + (g - 1))
                    for t, src in enumerate(srcs):
                        ins = pe.transpose(bank[g % 2][0:rows, t * P:(t + 1) * P], src, ident)
                    ins.then_inc(tr_r, 1)

                def norm_transposes(g0, n0, t):
                    pe.wait_ge(xn_s, l * 2 * NT + (n0 + t + 1))
                    xv = xn[:, t, :].rearrange("p (q c) -> p c q", c=NC)
                    for k in range(2):
                        transposes(g0 + 2 * t + k, [xv[:, 4 * k + c, :] for c in range(4)])

                norm_transposes(TR_N1, 0, 0)
                for i, (at, n) in enumerate(Z_ITEMS):
                    weights(i)
                    w = slot(i, NC, n)
                    for t in range(NT):
                        k = i * NT + t
                        if k >= 4:
                            pe.wait_ge(z_e, l * 16 + (k - 3))
                        for c in range(NC):
                            if i == 0 and c % 4 == 0:
                                if c and t + 1 < NT:
                                    norm_transposes(TR_N1, 0, t + 1)
                                pe.wait_ge(tr_e, l * TR + (TR_N1 + 2 * t + c // 4 + 1))
                            ins = pe.matmul(bank[2 + k % 4][:, 0:n], hT[:, c, t * P:(t + 1) * P], w[:, c, :],
                                            start=c == 0, stop=c == NC - 1)
                        ins.then_inc(z_r, 1)
                pe.wait_ge(qk_s, l * 4 + 4)
                for j in range(4):
                    transposes(TR_QK + j, [z[:, t, j * P:(j + 1) * P] for t in range(NT)])
                transposes(TR_QK + 4, [z[:, t, 512:640] for t in range(NT)])
                pe.wait_ge(lat_s, l * 2 + 1)
                for c in range(5):
                    at = Z_QL + c * P
                    transposes(TR_LAT + c, [z[:, t, at:at + P] for t in range(NT)])
                pe.wait_ge(tr_e, l * TR + TR_ADA[0])

                def mod_sum(i):
                    g = TR_ADA[i]
                    pe.wait_ge(aa_s, l * ADA_IN + (i + 1))
                    pe.wait_ge(mb_s, l * (16 * ADA_IN) + 16 * (i + 1))
                    pe.wait_ge(tr_e, l * TR + (g - 1))
                    pe.matmul(bank[g % 2][0:1, :], ones[:, 0:1], acc[:, i % 2, :], start=True, stop=False)
                    pe.matmul(bank[g % 2][0:1, :], ones[32:33, 0:1], mod_bias, start=False, stop=True).then_inc(tr_r, 1)

                def heads_product(hf, g):
                    t = g % NT
                    item = (8, 11)[hf]
                    lat, nk, n, w = (qlT, 3, 384, heads_q(item)) if g < NT else (kvlT, 2, 512, heads_kv(item))
                    if g == 0:
                        weights(item)
                    if g < 2:
                        pe.wait_ge(ex_s, l * UNITS + (31 + 16 * hf + g))
                    else:
                        pe.wait_ge(nat_e, l * 16 + (hf * 8 + g - 1))
                    for c in range(nk):
                        ins = pe.matmul(bank[4 + g % 2][:, 0:n], lat[:, c, t * P:(t + 1) * P], w[:, c, :],
                                        start=c == 0, stop=c == nk - 1)
                    ins.then_inc(nat_r, 1)

                def branch_product(j, q):
                    h = j // 4
                    item, src, nk, s = ((14 + 4 * h, hT, NC, ga_r), (15 + 4 * h, hT, NC, gb_r),
                                        (16 + 4 * h, oT, 4, ya_r), (17 + 4 * h, oT, 4, yb_r))[q]
                    if j % 4 == 0:
                        weights(item)
                    w = slot(item % R, nk, 512)
                    for c in range(nk):
                        ins = pe.matmul(bank[4 * (j % 2) + q][:, :], w[:, c, (j % 4) * P:(j % 4 + 1) * P],
                                        src[:, c + (4 if q == 3 else 0), :], start=c == 0, stop=c == nk - 1)
                    ins.then_inc(s, 1)

                def attend(u0, n, q_of, k_of, v_of, tail):
                    for k in range(n + 3):
                        if k >= n:
                            tail(k - n)
                        if k < n:
                            u = u0 + k
                            if u >= 2:
                                pe.wait_ge(ex_s, l * UNITS + (u - 1))
                            pe.matmul(bank[4 + u % 2][:, :], q_of(k), k_of(k), start=True, stop=True).then_inc(s_r, 1)
                        if 2 <= k < n + 2:
                            u = u0 + k - 2
                            pe.wait_ge(pn_s, l * UNITS + (u + 1))
                            if u >= 2:
                                pe.wait_ge(pt_e, l * UNITS + (u - 1))
                            for kc in range(NT):
                                ins = pe.transpose(bank[2 + u % 2][:, kc * P:(kc + 1) * P],
                                                   prob[:, u % 2, kc * P:(kc + 1) * P], ident)
                            ins.then_inc(pt_r, 1)
                        if k >= 3:
                            u = u0 + k - 3
                            pe.wait_ge(pt_e, l * UNITS + (u + 1))
                            if u >= 2:
                                pe.wait_ge(o_e, l * UNITS + (u - 1))
                            for kc in range(NT):
                                ins = pe.matmul(bank[6 + u % 2][0:HD, 0:P], v_of(k - 3, kc), probT[:, u % 2, kc, :],
                                                start=kc == 0, stop=kc == NT - 1)
                            ins.then_inc(o_r, 1)
                        if k < n and (u0 + k) % 8 == 3 and u0 + k >= 8:
                            mod_sum((u0 + k) // 8 - 1)

                def first_gate(g):
                    if g == 0:
                        pe.wait_ge(tr_e, l * TR + (TR_ADA[6] + 1))
                        branch_product(0, 0)

                def gqa(k):
                    hd, t = GQA_UNITS[k]
                    return hd // 4, hd % 4, t
                attend(0, 32,
                       lambda k: qaT[gqa(k)[0] * HD:(gqa(k)[0] + 1) * HD, gqa(k)[1], gqa(k)[2] * P:(gqa(k)[2] + 1) * P],
                       lambda k: kaT[gqa(k)[0] * HD:(gqa(k)[0] + 1) * HD, :],
                       lambda k, kc: va[:, kc, gqa(k)[0] * HD:(gqa(k)[0] + 1) * HD],
                       lambda g: heads_product(0, g))
                for hf in range(2):
                    for g in range(3, 2 * NT - 1):
                        heads_product(hf, g)
                    pe.wait_ge(rope_s, l * 2 + (hf + 1))
                    for h in range(4):
                        transposes(TR_MLA[hf] + h, [qn[:, t, h, :] for t in range(NT)], KD)
                    heads_product(hf, 2 * NT - 1)
                    pe.wait_ge(nat_e, l * 16 + (hf * 8 + 8))
                    for h in range(4):
                        transposes(TR_MLA[hf] + 4 + h, [kn[:, t, h, :] for t in range(NT)], KD)

                    def mla_keys(k):
                        if k % NT == 0:
                            pe.wait_ge(tr_e, l * TR + (TR_MLA[hf] + 4 + k // NT + 1))
                        return kbT[0:KD, k // NT, :]
                    attend(32 + 16 * hf, 16,
                           lambda k: qbT[0:KD, k // NT, (k % NT) * P:(k % NT + 1) * P],
                           mla_keys,
                           lambda k, kc: vb[:, kc, (k // NT) * HD:(k // NT + 1) * HD],
                           (lambda g: heads_product(1, g)) if hf == 0 else first_gate)
                mod_sum(7)
                for j in range(NC):
                    if j >= 2:
                        pe.wait_ge(m_s, l * NC + (j - 1))
                    for q in range(4):
                        if (j, q) == (0, 1):
                            pe.wait_ge(tr_e, l * TR + TR_N2)
                        if (j, q) == (0, 2):
                            pe.wait_ge(o_e, l * UNITS + UNITS)
                        if (j, q) != (0, 0):
                            branch_product(j, q)
                def logits(t):
                    for c in range(NC):
                        if c % 4 == 0:
                            pe.wait_ge(tr_e, l * TR + (TR_N2 + 2 * t + c // 4 + 1))
                        ins = pe.matmul(bank[2][:, t * E:(t + 1) * E], hT[:, c, t * P:(t + 1) * P], wr[:, c, :],
                                        start=c == 0, stop=c == NC - 1)
                    return ins

                weights(22)
                weights(23)
                for k in range(8):
                    t, n = k // 2, k % 2
                    if k >= 4:
                        pe.wait_ge(x1, l * 8 + (k - 3))
                    w = slot((22 + n) % R, NC, 512)
                    for c in range(NC):
                        if k == 0 and c in (0, NC - 1):
                            pe.wait_ge(m_s, l * NC + max(c + 1, NC - 1))
                        ins = pe.matmul(wo_bank(k)[:, :], mT[:, c, t * P:(t + 1) * P], w[:, c, :],
                                        start=c == 0, stop=c == NC - 1)
                    ins.then_inc(wo_r, 1)
                    if n == 0 and t >= 1:
                        norm_transposes(TR_N2, NT, t - 1)
                    if n == 1 and t >= 1:
                        logits(t - 1)
                norm_transposes(TR_N2, NT, NT - 1)
                logits(NT - 1).then_inc(lg_r, 1)
                with pe.If(l < DEPTH - 1):
                    pe.wait_ge(nu_s, l * NX + NX)
                    pe.wait_ge(x1, l * 8 + 8)
                    for m in range(2):
                        for c in range(NC):
                            ins = pe.matmul(bank[7][:, m * NC + c:m * NC + c + 1], nx_acc[:, m * D + c:(m + 1) * D:NC],
                                            ones[:, 0:1], start=True, stop=True)
                    ins.then_inc(nm_r, 1)
                pe.wait_ge(oh_s, l + 1)
                pe.matmul(bank[3][:, 0:NT * E], utri, r_a, start=True, stop=False)
                pe.matmul(bank[3][:, E:NT * E], ones[:, :], upto[:, 0:NT - 1, :], start=False, stop=True)
                pe.matmul(bank[3][:, NT * E:(NT + 1) * E], ones[:, :], upto[:, NT - 1, :], start=True, stop=True).then_inc(rk_r, 1)

                def slot_table(done):
                    for q in range(2 * NT):
                        ins = pe.matmul(bank[3][:, P:P + 2 * E], slot_of[:, q, :], chosen[:, q // NT, q % NT, :],
                                        start=q == 0, stop=q == 2 * NT - 1)
                    ins.then_inc(done, 1)
                pe.wait_ge(ds_s, l + 1)
                slot_table(tp_r)

                def token_transposes(g, p0, b):
                    xv = xg[:, b, :].rearrange("p (q c) -> p c q", c=NC)
                    for k in range(2):
                        pe.wait_ge(tr_e, g + (k - 1))
                        for c in range(4):
                            ins = pe.transpose(bank[(p0 + k) % 2][:, c * P:(c + 1) * P], xv[:, 4 * k + c, :], ident)
                        ins.then_inc(tr_r, 1)

                def up(tokens, w1s, w3s, s1, s3):
                    for s, bk, done in ((w1s, 4, s1), (w3s, 5, s3)):
                        w = slot(s, NC, F)
                        for c in range(NC):
                            ins = pe.matmul(bank[bk][:, :], tokens[:, c, :], w[:, c, :], start=c == 0, stop=c == NC - 1)
                        ins.then_inc(done, 1)

                def down(s, done):
                    w = slot(s, 4, D)
                    for n in range(2):
                        for c in range(4):
                            ins = pe.matmul(bank[6 + n][:, :], uT[:, c, :], w[:, c, n * 512:(n + 1) * 512],
                                            start=c == 0, stop=c == 3)
                        ins.then_inc(done, 1)

                def hidden_transposes(b):
                    for c in range(4):
                        ins = pe.transpose(bank[b][:, c * P:(c + 1) * P], u_s[:, c * P:(c + 1) * P], ident)
                    return ins

                def loaded(s, n):
                    pe.wait_ge(w_rdy[s], l * (16 * slot_total(s)) + n * 16)

                def nth(k):
                    return PRE[k % R] + slot_loads(k)

                def expert(e, p, g, slots, loads, gat, first=False, last=False):
                    loaded(slots[0], loads[0])
                    pe.wait_ge(tr_e, g - 1)
                    for s, n, bk, done in ((slots[0], loads[0], 4, h1_r), (slots[1], loads[1], 5, h3_r)):
                        loaded(s, n)
                        wv = slot(s, NC, F)
                        for c in range(NC):
                            if first and c == 4:
                                pe.wait_ge(tr_e, g)
                            ins = pe.matmul(bank[bk][:, :], xsT[:, p, c, :], wv[:, c, :], start=c == 0, stop=c == NC - 1)
                        ins.then_inc(done, 1)
                    if not last:
                        pe.wait_ge(xg_s[1 - p], l * 128 + gat)
                        token_transposes(g, p, 1 - p)
                    if not first:
                        loaded(slots[2], loads[2])
                        pe.wait_ge(tr_e, g)
                        if not (isinstance(e, int) and e == 1):
                            pe.wait_ge(y_e, (l * E + e - 1) * 2)
                        down(slots[2], y_r)
                    pe.wait_ge(u_s_s, l * E + e + 1)
                    gu = g if last else g + 2
                    pe.wait_ge(tr_e, gu - 1)
                    hidden_transposes(1 if last else p).then_inc(tr_r, 1)

                pe.wait_ge(xg_s[0], l * 128 + 16)
                token_transposes(l * TR + TR_X0, 0, 0)
                expert(0, 0, l * TR + (TR_X0 + 2), (0, 1), (nth(MIX_ITEMS), nth(MIX_ITEMS + 1)), 16, first=True)

                def items(e):
                    return [MIX_ITEMS + 2 + 3 * (e - 1) + q for q in range(3)]
                for e in (1, 2):
                    it = items(e)
                    expert(e, e % 2, l * TR + (TR_X0 + 2 + 3 * e), [k % R for k in it], [nth(k) for k in it],
                           16 * ((e + 1) // 2 + 1))
                with pe.Fori(0, 6) as i:
                    for r in range(2):
                        it = items(3 + r)
                        expert(2 * i + (3 + r), (3 + r) % 2, l * TR + (TR_X0 + 2 + 9 + 3 * r) + i * 6,
                               [k % R for k in it], [i + nth(k) for k in it],
                               i * 16 + 16 * ((4 + r) // 2 + 1))
                it = items(15)
                expert(15, 1, l * TR + (TR_X0 + 2 + 45), [k % R for k in it], [nth(k) for k in it], 0, last=True)
                loaded((ITEMS - 1) % R, nth(ITEMS - 1))
                pe.wait_ge(tr_e, l * TR + TR)
                pe.wait_ge(y_e, (l * E + 15) * 2)
                down((ITEMS - 1) % R, y_r)

                def body(e, n):
                    pe.wait_ge(ov_w, n * 48 + 48)
                    pe.wait_ge(ov_x, n * 16 + 16)
                    xv = xg[:, 0, :].rearrange("p (q c) -> p c q", c=NC)
                    for k in range(2):
                        for c in range(4):
                            ins = pe.transpose(bank[k][:, c * P:(c + 1) * P], xv[:, 4 * k + c, :], ident)
                        ins.then_inc(ov_t, 1)
                    pe.wait_ge(ov_te, n * 3 + 2)
                    up(xsT[:, 0, :, :], 3, 4, ov_h, ov_h)
                    pe.wait_ge(ov_u, n + 1)
                    hidden_transposes(0).then_inc(ov_t, 1)
                    pe.wait_ge(ov_te, n * 3 + 3)
                    down(5, ov_y)
                pe.wait_ge(y_e, l * 2 * E + 2 * E)
                wait(pe, ds_s, l + 1)

                def new_table(n, m):
                    pe.wait_ge(ov_sl, m + 1)
                    slot_table(ov_tp)
                extra_blocks(pe, n_ov, n_tab, body, new_table)


def kernel(**inputs):
    import concourse.bacc as bacc
    from concourse.bass_utils import run_bass_kernel_spmd

    names = ["x", "c", "w_ada", "b_ada", "norm1", "w_in", "q_norm_a", "k_norm_a", "q_a_norm", "kv_norm",
             "w_q_b", "w_kv_b", "w_proj_a", "w_proj_b", "w_o", "norm2", "w_router", "router_bias",
             "w1", "w3", "w2", "norm_f"]
    nc = bacc.Bacc("TRN2", target_bir_lowering=False, num_devices=1)
    arrays = {f"in_{n}": np.ascontiguousarray(inputs[n]) for n in names}
    arrays["in_constants"] = constants()
    args = [nc.dram_tensor(n, a.shape, mybir.dt.from_np(a.dtype), kind="ExternalInput").ap() for n, a in arrays.items()]
    out = nc.dram_tensor("out_0", (1, SEQ, D), mybir.dt.float32, kind="ExternalOutput").ap()
    trunk(nc, *args, out)
    r = run_bass_kernel_spmd(nc, [arrays], core_ids=[0])
    return r.results[0]["out_0"]
```
